# Optimizing a Trainium2 kernel written in Bass

```python
import jax, jax.numpy as jnp
from jax import lax
import numpy as np

D_MODEL = 1024
BATCH = 1
SEQ = 256
DEPTH = 2

CHUNK = 64
GLA_HEADS = 4
GLA_DK = 128
GLA_DV = 256
GLA_GATE_RANK = 16
GLA_TAU = 16.0
SG_WIDTH = 1024
SG_GROUPS = 4
SG_BLOCK = 128
MLA_HEADS = 8
MLA_Q_RANK = 384
MLA_KV_RANK = 256
MLA_NOPE = 128
MLA_ROPE = 64
MLA_V = 128
MLA_QK = MLA_NOPE + MLA_ROPE
ROPE_THETA = 10000.0
Q_BLOCK = 128
N_BRANCHES = 3
BRANCH_WIDTH = 1024
N_EXPERTS = 64
N_GROUPS = 8
TOPK_GROUPS = 4
TOP_K = 8
D_EXPERT = 256
D_SHARED = 256
ROUTED_SCALE = 2.5
EXPERT_BLOCK = 128
PLE_DIM = 256
ALPHA = (2 * DEPTH) ** 0.25
BETA = (8 * DEPTH) ** -0.25
IN_SPLIT = (GLA_HEADS * GLA_DK, GLA_HEADS * GLA_DK, GLA_HEADS * GLA_DV, GLA_HEADS * GLA_DV,
            GLA_GATE_RANK, 2 * SG_WIDTH, MLA_Q_RANK, MLA_KV_RANK + MLA_ROPE, N_BRANCHES * D_MODEL)
D_IN = sum(IN_SPLIT)

kernel_name = 'hybrid_gla_gmlp_mla_moe_deepnorm'

def layer_norm(x, g, b, eps=1e-5):
    xf = x.astype(jnp.float32)
    mu = jnp.mean(xf, -1, keepdims=True)
    var = jnp.mean(jnp.square(xf - mu), -1, keepdims=True)
    return ((xf - mu) * lax.rsqrt(var + eps)).astype(x.dtype) * g + b

def rms_norm(x, g, eps=1e-6):
    xf = x.astype(jnp.float32)
    return (xf * lax.rsqrt(jnp.mean(jnp.square(xf), -1, keepdims=True) + eps)).astype(x.dtype) * g

def rope(x, pos):
    half = x.shape[-1] // 2
    inv = ROPE_THETA ** (-jnp.arange(half, dtype=jnp.float32) / half)
    ang = pos.astype(jnp.float32)[:, None] * inv
    cos = jnp.cos(ang)[:, None, :]
    sin = jnp.sin(ang)[:, None, :]
    xf = x.astype(jnp.float32)
    x1, x2 = xf[..., :half], xf[..., half:]
    return jnp.concatenate([x1 * cos - x2 * sin, x1 * sin + x2 * cos], -1).astype(x.dtype)

def gla_chunked(q, k, v, glog):
    B, S, H, DK = q.shape
    DV = v.shape[-1]
    nc = S // CHUNK
    rs = lambda t: t.astype(jnp.float32).reshape(B, nc, CHUNK, H, t.shape[-1])
    q, k, v, glog = rs(q) * (DK ** -0.5), rs(k), rs(v), rs(glog)
    b = jnp.cumsum(glog, axis=2)
    b_last = b[:, :, -1:]
    q_dec = q * jnp.exp(b)
    k_inv = k * jnp.exp(-b)
    k_end = k * jnp.exp(b_last - b)
    causal = jnp.tril(jnp.ones((CHUNK, CHUNK), bool))
    att = jnp.where(causal, jnp.einsum('bcthd,bcshd->bchts', q_dec, k_inv), 0.0)
    o_intra = jnp.einsum('bchts,bcshv->bcthv', att, v)
    d_state = jnp.einsum('bcshk,bcshv->bchkv', k_end, v)
    decay = jnp.exp(b_last[:, :, 0])

    def step(state, inp):
        dec, ds = inp
        return dec[..., None] * state + ds, state

    init = jnp.zeros((B, H, DK, DV), jnp.float32)
    _, s_prev = lax.scan(step, init, (jnp.moveaxis(decay, 1, 0), jnp.moveaxis(d_state, 1, 0)))
    s_prev = jnp.moveaxis(s_prev, 0, 1)
    o_inter = jnp.einsum('bcthk,bchkv->bcthv', q_dec, s_prev)
    return (o_intra + o_inter).reshape(B, S, H, DV)

def spatial_gating(z, ln_g, ln_b, w_s, b_s):
    B, S, _ = z.shape
    u, v = jnp.split(jax.nn.gelu(z, approximate=False), 2, axis=-1)
    v = layer_norm(v, ln_g, ln_b).reshape(B, S // SG_BLOCK, SG_BLOCK, SG_GROUPS, SG_WIDTH // SG_GROUPS)
    w = jnp.where(jnp.tril(jnp.ones((SG_BLOCK, SG_BLOCK), bool)), w_s, 0)
    sv = jnp.einsum('gts,bnsgc->bntgc', w, v) + b_s.T[:, :, None]
    return u * sv.reshape(B, S, SG_WIDTH)

def mla_attention(q_down, kv_down, pos, qn_g, w_uq, kvn_g, w_ukv):
    B, S, _ = q_down.shape
    q = (rms_norm(q_down, qn_g) @ w_uq).reshape(B, S, MLA_HEADS, MLA_QK)
    c_kv, k_rope = jnp.split(kv_down, [MLA_KV_RANK], axis=-1)
    kv = (rms_norm(c_kv, kvn_g) @ w_ukv).reshape(B, S, MLA_HEADS, MLA_NOPE + MLA_V)
    k_nope, v = jnp.split(kv, [MLA_NOPE], axis=-1)
    q = jnp.concatenate([q[..., :MLA_NOPE], rope(q[..., MLA_NOPE:], pos)], -1)
    k_rope = jnp.broadcast_to(rope(k_rope[:, :, None, :], pos), (B, S, MLA_HEADS, MLA_ROPE))
    k = jnp.concatenate([k_nope, k_rope], -1)
    n_qb = S // Q_BLOCK
    qb = jnp.moveaxis(q.reshape(B, n_qb, Q_BLOCK, MLA_HEADS, MLA_QK), 1, 0)
    key_chunk = jnp.arange(S) // CHUNK
    scale = MLA_QK ** -0.5

    def attend(args):
        q_blk, qi = args
        s = jnp.einsum('bqhd,bkhd->bhqk', q_blk, k).astype(jnp.float32) * scale
        q_chunk = (qi * Q_BLOCK + jnp.arange(Q_BLOCK)) // CHUNK
        s = jnp.where(key_chunk[None, :] <= q_chunk[:, None], s, -jnp.inf)
        pr = jax.nn.softmax(s, axis=-1).astype(v.dtype)
        return jnp.einsum('bhqk,bkhd->bqhd', pr, v)

    o = lax.map(attend, (qb, jnp.arange(n_qb)))
    return jnp.moveaxis(o, 0, 1).reshape(B, S, MLA_HEADS * MLA_V)

def token_mixers(h, pos, w_in, fg_w, fg_b, gla_g, sg_g, sg_bn, sg_w, sg_b,
                 qn_g, w_uq, kvn_g, w_ukv, w_branch, w_out):
    B, S, _ = h.shape
    offs = np.cumsum(IN_SPLIT)[:-1].tolist()
    gq, gk, gv, gr, gfr, sgz, mq, mkv, gates = jnp.split(h @ w_in, offs, axis=-1)
    glog = jax.nn.log_sigmoid((gfr @ fg_w + fg_b).astype(jnp.float32)) / GLA_TAU
    o_a = gla_chunked(gq.reshape(B, S, GLA_HEADS, GLA_DK), gk.reshape(B, S, GLA_HEADS, GLA_DK),
                      gv.reshape(B, S, GLA_HEADS, GLA_DV), glog.reshape(B, S, GLA_HEADS, GLA_DK))
    o_a = rms_norm(o_a.astype(h.dtype), gla_g.reshape(GLA_HEADS, GLA_DV)).reshape(B, S, -1) * jax.nn.silu(gr)
    o_b = spatial_gating(sgz, sg_g, sg_bn, sg_w, sg_b)
    o_c = mla_attention(mq, mkv, pos, qn_g, w_uq, kvn_g, w_ukv)
    branches = jnp.stack([o_a, o_b, o_c], axis=2)
    proj = jnp.einsum('bsnc,ncd->bsnd', branches, w_branch)
    gate = jax.nn.sigmoid(gates).reshape(B, S, N_BRANCHES, D_MODEL)
    return (gate * proj).sum(2) @ w_out

def routed_experts(xt, idx, wts, w_gate, w_up, w_down):
    T, D = xt.shape
    A = T * TOP_K
    nb = -(-A // EXPERT_BLOCK) + N_EXPERTS
    e_flat = idx.reshape(A)
    tok = jnp.repeat(jnp.arange(T, dtype=jnp.int32), TOP_K)
    order = jnp.argsort(e_flat)
    e_sorted = e_flat[order]
    counts = jnp.bincount(e_flat, length=N_EXPERTS)
    padded = (counts + EXPERT_BLOCK - 1) // EXPERT_BLOCK * EXPERT_BLOCK
    pad_end = jnp.cumsum(padded)
    start = jnp.cumsum(counts) - counts
    dest = (pad_end - padded)[e_sorted] + jnp.arange(A) - start[e_sorted]
    slot_tok = jnp.full((nb * EXPERT_BLOCK,), T, jnp.int32).at[dest].set(tok[order])
    slot_w = jnp.zeros((nb * EXPERT_BLOCK,), wts.dtype).at[dest].set(wts.reshape(A)[order])
    blk_expert = jnp.minimum(jnp.searchsorted(pad_end, jnp.arange(nb) * EXPERT_BLOCK, side='right'),
                             N_EXPERTS - 1)
    x_pad = jnp.concatenate([xt, jnp.zeros((1, D), xt.dtype)], 0)

    def expert_block(args):
        tok_b, w_b, e = args
        xb = x_pad[tok_b]
        hb = jax.nn.silu(xb @ w_gate[e]) * (xb @ w_up[e])
        return (hb @ w_down[e]) * w_b[:, None]

    yb = lax.map(expert_block, (slot_tok.reshape(nb, EXPERT_BLOCK), slot_w.reshape(nb, EXPERT_BLOCK), blk_expert))
    y = jnp.zeros((T + 1, D), xt.dtype).at[slot_tok].add(yb.reshape(-1, D))
    return y[:T]

def moe_ffn(h, router_w, router_b, w_gate, w_up, w_down, sw_gate, sw_up, sw_down):
    B, S, D = h.shape
    T = B * S
    xt = h.reshape(T, D)
    scores = jax.nn.sigmoid((xt @ router_w).astype(jnp.float32))
    biased = scores + router_b.astype(jnp.float32)
    grp = biased.reshape(T, N_GROUPS, N_EXPERTS // N_GROUPS)
    grp_score = lax.top_k(grp, 2)[0].sum(-1)
    _, top_grp = lax.top_k(grp_score, TOPK_GROUPS)
    grp_mask = jax.nn.one_hot(top_grp, N_GROUPS).sum(1) > 0
    exp_mask = jnp.repeat(grp_mask, N_EXPERTS // N_GROUPS, axis=1)
    _, idx = lax.top_k(jnp.where(exp_mask, biased, -jnp.inf), TOP_K)
    wts = jnp.take_along_axis(scores, idx, axis=1)
    wts = wts / wts.sum(-1, keepdims=True) * ROUTED_SCALE
    routed = routed_experts(xt, idx, wts.astype(xt.dtype), w_gate, w_up, w_down)
    shared = (jax.nn.silu(xt @ sw_gate) * (xt @ sw_up)) @ sw_down
    return (routed + shared).reshape(B, S, D)

def setup_inputs(seed: int = 0) -> dict:
    key = jax.random.key(seed)
    ks = iter(jax.random.split(key, 40))
    L, D = DEPTH, D_MODEL

    def nrm(shape, scale):
        return jax.random.normal(next(ks), shape, jnp.float32) * scale

    def gain(shape):
        return 1.0 + nrm(shape, 0.02)

    return {
        'x': nrm((BATCH, SEQ, D), 1.0),
        'p': nrm((L, BATCH, SEQ, PLE_DIM), 1.0),
        'ln_in_g': gain((D,)),
        'ln_in_b': nrm((D,), 0.02),
        'w_in': nrm((L, D, D_IN), D ** -0.5),
        'gla_fg_w': nrm((L, GLA_GATE_RANK, GLA_HEADS * GLA_DK), GLA_GATE_RANK ** -0.5),
        'gla_fg_b': nrm((L, GLA_HEADS * GLA_DK), 0.1),
        'gla_norm_g': gain((L, GLA_HEADS * GLA_DV)),
        'sg_norm_g': gain((L, SG_WIDTH)),
        'sg_norm_b': nrm((L, SG_WIDTH), 0.02),
        'sg_w': nrm((L, SG_GROUPS, SG_BLOCK, SG_BLOCK), SG_BLOCK ** -0.5),
        'sg_b': gain((L, SG_GROUPS, SG_BLOCK)),
        'mla_qn_g': gain((L, MLA_Q_RANK)),
        'mla_w_uq': nrm((L, MLA_Q_RANK, MLA_HEADS * MLA_QK), MLA_Q_RANK ** -0.5),
        'mla_kvn_g': gain((L, MLA_KV_RANK)),
        'mla_w_ukv': nrm((L, MLA_KV_RANK, MLA_HEADS * (MLA_NOPE + MLA_V)), MLA_KV_RANK ** -0.5),
        'w_branch': nrm((L, N_BRANCHES, BRANCH_WIDTH, D), BRANCH_WIDTH ** -0.5),
        'w_out': nrm((L, D, D), BETA * D ** -0.5),
        'ln1_g': gain((L, D)),
        'ln1_b': nrm((L, D), 0.02),
        'router_w': nrm((L, D, N_EXPERTS), D ** -0.5),
        'router_b': nrm((L, N_EXPERTS), 0.01),
        'exp_w_gate': nrm((L, N_EXPERTS, D, D_EXPERT), D ** -0.5),
        'exp_w_up': nrm((L, N_EXPERTS, D, D_EXPERT), D ** -0.5),
        'exp_w_down': nrm((L, N_EXPERTS, D_EXPERT, D), BETA * D_EXPERT ** -0.5),
        'sh_w_gate': nrm((L, D, D_SHARED), D ** -0.5),
        'sh_w_up': nrm((L, D, D_SHARED), D ** -0.5),
        'sh_w_down': nrm((L, D_SHARED, D), BETA * D_SHARED ** -0.5),
        'ple_w_in': nrm((L, PLE_DIM, D), BETA * PLE_DIM ** -0.5),
        'ple_w_gate': nrm((L, D, D), D ** -0.5),
        'ln2_g': gain((L, D)),
        'ln2_b': nrm((L, D), 0.02),
    }

def reference(x, p, ln_in_g, ln_in_b, w_in, gla_fg_w, gla_fg_b, gla_norm_g, sg_norm_g, sg_norm_b,
              sg_w, sg_b, mla_qn_g, mla_w_uq, mla_kvn_g, mla_w_ukv, w_branch, w_out, ln1_g, ln1_b,
              router_w, router_b, exp_w_gate, exp_w_up, exp_w_down, sh_w_gate, sh_w_up, sh_w_down,
              ple_w_in, ple_w_gate, ln2_g, ln2_b):
    S = x.shape[1]
    pos = jnp.arange(S, dtype=jnp.int32)
    h = layer_norm(x, ln_in_g, ln_in_b)
    for i in range(DEPTH):
        mix = token_mixers(h, pos, w_in[i], gla_fg_w[i], gla_fg_b[i], gla_norm_g[i],
                           sg_norm_g[i], sg_norm_b[i], sg_w[i], sg_b[i],
                           mla_qn_g[i], mla_w_uq[i], mla_kvn_g[i], mla_w_ukv[i],
                           w_branch[i], w_out[i])
        h = layer_norm(ALPHA * h + mix, ln1_g[i], ln1_b[i])
        ffn = moe_ffn(h, router_w[i], router_b[i], exp_w_gate[i], exp_w_up[i], exp_w_down[i],
                      sh_w_gate[i], sh_w_up[i], sh_w_down[i])
        ple = (p[i] @ ple_w_in[i]) * jax.nn.sigmoid(h @ ple_w_gate[i])
        h = layer_norm(ALPHA * h + ffn + ple, ln2_g[i], ln2_b[i])
    return h


_drawn_inputs = setup_inputs


def setup_inputs(seed=0):
    import zlib

    import numpy as np

    out = dict(_drawn_inputs(seed))
    spreads = {}
    factors = {'gla_norm_g': 3.307,
     'sg_norm_g': 3.75,
     'sg_norm_b': 3.748,
     'sg_b': 3.89,
     'mla_qn_g': 6.334,
     'mla_kvn_g': 8.0}
    for name, (base, spread) in spreads.items():
        noise = np.random.default_rng([zlib.crc32(name.encode()), seed]).standard_normal(out[name].shape)
        drawn = base * np.exp(spread * noise) if base else spread * noise
        out[name] = __import__('jax').numpy.asarray(drawn.astype(out[name].dtype))
    for name, factor in factors.items():
        out[name] = (out[name] * factor).astype(out[name].dtype)
    return out
```

```python
from contextlib import ExitStack

import concourse.bass as bass
from concourse import mybir

F32 = mybir.dt.float32
I32 = mybir.dt.int32
ACT = mybir.ActivationFunctionType
ALU = mybir.AluOpType

P = 128
DEPTH = 2
S = 256
TILES = S // P
D = 1024
DC = D // P
CHUNK = 64
GH, GDK, GDV, GR = 4, 128, 256, 16
GATE_TAU = 16.0
SGW, SGG = 1024, 4
MH, QR, KVR, NOPE, ROPE, MV = 8, 384, 256, 128, 64, 128
QK = NOPE + ROPE
HALF = ROPE // 2
NE, NG, TOPG, TOPK, DE = 64, 8, 4, 8, 256
PLE = 256
ROUTED_SCALE = 2.5
ALPHA = (2 * DEPTH) ** 0.25
COL_GQ = 0
COL_GK = COL_GQ + GH * GDK
COL_GV = COL_GK + GH * GDK
COL_GR = COL_GV + GH * GDV
COL_GF = COL_GR + GH * GDV
COL_SG = COL_GF + GR
COL_MQ = COL_SG + 2 * SGW
COL_MKV = COL_MQ + QR
COL_GATE = COL_MKV + KVR + ROPE
SLOTS = 6
SLOT = 4096
BANKS = 8
LN_EPS, RMS_EPS = 1e-5, 1e-6
PARAMS = 12
LOW_FILL = -3.0e38
TAKEN = 3.0e38

JOBS = (
    [("hT", t, f) for t in range(2) for f in range(2)] + [("gfr",)]
    + [("q", i) for i in range(2)] + [("k", i) for i in range(2)] + [("fg", i) for i in range(2)]
    + [("v", j, t) for j in range(2) for t in range(2)] + [("gr", j, t) for j in range(2) for t in range(2)]
    + [("ke", t) for t in range(2)] + [("sgwT",)]
    + [x for h in range(GH + 1) for x in
       ([("att", h), ("ds", h, 0), ("ds", h, 1)] if h < GH else []) + ([("o", h - 1)] if h else [])]
    + [("sg", z, t) for z in range(4) for t in range(2)]
    + [("mq", t) for t in range(2)] + [("mkv", t) for t in range(2)]
    + [("oaT", t, f) for t in range(2) for f in range(2)]
    + [x for j in range(2) for t in range(2) for x in (("gate", 0, j, t), ("proj", 0, j, t))]
    + [("qnT", t) for t in range(2)] + [("ckT", t) for t in range(2)] + [("krT",)]
    + [("sv", t, i) for t in range(2) for i in range(2)]
    + [("obT", t, f) for t in range(2) for f in range(2)]
    + [x for j in range(2) for t in range(2) for x in (("gate", 1, j, t), ("proj", 1, j, t))]
    + [("qn", i) for i in range(4)] + [("qr", t) for t in range(2)]
    + [("kn", i) for i in range(4)] + [("vm", t, j) for t in range(2) for j in range(2)]
    + [("qrT", t) for t in range(2)]
    + [x for h in range(MH + 2) for x in
       ([("s", h)] if h < MH else []) + ([("pT", h - 1)] if 1 <= h <= MH else []) + ([("oc", h - 2)] if h >= 2 else [])]
    + [x for j in range(2) for t in range(2) for x in (("gate", 2, j, t), ("proj", 2, j, t))]
    + [("mT", t, f) for t in range(2) for f in range(2)]
    + [("wo", j, t) for j in range(2) for t in range(2)]
    + [("hT2", t, f) for t in range(2) for f in range(2)]
    + [("rt", t) for t in range(2)] + [("ppT",)]
    + [x for j in range(2) for t in range(2) for x in (("pli", j, t), ("plg", j, t))]
)
BANK, NTH, TOTAL = {}, {}, [0] * BANKS
for n_, key_ in enumerate(JOBS):
    BANK[key_] = n_ % BANKS
    TOTAL[n_ % BANKS] += 1
    NTH[key_] = TOTAL[n_ % BANKS]
GU_BANK, T_BANK = 4, 6
EXPERT_BASE = {b: TOTAL[b] for b in (4, 5, 6)}
for b_ in (4, 5, 6):
    TOTAL[b_] += NE + 1
for t_ in range(2):
    for j_ in range(2):
        b_ = 2 * t_ + j_
        TOTAL[b_] += 1
        BANK["y", t_, j_], NTH["y", t_, j_] = b_, TOTAL[b_]

LOADS = [
    ("gf", ("gfr",)), ("gq", ("q", 1)), ("gk", ("k", 1)), ("gv0", ("v", 0, 1)), ("gv1", ("v", 1, 1)),
    ("gr0", ("gr", 0, 1)), ("gr1", ("gr", 1, 1)), ("sg0", ("sg", 0, 1)), ("sg1", ("sg", 1, 1)),
    ("sg2", ("sg", 2, 1)), ("sg3", ("sg", 3, 1)), ("mq", ("mq", 1)), ("mkv", ("mkv", 1)),
]
for n_ in range(3):
    if n_ == 2:
        LOADS += [("uq0", ("qr", 1)), ("uq1", ("qr", 1)), ("uq2", ("qr", 1)), ("ukv", ("vm", 1, 1))]
    for j_ in range(2):
        LOADS += [(f"g{n_}{j_}", ("gate", n_, j_, 1)), (f"b{n_}{j_}", ("proj", n_, j_, 1))]
LOADS += [("wo0", ("wo", 0, 1)), ("wo1", ("wo", 1, 1)), ("shgu", "shared"), ("rt", "shared_down"),
          ("pli", ("pli", 1, 1)), ("plg0", ("plg", 0, 1)), ("plg1", ("plg", 1, 1))]
LOADS = [x for x in LOADS if x[0] != "gf"]
LOADS = [("gf", ("gfr",))] + LOADS
assert len(LOADS) == 36, len(LOADS)
assert len(LOADS) % SLOTS == 0
POS = {name: n for n, (name, _) in enumerate(LOADS)}
DMAS = {"shgu": 2, "rt": 2}
LANDED, SLOT_DMAS = {}, [0] * SLOTS
for n_, (name_, _) in enumerate(LOADS):
    SLOT_DMAS[n_ % SLOTS] += DMAS.get(name_, 1)
    LANDED[name_] = SLOT_DMAS[n_ % SLOTS]
TRUNK_DMAS = list(SLOT_DMAS)
ROUNDS = NE // 4
EXPERT_DMAS = [2, 2, 1, 2, 2, 1]
SLOT_DMAS = [a + ROUNDS * b for a, b in zip(TRUNK_DMAS, EXPERT_DMAS)]


def build_trunk(nc, w, cos_tab, sin_tab, out):
    with ExitStack() as ctx:
        sb = lambda name, shape, dt=F32: ctx.enter_context(nc.sbuf_tensor(name, shape, dt))
        sem = lambda name: ctx.enter_context(nc.semaphore(name))

        ring = sb("ring", [P, SLOTS, SLOT])
        h = sb("h", [P, TILES, D])
        hT = sb("hT", [P, DC, S])
        bT = sb("bT", [P, DC, S])
        mixed = sb("mixed", [P, TILES, D])
        arena = sb("arena", [P, 11520])
        ident = sb("ident", [P, P])
        gla_mask = sb("gla_mask", [P, TILES, P], I32)
        restart = sb("restart", [P, S])
        cos_t = sb("cos_t", [P, TILES, HALF])
        sin_t = sb("sin_t", [P, TILES, HALF])
        ln_g = sb("ln_g", [P, D])
        ln_b = sb("ln_b", [P, D])
        sgn_g = sb("sgn_g", [P, SGW])
        sgn_b = sb("sgn_b", [P, SGW])
        sgw = sb("sgw", [P, SGG, P])
        sgwT = sb("sgwT", [P, SGG, P])
        sgb = sb("sgb", [P, SGG])
        gsig = sb("gsig", [P, 2, 512])
        junk = gsig
        gfrT = sb("gfrT", [GR, S])
        fgw = sb("fgw", [GR, GH * GDK])
        fgb = sb("fgb", [P, GH])
        glag = sb("glag", [P, DC])
        qng = sb("qng", [P, QR // P])
        kvng = sb("kvng", [P, KVR // P])
        rbias = sb("rbias", [P, NE])
        ssq = sb("ssq", [P, 16])
        rstd = sb("rstd", [P, 16])
        neg_half = sb("neg_half", [P, 8])
        stats = sb("stats", [P, TILES, 2, 6])
        mv = sb("mv", [P, TILES, 2])
        decay = sb("decay", [P, GH, S // CHUNK])
        earlier = sb("earlier", [P, NG, NG])
        sm_top = sb("sm_top", [P, 2, 2])
        sm_max = sb("sm_max", [P, 2, 2])
        sm_sum = sb("sm_sum", [P, 2, 2])
        sm_inv = sb("sm_inv", [P, 2, 2])

        def carve(start, *shape):
            size = 1
            for x in shape:
                size *= x
            view = arena[:, start:start + size]
            if len(shape) == 2:
                view = view.rearrange("p (a b) -> p a b", a=shape[0])
            if len(shape) == 3:
                view = view.rearrange("p (a b c) -> p a b c", a=shape[0], b=shape[1])
            return view

        qd, ki, b_cum, tmp_e, keT = (carve(i * 1024, GH, S) for i in range(5))
        ke = carve(5 * 1024, TILES, GH * GDK)
        gv = carve(6144, TILES, GH * GDV)
        gr = carve(8192, TILES, GH * GDV)
        att = carve(10240, 2, TILES * P)
        state = carve(10752, 3, GDV)
        u = carve(0, TILES, SGW)
        vv = carve(2048, TILES, SGW)
        mq = carve(4096, TILES, QR)
        mkv = carve(4864, TILES, KVR + ROPE)
        qnT = carve(5504, QR // P, S)
        ckT = carve(6272, KVR // P, S)
        rtmp = carve(6784, 4, MH * HALF)
        krot = carve(7808, TILES, P)
        qnope = carve(8192, MH, S)
        qrT = carve(10240, 4, S)
        krT = carve(11264, S)
        knope = carve(0, MH, S)
        vm = carve(2048, TILES, MH * MV)
        prob = carve(6784, 2, 384)
        pT = carve(5120, 2, 384)
        qrot = carve(4096, 2, 512)
        regions = [(slice(CHUNK * i, CHUNK * i + CHUNK), P * t, P * t + CHUNK * (i + 1)) for t in range(2) for i in range(2)]
        pleT = carve(0, PLE // P, S)
        ptok = carve(512, TILES, PLE)
        sgate = carve(1024, TILES, DE)
        hb = carve(1536, 2, TILES * DE)
        hbT = carve(2560, 2, S)
        score = carve(3072, TILES, NE)
        biased = carve(3200, TILES, NE)
        wts = carve(3328, TILES, NE)
        grp8 = carve(3456, NG, 8)
        gsum = carve(3520, NG)
        cmp = carve(3584, NG, NG)
        cmp2 = carve(3648, NG, NG)
        top8 = carve(3712, 8)
        rep = carve(3776, NE)
        wsum = carve(3840, 2)
        gkeep = carve(3856, NG)

        psum = ctx.enter_context(nc.psum_tensor("psum", [P, BANKS, 512], F32))

        bank_filled = [sem(f"bank_filled{b}") for b in range(BANKS)]
        bank_drained = [sem(f"bank_drained{b}") for b in range(BANKS)]
        slot_loaded = [sem(f"slot_loaded{s}") for s in range(SLOTS)]
        names = dict(params_loaded=16 * PARAMS, ln2_loaded=32, p_loaded=16, h_ready=1, ln1_done=1, var_ready=3,
                     rstd_ready=3, ms_ready=GH + 2, rms_ready=GH + 2, sgw_masked=1, abs_ready=1, log_ready=1,
                     cum_ready=2, exp_ready=3, ke_ready=1, vln_ready=1, krot_ready=1, qrot_ready=2,
                     max_ready=MH, exp_p=MH, prob_ready=MH, silu_ready=2 * (NE + 1), expert_down_done=NE + 1)
        sems = {k: sem(k) for k in names}
        settled = {k: sem(f"settled_{k}") for k in ("SP", "Pool", "DVE")}
        setup_done, x_loaded, tables_loaded, var_in_ready, rstd_in_ready, dve_chain, act_chain, pool_chain, out_stored = (
            sem(k) for k in ("setup_done", "x_loaded", "tables_loaded", "var_in_ready", "rstd_in_ready", "dve_chain",
                             "act_chain", "pool_chain", "out_stored"))

        def settle(eng):
            eng.sem_inc(settled[eng.engine.name], 1)

        def filled(eng, l, key, more=0):
            b = BANK[key]
            eng.wait_ge(bank_filled[b], l * TOTAL[b] + (NTH[key] + more))

        def drained(eng, l, key, before=False):
            b = BANK[key]
            n = NTH[key] - before
            if n > 0:
                eng.wait_ge(bank_drained[b], l * TOTAL[b] + (n - TOTAL[b]))

        def signal(eng, l, name, n):
            eng.wait_ge(sems[name], l * names[name] + (n - names[name]))

        def loaded(eng, l, name):
            s = POS[name] % SLOTS
            eng.wait_ge(slot_loaded[s], l * (16 * SLOT_DMAS[s]) + 16 * (LANDED[name] - SLOT_DMAS[s]))

        def slot(name, chunks, cols):
            return ring[:, POS[name] % SLOTS, 0:chunks * cols].rearrange("p (c n) -> p c n", c=chunks)

        def bank(key):
            return psum[:, BANK[key], :]

        def layer_of(name, l):
            return w[name][bass.ds(l - 1, 1)]

        block = ctx.enter_context(nc.Block())

        @block.sync
        def _(sp):
            def cols(l, a, n):
                return layer_of("w_in", l).rearrange("o (p c) n -> p (o c) n", c=DC)[:, :, a:a + n]

            def source(name, l):
                if name == "gf":
                    return [(slot(name, DC, GR), cols(l, COL_GF, GR))]
                if name == "gq":
                    return [(slot(name, DC, 512), cols(l, COL_GQ, 512))]
                if name == "gk":
                    return [(slot(name, DC, 512), cols(l, COL_GK, 512))]
                if name[:2] in ("gv", "gr", "sg"):
                    a = {"gv": COL_GV, "gr": COL_GR, "sg": COL_SG}[name[:2]] + 512 * int(name[2])
                    return [(slot(name, DC, 512), cols(l, a, 512))]
                if name == "mq":
                    return [(slot(name, DC, QR), cols(l, COL_MQ, QR))]
                if name == "mkv":
                    return [(slot(name, DC, KVR + ROPE), cols(l, COL_MKV, KVR + ROPE))]
                if name[0] == "g":
                    a = COL_GATE + int(name[1]) * D + 512 * int(name[2])
                    return [(slot(name, DC, 512), cols(l, a, 512))]
                if name[0] == "b":
                    n, j = int(name[1]), int(name[2])
                    src = w["w_branch"][bass.ds(l - 1, 1), n].rearrange("o (c p) n -> p (o c) n", p=P)
                    return [(slot(name, DC, 512), src[:, :, 512 * j:512 * j + 512])]
                if name[:2] == "uq":
                    c = int(name[2])
                    src = layer_of("mla_w_uq", l)[:, P * c:P * c + P].rearrange("o p n -> p (o n)")
                    return [(ring[:, POS[name] % SLOTS, 0:MH * QK], src)]
                if name == "ukv":
                    return [(slot(name, 2, 2048), layer_of("mla_w_ukv", l).rearrange("o (c p) n -> p (o c) n", p=P))]
                if name[:2] == "wo":
                    j = int(name[2])
                    src = layer_of("w_out", l).rearrange("o (c p) n -> p (o c) n", p=P)
                    return [(slot(name, DC, 512), src[:, :, 512 * j:512 * j + 512])]
                if name == "shgu":
                    return [(ring[:, POS[name] % SLOTS, i * 2048:i * 2048 + 2048],
                             layer_of(k, l).rearrange("o (p c) n -> p (o c n)", c=DC))
                            for i, k in enumerate(("sh_w_gate", "sh_w_up"))]
                if name == "rt":
                    s = POS[name] % SLOTS
                    return [(ring[:, s, 0:2048], layer_of("sh_w_down", l).rearrange("o (p c) n -> p (o c n)", c=2)),
                            (ring[:, s, 2048:2560], layer_of("router_w", l).rearrange("o (p c) n -> p (o c n)", c=DC))]
                if name == "pli":
                    return [(slot(name, 2, D), layer_of("ple_w_in", l).rearrange("o (c p) n -> p (o c) n", p=P))]
                j = int(name[3])
                src = layer_of("ple_w_gate", l).rearrange("o (p c) n -> p (o c) n", c=DC)
                return [(slot(name, DC, 512), src[:, :, 512 * j:512 * j + 512])]

            def expert_loads(l, i, wait):
                for s in range(SLOTS):
                    wait(s)
                    settle(sp)
                    if s % 3 < 2:
                        e = 4 * i + (2 * (s // 3) + s % 3)
                        for k, name in enumerate(("exp_w_gate", "exp_w_up")):
                            src = w[name][bass.ds(l - 1, 1), bass.ds(e, 1)].rearrange("o e (p c) n -> p (o e c n)", c=DC)
                            sp.dma_start(ring[:, s, 2048 * k:2048 * k + 2048], src).then_inc(slot_loaded[s], 16)
                    else:
                        e = 4 * i + 2 * (s // 3)
                        src = w["exp_w_down"][bass.ds(l - 1, 1), bass.ds(e, 2)].rearrange("o e (p c) n -> p (o e) (c n)", c=2)
                        sp.dma_start(ring[:, s, :].rearrange("p (e n) -> p e n", e=2), src).then_inc(slot_loaded[s], 16)

            def expert_slot_free(l, i, s):
                if s % 3 < 2:
                    n = 2 * (s // 3) + s % 3 + 1
                    sp.wait_ge(bank_filled[GU_BANK + 1], l * TOTAL[5] + (4 * i + (EXPERT_BASE[5] + n + 1)))
                else:
                    n = 2 * (s // 3) + 2
                    sp.wait_ge(sems["expert_down_done"], l * (NE + 1) + (4 * i + (n + 1)))

            with sp.Fori(1, DEPTH + 1) as l:
                for n, (name, _) in enumerate(LOADS):
                    if n < SLOTS:
                        expert_slot_free(l - 1, ROUNDS - 1, n)
                    else:
                        filled(sp, l, LOADS[n - SLOTS][1])
                    settle(sp)
                    for dst, src in source(name, l):
                        sp.dma_start(dst, src).then_inc(slot_loaded[n % SLOTS], 16)

                def trunk_slot_free(s):
                    last = LOADS[len(LOADS) - SLOTS + s][1]
                    if last == "shared":
                        sp.wait_ge(bank_filled[GU_BANK + 1], l * TOTAL[5] + (EXPERT_BASE[5] + 1))
                    elif last == "shared_down":
                        sp.wait_ge(sems["expert_down_done"], l * (NE + 1) + 1)
                    else:
                        filled(sp, l, last)

                expert_loads(l, 0, trunk_slot_free)
                with sp.Fori(1, ROUNDS) as i:
                    expert_loads(l, i, lambda s: expert_slot_free(l, i - 1, s))
            sp.wait_ge(sems["h_ready"], DEPTH + 1)
            sp.dma_start(out.rearrange("b (t p) d -> p (b t) d", p=P), h[:]).then_inc(out_stored, 16)
            sp.wait_ge(out_stored, 16)

        @block.gpsimd
        def _(pool):
            chain = [0]

            def link(ins):
                chain[0] += 1
                ins.then_inc(pool_chain, 1)
                pool.wait_ge(pool_chain, chain[0])

            pool.dma_start(h[:], w["x"].rearrange("b (t p) d -> p (b t) d", p=P)).then_inc(x_loaded, 16)
            pool.dma_start(ln_g[:], w["ln_in_g"].partition_broadcast(P)).then_inc(x_loaded, 16)
            pool.dma_start(ln_b[:], w["ln_in_b"].partition_broadcast(P)).then_inc(x_loaded, 16)
            pool.dma_start(cos_t[:], cos_tab.rearrange("(t p) i -> p t i", p=P)).then_inc(tables_loaded, 16)
            pool.dma_start(sin_t[:], sin_tab.rearrange("(t p) i -> p t i", p=P)).then_inc(tables_loaded, 16)
            link(pool.memset(neg_half[:], -0.5))
            link(pool.memset(ident[:], 0.0))
            link(pool.affine_select(out=ident[:], in_=ident[:], compare_op=ALU.not_equal, fill=1.0, base=0,
                                    pattern=[[-1, P]], channel_multiplier=1))
            link(pool.memset(gla_mask[:], 1))
            link(pool.affine_select(out=gla_mask[:], in_=gla_mask[:], compare_op=ALU.is_ge, fill=0.0, base=0,
                                    pattern=[[0, TILES], [1, P]], channel_multiplier=-1))
            right = gla_mask[:, :, CHUNK:P]
            link(pool.affine_select(out=right, in_=right, compare_op=ALU.is_ge, fill=0.0, base=-CHUNK,
                                    pattern=[[0, TILES], [0, P - CHUNK]], channel_multiplier=1))
            link(pool.memset(restart[:], 1.0))
            link(pool.memset(restart[:, 0:S:CHUNK], 0.0))
            link(pool.memset(earlier[:], 1.0))
            pool.affine_select(out=earlier[:], in_=earlier[:], compare_op=ALU.is_gt, fill=0.0, base=0,
                               pattern=[[1, NG], [-1, NG]], channel_multiplier=0).then_inc(setup_done, 1)

            def rsqrt(x):
                return pool.tensor_tensor(x, x, neg_half[:, 0:2], ALU.pow)

            pool.wait_ge(var_in_ready, 1)
            rsqrt(rstd[:, 0:2]).then_inc(rstd_in_ready, 1)

            with pool.Fori(1, DEPTH + 1) as l:
                signal(pool, l, "h_ready", 1)
                settle(pool)

                def small(dst, src):
                    pool.dma_start(dst, src).then_inc(sems["params_loaded"], 16)

                row = lambda name: layer_of(name, l).partition_broadcast(P).rearrange("p o n -> p (o n)")
                with nc.allow_non_contiguous_dma(reason="per-channel vectors onto partitions"):
                    small(fgw[:], layer_of("gla_fg_w", l).rearrange("o r n -> r (o n)"))
                    small(fgb[:], layer_of("gla_fg_b", l).rearrange("o (c p) -> p (o c)", p=P))
                    small(glag[:], layer_of("gla_norm_g", l).rearrange("o (c p) -> p (o c)", p=P))
                    small(qng[:], layer_of("mla_qn_g", l).rearrange("o (c p) -> p (o c)", p=P))
                    small(kvng[:], layer_of("mla_kvn_g", l).rearrange("o (c p) -> p (o c)", p=P))
                    small(sgb[:], layer_of("sg_b", l).rearrange("o g t -> t (o g)"))
                small(sgw[:], layer_of("sg_w", l).rearrange("o g t s -> t (o g) s"))
                small(sgn_g[:], row("sg_norm_g"))
                small(sgn_b[:], row("sg_norm_b"))
                small(ln_g[:], row("ln1_g"))
                small(ln_b[:], row("ln1_b"))
                small(rbias[:], row("router_b"))
                pool.wait_ge(sems["params_loaded"], l * (16 * PARAMS))
                settle(pool)
                pool.affine_select(out=sgw[:], in_=sgw[:], compare_op=ALU.is_ge, fill=0.0, base=0,
                                   pattern=[[0, SGG], [-1, P]], channel_multiplier=1).then_inc(sems["sgw_masked"], 1)
                for i in range(GH):
                    signal(pool, l, "ms_ready", i + 1)
                    rsqrt(rstd[:, 2 * i:2 * i + 2]).then_inc(sems["rms_ready"], 1)
                for i in range(2):
                    signal(pool, l, "ms_ready", GH + i + 1)
                    rsqrt(rstd[:, 8 + 2 * i:10 + 2 * i]).then_inc(sems["rms_ready"], 1)
                signal(pool, l, "var_ready", 1)
                rsqrt(rstd[:, 12:14]).then_inc(sems["rstd_ready"], 1)
                signal(pool, l, "var_ready", 2)
                rsqrt(rstd[:, 12:14]).then_inc(sems["rstd_ready"], 1)
                signal(pool, l, "ln1_done", 1)
                settle(pool)
                pool.dma_start(ptok, w["p"][bass.ds(l - 1, 1)].rearrange("l b (t p) d -> p (l b t) d", p=P)
                               ).then_inc(sems["p_loaded"], 16)
                pool.dma_start(ln_g[:], row("ln2_g")).then_inc(sems["ln2_loaded"], 16)
                pool.dma_start(ln_b[:], row("ln2_b")).then_inc(sems["ln2_loaded"], 16)
                signal(pool, l, "var_ready", 3)
                rsqrt(rstd[:, 12:14]).then_inc(sems["rstd_ready"], 1)

        @block.tensor
        def _(pe):
            for b in range(BANKS):
                pe.sem_inc(bank_filled[b], TOTAL[b])
            pe.sem_inc(sems["expert_down_done"], NE + 1)
            pe.wait_ge(setup_done, 1)

            def rows(t):
                return slice(t * P, t * P + P)

            with pe.Fori(1, DEPTH + 1) as l:

                def transposes(key, tiles):
                    drained(pe, l, key, before=True)
                    for i, x in enumerate(tiles):
                        last = pe.transpose(bank(key)[:, i * P:i * P + P], x, ident[:])
                    last.then_inc(bank_filled[BANK[key]], 1)

                def by_token(key, name, t, left, cols, chunks=DC, at=None):
                    drained(pe, l, key, before=True)
                    src = slot(name, chunks, cols) if at is None else at
                    for c in range(chunks):
                        last = pe.matmul(bank(key)[:, 0:cols], left[:, c, rows(t)], src[:, c, :],
                                         start=c == 0, stop=c == chunks - 1)
                    last.then_inc(bank_filled[BANK[key]], 1)

                def by_channel(key, stationary, right, m=P):
                    drained(pe, l, key, before=True)
                    for i, blocks in enumerate(stationary):
                        for c, x in enumerate(blocks):
                            last = pe.matmul(bank(key)[0:m, i * S:i * S + S], x, right[:, c, :],
                                             start=c == 0, stop=c == len(blocks) - 1)
                    last.then_inc(bank_filled[BANK[key]], 1)

                signal(pe, l, "h_ready", 1)
                for t in range(2):
                    for f in range(2):
                        transposes(("hT", t, f), [h[:, t, 4 * f + i:D:DC] for i in range(4)])
                for t in range(2):
                    for f in range(2):
                        drained(pe, l, ("hT", t, f))
                loaded(pe, l, "gf")
                by_channel(("gfr",), [[slot("gf", DC, GR)[:, c, :] for c in range(DC)]], hT, m=GR)
                for kind, name in (("q", "gq"), ("k", "gk")):
                    loaded(pe, l, name)
                    for i in range(2):
                        by_channel((kind, i), [[slot(name, DC, 512)[:, c, (2 * i + n) * P:(2 * i + n + 1) * P]
                                                for c in range(DC)] for n in range(2)], hT)
                pe.wait_ge(sems["params_loaded"], l * (16 * PARAMS))
                drained(pe, l, ("gfr",))
                for i in range(2):
                    drained(pe, l, ("fg", i), before=True)
                    for n in range(2):
                        last = pe.matmul(bank(("fg", i))[:, n * S:n * S + S], fgw[:, (2 * i + n) * P:(2 * i + n + 1) * P],
                                         gfrT[:], start=True, stop=True)
                    last.then_inc(bank_filled[BANK["fg", i]], 1)
                for kind, name in (("v", "gv"), ("gr", "gr")):
                    for j in range(2):
                        loaded(pe, l, f"{name}{j}")
                        for t in range(2):
                            by_token((kind, j, t), f"{name}{j}", t, hT, 512)
                signal(pe, l, "ke_ready", 1)
                for t in range(2):
                    transposes(("ke", t), [keT[:, n, rows(t)] for n in range(GH)])
                signal(pe, l, "sgw_masked", 1)
                transposes(("sgwT",), [sgw[:, g, :] for g in range(SGG)])
                for j in range(2):
                    for t in range(2):
                        drained(pe, l, ("v", j, t))
                for t in range(2):
                    drained(pe, l, ("ke", t))
                for n in range(GH + 1):
                    if n < GH:
                        key = ("att", n)
                        drained(pe, l, key, before=True)
                        for t in range(2):
                            last = pe.matmul(bank(key)[:, rows(t)], ki[:, n, rows(t)], qd[:, n, rows(t)],
                                             start=True, stop=True)
                        last.then_inc(bank_filled[BANK[key]], 1)
                        for c in (0, 2, 1):
                            key = ("ds", n, c % 2)
                            if c < 2:
                                drained(pe, l, key, before=True)
                            part = slice(CHUNK * (c % 2), CHUNK * (c % 2) + CHUNK)
                            last = pe.matmul(bank(key)[:, GDV * (c // 2):GDV * (c // 2) + GDV],
                                             ke[part, c // 2, n * P:n * P + P], gv[part, c // 2, n * GDV:(n + 1) * GDV],
                                             start=True, stop=True)
                            if c:
                                last.then_inc(bank_filled[BANK[key]], 1)
                    if n:
                        key, m = ("o", n - 1), n - 1
                        drained(pe, l, key, before=True)
                        drained(pe, l, ("att", m))
                        drained(pe, l, ("ds", m, 0))
                        for c in range(S // CHUNK):
                            t, queries = c // 2, slice(CHUNK * c, CHUNK * c + CHUNK)
                            o = bank(key)[CHUNK * (c % 2):CHUNK * (c % 2) + CHUNK, t * GDV:(t + 1) * GDV]
                            last = pe.matmul(o, att[:, m % 2, queries], gv[:, t, m * GDV:(m + 1) * GDV],
                                             start=True, stop=c == 0)
                            if c:
                                last = pe.matmul(o, qd[:, m, queries], state[:, c - 1, :], start=False, stop=True)
                        last.then_inc(bank_filled[BANK[key]], 1)
                for z in range(4):
                    loaded(pe, l, f"sg{z}")
                    for t in range(2):
                        by_token(("sg", z, t), f"sg{z}", t, hT, 512)
                for kind, n in (("mq", QR), ("mkv", KVR + ROPE)):
                    loaded(pe, l, kind)
                    for t in range(2):
                        by_token((kind, t), kind, t, hT, n)

                def branch(n):
                    for j in range(2):
                        loaded(pe, l, f"g{n}{j}")
                        loaded(pe, l, f"b{n}{j}")
                        for t in range(2):
                            by_token(("gate", n, j, t), f"g{n}{j}", t, hT, 512)
                            by_token(("proj", n, j, t), f"b{n}{j}", t, bT, 512)

                drained(pe, l, ("o", GH - 1))
                for t in range(2):
                    for f in range(2):
                        transposes(("oaT", t, f), [gr[:, t, (4 * f + i) * P:(4 * f + i + 1) * P] for i in range(4)])
                for t in range(2):
                    for f in range(2):
                        drained(pe, l, ("oaT", t, f))
                branch(0)
                for t in range(2):
                    drained(pe, l, ("mq", t))
                    transposes(("qnT", t), [mq[:, t, c * P:c * P + P] for c in range(QR // P)])
                for t in range(2):
                    drained(pe, l, ("mkv", t))
                    transposes(("ckT", t), [mkv[:, t, c * P:c * P + P] for c in range(KVR // P)])
                signal(pe, l, "krot_ready", 1)
                transposes(("krT",), [krot[:, t, :] for t in range(2)])
                drained(pe, l, ("sgwT",))
                signal(pe, l, "vln_ready", 1)
                for t in range(2):
                    for i in range(2):
                        key = ("sv", t, i)
                        drained(pe, l, key, before=True)
                        for n in range(2):
                            g = 2 * i + n
                            last = pe.matmul(bank(key)[:, n * 256:n * 256 + 256], sgwT[:, g, :],
                                             vv[:, t, g * 256:g * 256 + 256], start=True, stop=True)
                        last.then_inc(bank_filled[BANK[key]], 1)
                for t in range(2):
                    for i in range(2):
                        drained(pe, l, ("sv", t, i))
                    for f in range(2):
                        transposes(("obT", t, f), [u[:, t, (4 * f + i) * P:(4 * f + i + 1) * P] for i in range(4)])
                for t in range(2):
                    for f in range(2):
                        drained(pe, l, ("obT", t, f))
                branch(1)
                for c in range(3):
                    loaded(pe, l, f"uq{c}")
                uq = [ring[:, POS[f"uq{c}"] % SLOTS, 0:MH * QK].rearrange("p (h n) -> p h n", h=MH) for c in range(3)]
                for t in range(2):
                    drained(pe, l, ("qnT", t))
                    drained(pe, l, ("ckT", t))
                drained(pe, l, ("krT",))
                for i in range(4):
                    by_channel(("qn", i), [[uq[c][:, 2 * i + n, 0:NOPE] for c in range(3)] for n in range(2)], qnT)
                for t in range(2):
                    key = ("qr", t)
                    drained(pe, l, key, before=True)
                    for c in range(3):
                        last = pe.matmul(bank(key), qnT[:, c, rows(t)], uq[c][:, :, NOPE:QK], start=c == 0, stop=c == 2)
                    last.then_inc(bank_filled[BANK[key]], 1)
                loaded(pe, l, "ukv")
                ukv = slot("ukv", 2, 2048).rearrange("p c (h n) -> p c h n", h=MH)
                for i in range(4):
                    by_channel(("kn", i), [[ukv[:, c, 2 * i + n, 0:NOPE] for c in range(2)] for n in range(2)], ckT)
                for t in range(2):
                    for j in range(2):
                        key = ("vm", t, j)
                        drained(pe, l, key, before=True)
                        for c in range(2):
                            last = pe.matmul(bank(key), ckT[:, c, rows(t)], ukv[:, c, 4 * j:4 * j + 4, NOPE:NOPE + MV],
                                             start=c == 0, stop=c == 1)
                        last.then_inc(bank_filled[BANK[key]], 1)
                for t in range(2):
                    signal(pe, l, "qrot_ready", t + 1)
                    transposes(("qrT", t), [qrot[:, t, i * P:i * P + P] for i in range(4)])
                for i in range(4):
                    drained(pe, l, ("qn", i))
                    drained(pe, l, ("kn", i))
                for t in range(2):
                    drained(pe, l, ("qrT", t))
                    for j in range(2):
                        drained(pe, l, ("vm", t, j))
                for n in range(MH + 2):
                    if n < MH:
                        key = ("s", n)
                        drained(pe, l, key, before=True)
                        part = slice(ROPE * (n % 2), ROPE * (n % 2) + ROPE)
                        for t in range(2):
                            o, keys = bank(key)[:, P * t:P * t + P * (t + 1)], P * (t + 1)
                            pe.matmul(o, qnope[:, n, rows(t)], knope[:, n, 0:keys], start=True, stop=False)
                            last = pe.matmul(o, qrT[part, n // 2, rows(t)], krT[part, 0:keys], start=False, stop=True)
                        last.then_inc(bank_filled[BANK[key]], 1)
                    if 1 <= n <= MH:
                        signal(pe, l, "prob_ready", n)
                        m = (n - 1) % 2
                        transposes(("pT", n - 1), [prob[:, m, 0:128], prob[:, m, 128:256], prob[:, m, 256:384]])
                    if n >= 2:
                        key, m = ("oc", n - 2), n - 2
                        drained(pe, l, key, before=True)
                        drained(pe, l, ("pT", m))
                        pe.matmul(bank(key)[:, 0:S], vm[:, 0, m * MV:(m + 1) * MV], pT[:, m % 2, 0:S], start=True, stop=False)
                        pe.matmul(bank(key)[:, P:S], vm[:, 1, m * MV:(m + 1) * MV], pT[:, m % 2, S:S + P],
                                  start=False, stop=True).then_inc(bank_filled[BANK[key]], 1)
                for n in range(MH):
                    drained(pe, l, ("oc", n))
                branch(2)
                for j in range(2):
                    for t in range(2):
                        drained(pe, l, ("proj", 2, j, t))
                for t in range(2):
                    for f in range(2):
                        transposes(("mT", t, f), [mixed[:, t, (4 * f + i) * P:(4 * f + i + 1) * P] for i in range(4)])
                for t in range(2):
                    for f in range(2):
                        drained(pe, l, ("mT", t, f))
                for j in range(2):
                    loaded(pe, l, f"wo{j}")
                    for t in range(2):
                        by_token(("wo", j, t), f"wo{j}", t, bT, 512)
                signal(pe, l, "ln1_done", 1)
                for t in range(2):
                    for f in range(2):
                        transposes(("hT2", t, f), [h[:, t, 4 * f + i:D:DC] for i in range(4)])
                for t in range(2):
                    for f in range(2):
                        drained(pe, l, ("hT2", t, f))
                loaded(pe, l, "rt")
                router = ring[:, POS["rt"] % SLOTS, 2048:2560].rearrange("p (c n) -> p c n", c=DC)
                for t in range(2):
                    by_token(("rt", t), "rt", t, hT, NE, at=router)
                signal(pe, l, "p_loaded", 16)
                transposes(("ppT",), [ptok[:, t, c * P:c * P + P] for c in range(2) for t in range(2)])
                drained(pe, l, ("ppT",))
                loaded(pe, l, "pli")
                for j in range(2):
                    loaded(pe, l, f"plg{j}")
                    for t in range(2):
                        by_token(("pli", j, t), "pli", t, pleT, 512, chunks=2,
                                 at=slot("pli", 2, D)[:, :, 512 * j:512 * j + 512])
                        by_token(("plg", j, t), f"plg{j}", t, hT, 512)

                def gate_up(s, t, i, k):
                    b = GU_BANK + t
                    pe.wait_ge(bank_drained[b], l * TOTAL[b] + (4 * i + (EXPERT_BASE[b] + k - TOTAL[b])))
                    src = ring[:, s, :].rearrange("p (g c n) -> p g c n", g=2, c=DC)
                    for c in range(DC):
                        last = pe.matmul(psum[:, b, :], hT[:, c, rows(t)], src[:, :, c, :], start=c == 0, stop=c == DC - 1)
                    last.then_inc(bank_filled[b], 1)

                def turn(i, k):
                    for t in range(2):
                        b = GU_BANK + t
                        pe.wait_ge(bank_drained[b], l * TOTAL[b] + (4 * i + (EXPERT_BASE[b] + k + 1 - TOTAL[b])))
                    pe.wait_ge(bank_drained[T_BANK], l * TOTAL[T_BANK] + (4 * i + (EXPERT_BASE[T_BANK] + k - TOTAL[T_BANK])))
                    for c in range(2):
                        for t in range(2):
                            last = pe.transpose(psum[:, T_BANK, (2 * c + t) * P:(2 * c + t + 1) * P],
                                                hb[:, k % 2, t * DE + c:(t + 1) * DE:2], ident[:])
                    last.then_inc(bank_filled[T_BANK], 1)

                def down(weights, i, k, first=False, last_one=False):
                    pe.wait_ge(bank_drained[T_BANK], l * TOTAL[T_BANK] + (4 * i + (EXPERT_BASE[T_BANK] + k + 1 - TOTAL[T_BANK])))
                    for t in range(2):
                        for j in range(2):
                            if first:
                                drained(pe, l, ("y", t, j), before=True)
                            for c in range(2):
                                last = pe.matmul(psum[:, 2 * t + j, :], hbT[:, c, rows(t)], weights[:, c, 512 * j:512 * j + 512],
                                                 start=first and c == 0, stop=last_one and c == 1)
                            if last_one:
                                last.then_inc(bank_filled[2 * t + j], 1)
                    if not last_one:
                        last.then_inc(sems["expert_down_done"], 1)
                    else:
                        pe.drain().then_inc(sems["expert_down_done"], 1)

                def down_of(s, half):
                    return ring[:, s, 2048 * half:2048 * half + 2048].rearrange("p (c n) -> p c n", c=2)

                loaded(pe, l, "shgu")
                for t in range(2):
                    gate_up(POS["shgu"] % SLOTS, t, 0, 0)

                def landed(s, i):
                    a, b = TRUNK_DMAS[s], EXPERT_DMAS[s]
                    pe.wait_ge(slot_loaded[s], l * (16 * SLOT_DMAS[s]) + (i * (16 * b) + 16 * (a + b - SLOT_DMAS[s])))

                def four(i, previous_down, first):
                    for k in range(1, 5):
                        s = 3 * ((k - 1) // 2) + (k - 1) % 2
                        landed(s, i)
                        gate_up(s, 0, i, k)
                        turn(i, k - 1)
                        gate_up(s, 1, i, k)
                        if k == 1:
                            down(previous_down, i, 0, first=first)
                        else:
                            half = (k - 2) % 2
                            ds_ = 2 + 3 * ((k - 2) // 2)
                            if half == 0:
                                landed(ds_, i)
                            down(down_of(ds_, half), i, k - 1)

                four(0, down_of(POS["rt"] % SLOTS, 0), True)
                with pe.Fori(1, ROUNDS) as i:
                    four(i, down_of(5, 1), False)
                turn(ROUNDS - 1, 4)
                down(down_of(5, 1), ROUNDS - 1, 4, last_one=True)

        @block.scalar
        def _(act):
            chain = [0]

            def link(ins):
                chain[0] += 1
                ins.then_inc(act_chain, 1)
                act.wait_ge(act_chain, chain[0])

            with act.Fori(1, DEPTH + 1) as l:
                chain[0] = 0

                def move(key, dst, src, func=ACT.Copy, scale=1.0):
                    filled(act, l, key)
                    act.activation(dst, src, func, scale=scale).then_inc(bank_drained[BANK[key]], 1)

                def four_blocks(key):
                    return bank(key).rearrange("p (c n) -> p c n", c=4)

                for t in range(2):
                    move(("hT", t, 0), hT[:, 0:4, t * P:t * P + P], four_blocks(("hT", t, 0)))
                move(("gfr",), gfrT[:], psum[0:GR, BANK["gfr",], 0:S])
                signal(act, l, "abs_ready", 1)
                link(act.activation(tmp_e, tmp_e, ACT.Exp, scale=-1.0))
                act.activation(tmp_e, tmp_e, ACT.Ln, bias=1.0).then_inc(sems["log_ready"], 1)
                signal(act, l, "cum_ready", 1)
                act.activation(qd, b_cum, ACT.Exp, scale=1.0 / GATE_TAU).then_inc(sems["exp_ready"], 1)
                act.activation(ki, b_cum, ACT.Exp, scale=-1.0 / GATE_TAU).then_inc(sems["exp_ready"], 1)
                signal(act, l, "cum_ready", 2)
                act.activation(keT, tmp_e, ACT.Exp, scale=1.0 / GATE_TAU).then_inc(sems["exp_ready"], 1)
                for j in range(2):
                    for t in range(2):
                        move(("v", j, t), gv[:, t, 512 * j:512 * j + 512], bank(("v", j, t)))
                for j in range(2):
                    for t in range(2):
                        move(("gr", j, t), gr[:, t, 512 * j:512 * j + 512], bank(("gr", j, t)), ACT.Silu)
                for t in range(2):
                    move(("ke", t), ke[:, t, :], bank(("ke", t)))
                move(("sgwT",), sgwT[:], four_blocks(("sgwT",)))
                for n in range(GH):
                    key = ("o", n)
                    filled(act, l, key)
                    for t in range(2):
                        ins = act.activation(junk[:, t, 0:GDV], bank(key)[:, t * GDV:(t + 1) * GDV], ACT.Square,
                                             accum_out=ssq[:, 2 * n + t:2 * n + t + 1])
                        if t == 0:
                            link(ins)
                    link(ins)
                    act.activation(rstd[:, 2 * n:2 * n + 2], ssq[:, 2 * n:2 * n + 2], ACT.Copy, scale=1.0 / GDV,
                                   bias=RMS_EPS).then_inc(sems["ms_ready"], 1)
                for z in range(4):
                    for t in range(2):
                        half = u if z < 2 else vv
                        move(("sg", z, t), half[:, t, 512 * (z % 2):512 * (z % 2) + 512], bank(("sg", z, t)), ACT.Gelu)
                for t in range(2):
                    filled(act, l, ("mq", t))
                    filled(act, l, ("mkv", t))
                    link(act.activation(junk[:, t, 0:QR], bank(("mq", t))[:, 0:QR], ACT.Square,
                                        accum_out=ssq[:, 8 + 2 * t:9 + 2 * t]))
                    link(act.activation(junk[:, t, 0:KVR], bank(("mkv", t))[:, 0:KVR], ACT.Square,
                                        accum_out=ssq[:, 9 + 2 * t:10 + 2 * t]))
                    link(act.activation(rstd[:, 8 + 2 * t:9 + 2 * t], ssq[:, 8 + 2 * t:9 + 2 * t], ACT.Copy,
                                        scale=1.0 / QR, bias=RMS_EPS))
                    act.activation(rstd[:, 9 + 2 * t:10 + 2 * t], ssq[:, 9 + 2 * t:10 + 2 * t], ACT.Copy,
                                   scale=1.0 / KVR, bias=RMS_EPS).then_inc(sems["ms_ready"], 1)

                def gates(kind, pair):
                    for j in range(2):
                        for t in range(2):
                            key = kind(j, t)
                            filled(act, l, key)
                            if (j, t) != (0, 0):
                                before = pair(*[(0, 0), (0, 1), (1, 0)][2 * j + t - 1])
                                drained(act, l, before)
                            act.activation(gsig[:, t, :], bank(key), ACT.Sigmoid).then_inc(bank_drained[BANK[key]], 1)

                gates(lambda j, t: ("gate", 0, j, t), lambda j, t: ("proj", 0, j, t))
                for t in range(2):
                    for f in range(2):
                        move(("obT", t, f), bT[:, 4 * f:4 * f + 4, t * P:t * P + P], four_blocks(("obT", t, f)))
                gates(lambda j, t: ("gate", 1, j, t), lambda j, t: ("proj", 1, j, t))
                for kind, dst in (("qn", qnope), ("kn", knope)):
                    for i in range(4):
                        move((kind, i), dst[:, 2 * i:2 * i + 2, :], bank((kind, i)).rearrange("p (c n) -> p c n", c=2))
                for t in range(2):
                    for j in range(2):
                        move(("vm", t, j), vm[:, t, 512 * j:512 * j + 512], bank(("vm", t, j)))
                for t in range(2):
                    move(("qrT", t), qrT[:, :, t * P:t * P + P], four_blocks(("qrT", t)))
                for n in range(MH + 1):
                    if n < MH:
                        signal(act, l, "max_ready", n + 1)
                        if n >= 2:
                            filled(act, l, ("pT", n - 2))
                        for r, (part, a, k) in enumerate(regions):
                            ins = act.activation(prob[part, n % 2, a:a + k], bank(("s", n))[part, a:a + k], ACT.Exp,
                                                 bias=sm_max[part, n % 2, a // P:a // P + 1], scale=QK ** -0.5,
                                                 accum_out=sm_sum[part, n % 2, a // P:a // P + 1])
                            if r < 3:
                                link(ins)
                        ins.then_inc(sems["exp_p"], 1)
                    if n:
                        move(("pT", n - 1), pT[:, (n - 1) % 2, :], bank(("pT", n - 1))[:, 0:384])
                gates(lambda j, t: ("gate", 2, j, t), lambda j, t: ("proj", 2, j, t))
                for t in range(2):
                    move(("mT", t, 0), bT[:, 0:4, t * P:t * P + P], four_blocks(("mT", t, 0)))
                for t in range(2):
                    move(("hT2", t, 0), hT[:, 0:4, t * P:t * P + P], four_blocks(("hT2", t, 0)))
                for t in range(2):
                    move(("rt", t), score[:, t, :], bank(("rt", t))[:, 0:NE], ACT.Sigmoid)
                move(("ppT",), pleT, bank(("ppT",)).rearrange("p (c n) -> p c n", c=2))
                gates(lambda j, t: ("plg", j, t), lambda j, t: ("pli", j, t))

                def silu(i, k):
                    for t in range(2):
                        b = GU_BANK + t
                        act.wait_ge(bank_filled[b], l * TOTAL[b] + (4 * i + (EXPERT_BASE[b] + k + 1)))
                        act.activation(sgate[:, t, :], psum[:, b, 0:DE], ACT.Silu).then_inc(sems["silu_ready"], 1)

                silu(0, 0)
                with act.Fori(0, ROUNDS) as i:
                    for k in range(1, 5):
                        silu(i, k)
                act.wait_ge(act_chain, chain[0])
                act.sem_clear(act_chain)

        @block.vector
        def _(dve):
            chain = [0]

            def link(ins):
                chain[0] += 1
                ins.then_inc(dve_chain, 1)
                dve.wait_ge(dve_chain, chain[0])

            def end_chain():
                dve.sem_clear(dve_chain)
                chain[0] = 0

            def normalise(x, g, b, announce_var, wait_rstd, column, announce):
                for t in range(2):
                    for i in range(2):
                        link(dve.bn_stats(stats[:, t, i, :], x[:, t, 512 * i:512 * i + 512]))
                    link(dve.bn_aggr(mv[:, t, :], stats[:, t, :, :].rearrange("p a b -> p (a b)")))
                announce_var(dve.tensor_scalar(rstd[:, column:column + 2], mv[:, :, 1], LN_EPS, None, ALU.add))
                wait_rstd()
                for t in range(2):
                    link(dve.tensor_scalar(x[:, t, :], x[:, t, :], mv[:, t, 0:1], rstd[:, column + t:column + t + 1],
                                           ALU.subtract, ALU.mult))
                link(dve.tensor_tensor(x, x, g[:].unsqueeze(1).to_broadcast([P, 2, D]), ALU.mult))
                announce(dve.tensor_tensor(x, x, b[:].unsqueeze(1).to_broadcast([P, 2, D]), ALU.add))

            dve.wait_ge(x_loaded, 48)
            normalise(h[:], ln_g, ln_b, lambda ins: ins.then_inc(var_in_ready, 1),
                      lambda: dve.wait_ge(rstd_in_ready, 1), 0, lambda ins: ins.then_inc(sems["h_ready"], 1))
            dve.wait_ge(setup_done, 1)
            dve.wait_ge(tables_loaded, 32)
            end_chain()

            with dve.Fori(1, DEPTH + 1) as l:

                def done(ins, key):
                    ins.then_inc(bank_drained[BANK[key]], 1)

                def four_blocks(key):
                    return bank(key).rearrange("p (c n) -> p c n", c=4)

                for t in range(2):
                    filled(dve, l, ("hT", t, 1))
                    done(dve.tensor_copy(hT[:, 4:8, t * P:t * P + P], four_blocks(("hT", t, 1))), ("hT", t, 1))
                link(dve.memset(att, 0.0))
                dve.wait_ge(sems["params_loaded"], l * (16 * PARAMS))
                for i in range(2):
                    filled(dve, l, ("fg", i))
                    for n in range(2):
                        ins = dve.tensor_scalar(b_cum[:, 2 * i + n, :], bank(("fg", i))[:, n * S:n * S + S],
                                                fgb[:, 2 * i + n:2 * i + n + 1], None, ALU.add)
                        if n == 0:
                            link(ins)
                    done(ins, ("fg", i))
                    drained(dve, l, ("fg", i))
                dve.scalar_tensor_tensor(tmp_e, b_cum, -1.0, b_cum, ALU.mult, ALU.max).then_inc(sems["abs_ready"], 1)
                signal(dve, l, "log_ready", 1)
                link(dve.scalar_tensor_tensor(keT, b_cum, 0.0, tmp_e, ALU.min, ALU.subtract))
                for n in range(GH):
                    ins = dve.tensor_tensor_scan(b_cum[:, n, :], restart[:], keT[:, n, :], 0.0, ALU.mult, ALU.add)
                    if n < GH - 1:
                        link(ins)
                ins.then_inc(sems["cum_ready"], 1)
                signal(dve, l, "cum_ready", 1)
                chunks = lambda x: x.rearrange("p h (c t) -> p (h c) t", t=CHUNK)
                ends = chunks(b_cum)[:, :, CHUNK - 1:CHUNK].to_broadcast([P, GH * S // CHUNK, CHUNK])
                dve.tensor_tensor(chunks(tmp_e), ends, chunks(b_cum), ALU.subtract).then_inc(sems["cum_ready"], 1)
                signal(dve, l, "exp_ready", 1)
                link(dve.tensor_copy(decay[:].rearrange("p h c -> p (h c)"), chunks(qd)[:, :, CHUNK - 1]))
                two = lambda key: bank(key).rearrange("p (c n) -> p c n", c=2)
                for i in range(2):
                    filled(dve, l, ("q", i))
                    done(dve.scalar_tensor_tensor(qd[:, 2 * i:2 * i + 2, :], two(("q", i)), GDK ** -0.5,
                                                  qd[:, 2 * i:2 * i + 2, :], ALU.mult, ALU.mult), ("q", i))
                signal(dve, l, "exp_ready", 3)
                for i in range(2):
                    filled(dve, l, ("k", i))
                    link(dve.tensor_tensor(ki[:, 2 * i:2 * i + 2, :], two(("k", i)), ki[:, 2 * i:2 * i + 2, :], ALU.mult))
                    done(dve.tensor_tensor(keT[:, 2 * i:2 * i + 2, :], two(("k", i)), keT[:, 2 * i:2 * i + 2, :],
                                           ALU.mult), ("k", i))
                    drained(dve, l, ("k", i))
                dve.nop().then_inc(sems["ke_ready"], 1)
                for n in range(GH + 1):
                    if n < GH:
                        filled(dve, l, ("att", n))
                        settle(dve)
                        done(dve.copy_predicated(att[:, n % 2, :], gla_mask[:].rearrange("p t s -> p (t s)"),
                                                 bank(("att", n))[:, 0:S]), ("att", n))
                        filled(dve, l, ("ds", n, 1))
                        if n:
                            filled(dve, l, ("o", n - 1))
                        ds = bank(("ds", n, 0))
                        link(dve.tensor_copy(state[:, 0, :], ds[:, 0:GDV]))
                        done(dve.scalar_tensor_tensor(state[:, 1, :], state[:, 0, :], decay[:, n, 1:2],
                                                      bank(("ds", n, 1))[:, 0:GDV], ALU.mult, ALU.add), ("ds", n, 1))
                        drained(dve, l, ("ds", n, 1))
                        done(dve.scalar_tensor_tensor(state[:, 2, :], state[:, 1, :], decay[:, n, 2:3],
                                                      ds[:, GDV:2 * GDV], ALU.mult, ALU.add), ("ds", n, 0))
                    if n:
                        m = n - 1
                        if n == 1:
                            for j in range(2):
                                for t in range(2):
                                    drained(dve, l, ("gr", j, t))
                        signal(dve, l, "rms_ready", m + 1)
                        for t in range(2):
                            g = gr[:, t, m * GDV:(m + 1) * GDV]
                            ins = dve.scalar_tensor_tensor(g, bank(("o", m))[:, t * GDV:(t + 1) * GDV],
                                                           rstd[:, 2 * m + t:2 * m + t + 1], g, ALU.mult, ALU.mult)
                        done(ins, ("o", m))
                for t in range(2):
                    signal(dve, l, "rms_ready", GH + t + 1)
                    done(dve.tensor_scalar(mq[:, t, :], bank(("mq", t))[:, 0:QR], rstd[:, 8 + 2 * t:9 + 2 * t], None,
                                           ALU.mult), ("mq", t))
                    link(dve.tensor_scalar(mkv[:, t, 0:KVR], bank(("mkv", t))[:, 0:KVR], rstd[:, 9 + 2 * t:10 + 2 * t],
                                           None, ALU.mult))
                    done(dve.tensor_copy(mkv[:, t, KVR:KVR + ROPE], bank(("mkv", t))[:, KVR:KVR + ROPE]), ("mkv", t))
                    drained(dve, l, ("mkv", t))
                for z in (2, 3):
                    for t in range(2):
                        drained(dve, l, ("sg", z, t))
                normalise(vv, sgn_g, sgn_b, lambda ins: ins.then_inc(sems["var_ready"], 1),
                          lambda: signal(dve, l, "rstd_ready", 1), 12, lambda ins: ins.then_inc(sems["vln_ready"], 1))
                k1, k2 = mkv[:, :, KVR:KVR + HALF], mkv[:, :, KVR + HALF:KVR + ROPE]
                kt = [rtmp[:, i, 0:2 * HALF].rearrange("p (t n) -> p t n", t=2) for i in range(4)]
                for i, (a, b) in enumerate(((k1, cos_t), (k2, sin_t), (k1, sin_t), (k2, cos_t))):
                    link(dve.tensor_tensor(kt[i], a, b[:], ALU.mult))
                for n in range(2):
                    link(dve.tensor_tensor(krot[:, :, ROPE * n:ROPE * n + HALF], kt[0], kt[1], ALU.subtract))
                    ins = dve.tensor_tensor(krot[:, :, ROPE * n + HALF:ROPE * n + ROPE], kt[2], kt[3], ALU.add)
                    if n == 0:
                        link(ins)
                ins.then_inc(sems["krot_ready"], 1)
                for t in range(2):
                    for f in range(2):
                        key = ("oaT", t, f)
                        filled(dve, l, key)
                        gain = glag[:, 4 * f:4 * f + 4].unsqueeze(2).to_broadcast([P, 4, P])
                        done(dve.tensor_tensor(bT[:, 4 * f:4 * f + 4, t * P:t * P + P], four_blocks(key), gain,
                                               ALU.mult), key)

                def merge(n):
                    for j in range(2):
                        for t in range(2):
                            filled(dve, l, ("proj", n, j, t))
                            drained(dve, l, ("gate", n, j, t))
                            m = mixed[:, t, 512 * j:512 * j + 512]
                            if n == 0:
                                done(dve.tensor_tensor(m, bank(("proj", n, j, t)), gsig[:, t, :], ALU.mult),
                                     ("proj", n, j, t))
                            else:
                                if (j, t) == (0, 0):
                                    drained(dve, l, ("proj", n - 1, 1, 1))
                                link(dve.tensor_tensor(gsig[:, t, :], bank(("proj", n, j, t)), gsig[:, t, :], ALU.mult))
                                done(dve.tensor_tensor(m, m, gsig[:, t, :], ALU.add), ("proj", n, j, t))

                merge(0)
                for t in range(2):
                    key = ("qnT", t)
                    filled(dve, l, key)
                    done(dve.tensor_tensor(qnT[:, :, t * P:t * P + P],
                                           bank(key)[:, 0:QR].rearrange("p (c n) -> p c n", c=3),
                                           qng[:].unsqueeze(2).to_broadcast([P, 3, P]), ALU.mult), key)
                for t in range(2):
                    key = ("ckT", t)
                    filled(dve, l, key)
                    done(dve.tensor_tensor(ckT[:, :, t * P:t * P + P],
                                           bank(key)[:, 0:KVR].rearrange("p (c n) -> p c n", c=2),
                                           kvng[:].unsqueeze(2).to_broadcast([P, 2, P]), ALU.mult), key)
                filled(dve, l, ("krT",))
                done(dve.tensor_copy(krT, bank(("krT",))[:, 0:S]), ("krT",))
                for z in (0, 1):
                    for t in range(2):
                        drained(dve, l, ("sg", z, t))
                for t in range(2):
                    for i in range(2):
                        filled(dve, l, ("sv", t, i))
                        for n in range(2):
                            g = 2 * i + n
                            part = u[:, t, g * 256:g * 256 + 256]
                            ins = dve.scalar_tensor_tensor(part, bank(("sv", t, i))[:, n * 256:n * 256 + 256],
                                                           sgb[:, g:g + 1], part, ALU.add, ALU.mult)
                        done(ins, ("sv", t, i))
                merge(1)
                pair = lambda x: x.rearrange("p (h n) -> p h n", h=MH)
                for t in range(2):
                    key = ("qr", t)
                    filled(dve, l, key)
                    q1, q2 = pair(bank(key))[:, :, 0:HALF], pair(bank(key))[:, :, HALF:ROPE]
                    cs, sn = (x[:, t, :].unsqueeze(1).to_broadcast([P, MH, HALF]) for x in (cos_t, sin_t))
                    qt = [rtmp[:, i, :].rearrange("p (h n) -> p h n", h=MH) for i in range(4)]
                    for i, (a, b) in enumerate(((q1, cs), (q2, sn), (q1, sn), (q2, cs))):
                        link(dve.tensor_tensor(qt[i], a, b, ALU.mult))
                    dve.nop().then_inc(bank_drained[BANK[key]], 1)
                    link(dve.tensor_tensor(pair(qrot[:, t, :])[:, :, 0:HALF], qt[0], qt[1], ALU.subtract))
                    link(dve.tensor_tensor(pair(qrot[:, t, :])[:, :, HALF:ROPE], qt[2], qt[3], ALU.add))
                    dve.nop().then_inc(sems["qrot_ready"], 1)
                for n in range(2):
                    link(dve.memset(prob[0:CHUNK, n, P - CHUNK:P], 0.0))
                    link(dve.memset(prob[0:CHUNK, n, 3 * P - CHUNK:3 * P], 0.0))
                for n in range(MH + 2):
                    if n < MH:
                        filled(dve, l, ("s", n))
                        if n >= 2:
                            signal(dve, l, "exp_p", n - 1)
                        for part, a, k in regions:
                            link(dve.reduce_max(sm_top[part, n % 2, a // P:a // P + 1], bank(("s", n))[part, a:a + k],
                                                axis=mybir.AxisListType.X))
                        dve.tensor_scalar(sm_max[:, n % 2, :], sm_top[:, n % 2, :], -(QK ** -0.5), None,
                                          ALU.mult).then_inc(sems["max_ready"], 1)
                        signal(dve, l, "exp_p", n + 1)
                        link(dve.reciprocal(sm_inv[:, n % 2, :], sm_sum[:, n % 2, :]))
                        dve.nop().then_inc(bank_drained[BANK["s", n]], 1)
                        link(dve.tensor_scalar(prob[:, n % 2, 0:P], prob[:, n % 2, 0:P], sm_inv[:, n % 2, 0:1], None,
                                               ALU.mult))
                        dve.tensor_scalar(prob[:, n % 2, P:3 * P], prob[:, n % 2, P:3 * P], sm_inv[:, n % 2, 1:2], None,
                                          ALU.mult).then_inc(sems["prob_ready"], 1)
                    if n >= 2:
                        filled(dve, l, ("oc", n - 2))
                        done(dve.tensor_copy(bT[:, n - 2, :], bank(("oc", n - 2))[:, 0:S]), ("oc", n - 2))
                merge(2)
                for t in range(2):
                    key = ("mT", t, 1)
                    filled(dve, l, key)
                    done(dve.tensor_copy(bT[:, 4:8, t * P:t * P + P], four_blocks(key)), key)
                for j in range(2):
                    for t in range(2):
                        key, part = ("wo", j, t), h[:, t, 512 * j:512 * j + 512]
                        filled(dve, l, key)
                        done(dve.scalar_tensor_tensor(part, part, ALPHA, bank(key), ALU.mult, ALU.add), key)
                for j in range(2):
                    for t in range(2):
                        drained(dve, l, ("wo", j, t))
                normalise(h[:], ln_g, ln_b, lambda ins: ins.then_inc(sems["var_ready"], 1),
                          lambda: signal(dve, l, "rstd_ready", 2), 12, lambda ins: ins.then_inc(sems["ln1_done"], 1))
                for t in range(2):
                    key = ("hT2", t, 1)
                    filled(dve, l, key)
                    done(dve.tensor_copy(hT[:, 4:8, t * P:t * P + P], four_blocks(key)), key)
                end_chain()
                signal(dve, l, "ln1_done", 1)
                for t in range(2):
                    drained(dve, l, ("rt", t))
                    link(dve.tensor_tensor(biased[:, t, :], score[:, t, :], rbias[:], ALU.add))
                    for g in range(NG):
                        ins = dve.max(grp8[:, g, :], biased[:, t, 8 * g:8 * g + 8])
                    link(ins)
                    link(dve.tensor_tensor(gsum, grp8[:, :, 0], grp8[:, :, 1], ALU.add))
                    mine = gsum.unsqueeze(2).to_broadcast([P, NG, NG])
                    other = gsum.unsqueeze(1).to_broadcast([P, NG, NG])
                    link(dve.tensor_tensor(cmp, other, mine, ALU.is_equal))
                    link(dve.tensor_tensor(cmp2, cmp, earlier[:], ALU.mult))
                    link(dve.tensor_tensor(cmp, other, mine, ALU.is_gt))
                    link(dve.tensor_tensor(cmp, cmp, cmp2, ALU.add))
                    link(dve.reduce_sum(gkeep, cmp, axis=mybir.AxisListType.X))
                    link(dve.tensor_scalar(gkeep, gkeep, TOPG - 0.5, None, ALU.is_lt))
                    keep8 = gkeep.unsqueeze(2).to_broadcast([P, NG, 8])
                    by_group = lambda x: x.rearrange("p (g n) -> p g n", g=NG)
                    link(dve.tensor_tensor(by_group(biased[:, t, :]), by_group(biased[:, t, :]), keep8, ALU.mult))
                    link(dve.tensor_scalar(gkeep, gkeep, 1.0, -LOW_FILL, ALU.subtract, ALU.mult))
                    link(dve.tensor_tensor(by_group(biased[:, t, :]), by_group(biased[:, t, :]), keep8, ALU.add))
                    link(dve.max(top8, biased[:, t, :]))
                    link(dve.match_replace(rep, top8, biased[:, t, :], TAKEN))
                    link(dve.tensor_tensor(rep, rep, biased[:, t, :], ALU.not_equal))
                    link(dve.tensor_tensor(wts[:, t, :], rep, score[:, t, :], ALU.mult))
                    link(dve.reduce_sum(wsum[:, 0:1], wts[:, t, :], axis=mybir.AxisListType.X))
                    link(dve.reciprocal(wsum[:, 1:2], wsum[:, 0:1]))
                    link(dve.tensor_scalar(wts[:, t, :], wts[:, t, :], wsum[:, 1:2], ROUTED_SCALE, ALU.mult, ALU.mult))
                for j in range(2):
                    for t in range(2):
                        filled(dve, l, ("pli", j, t))
                        drained(dve, l, ("plg", j, t))
                        link(dve.tensor_tensor(mixed[:, t, 512 * j:512 * j + 512], bank(("pli", j, t)), gsig[:, t, :],
                                               ALU.mult))
                        dve.nop().then_inc(bank_drained[BANK["pli", j, t]], 1)
                for t in range(2):
                    link(dve.scalar_tensor_tensor(mixed[:, t, :], h[:, t, :], ALPHA, mixed[:, t, :], ALU.mult, ALU.add))

                def gated(t, i, k, weight):
                    b = GU_BANK + t
                    signal_k = l * names["silu_ready"] + (8 * i + (2 * k + t + 1 - names["silu_ready"]))
                    dve.wait_ge(sems["silu_ready"], signal_k)
                    o = hb[:, k % 2, t * DE:(t + 1) * DE]
                    if weight is None:
                        ins = dve.tensor_tensor(o, psum[:, b, DE:2 * DE], sgate[:, t, :], ALU.mult)
                    else:
                        ins = dve.scalar_tensor_tensor(o, psum[:, b, DE:2 * DE], weight, sgate[:, t, :], ALU.mult, ALU.mult)
                    ins.then_inc(bank_drained[b], 1)

                def take_turned(i, k):
                    dve.wait_ge(bank_filled[T_BANK], l * TOTAL[T_BANK] + (4 * i + (EXPERT_BASE[T_BANK] + k + 1)))
                    dve.tensor_copy(hbT, psum[:, T_BANK, :].rearrange("p (c n) -> p c n", c=2)
                                    ).then_inc(bank_drained[T_BANK], 1)

                for t in range(2):
                    gated(t, 0, 0, None)
                with dve.Fori(0, ROUNDS) as i:
                    for k in range(1, 5):
                        weight = [wts[:, t, bass.ds(4 * i + (k - 1), 1)] for t in range(2)]
                        gated(0, i, k, weight[0])
                        take_turned(i, k - 1)
                        gated(1, i, k, weight[1])
                take_turned(ROUNDS - 1, 4)
                for t in range(2):
                    for j in range(2):
                        key, part = ("y", t, j), slice(512 * j, 512 * j + 512)
                        filled(dve, l, key)
                        done(dve.tensor_tensor(h[:, t, part], bank(key), mixed[:, t, part], ALU.add), key)
                for t in range(2):
                    for j in range(2):
                        drained(dve, l, ("y", t, j))
                signal(dve, l, "ln2_loaded", 32)
                normalise(h[:], ln_g, ln_b, lambda ins: ins.then_inc(sems["var_ready"], 1),
                          lambda: signal(dve, l, "rstd_ready", 3), 12, lambda ins: ins.then_inc(sems["h_ready"], 1))
                end_chain()


NAMES = ["x", "p", "ln_in_g", "ln_in_b", "w_in", "gla_fg_w", "gla_fg_b", "gla_norm_g", "sg_norm_g", "sg_norm_b", "sg_w",
         "sg_b", "mla_qn_g", "mla_w_uq", "mla_kvn_g", "mla_w_ukv", "w_branch", "w_out", "ln1_g", "ln1_b", "router_w",
         "router_b", "exp_w_gate", "exp_w_up", "exp_w_down", "sh_w_gate", "sh_w_up", "sh_w_down", "ple_w_in",
         "ple_w_gate", "ln2_g", "ln2_b"]


def kernel(**inputs):
    import numpy as np
    import concourse.bacc as bacc
    from concourse.bass_utils import run_bass_kernel_spmd

    nc = bacc.Bacc("TRN2", target_bir_lowering=False, num_devices=1)
    arrays, weights = {}, {}

    def given(name, a):
        arrays[f"in_{name}"] = a
        return nc.dram_tensor(f"in_{name}", a.shape, mybir.dt.from_np(a.dtype), kind="ExternalInput").ap()

    for name in NAMES:
        weights[name] = given(name, np.ascontiguousarray(inputs[name]))
    inv = np.float32(10000.0) ** (-np.arange(HALF, dtype=np.float32) / np.float32(HALF))
    angle = np.arange(S, dtype=np.float32)[:, None] * inv
    cos_tab, sin_tab = given("cos", np.cos(angle).astype(np.float32)), given("sin", np.sin(angle).astype(np.float32))
    out = nc.dram_tensor("out_0", (1, S, D), F32, kind="ExternalOutput").ap()
    build_trunk(nc, weights, cos_tab, sin_tab, out)
    r = run_bass_kernel_spmd(nc, [arrays], core_ids=[0])
    return r.results[0]["out_0"]
```

```python
from contextlib import ExitStack

import concourse.bass as bass
from concourse import mybir

F32 = mybir.dt.float32
I32 = mybir.dt.int32
BF16 = mybir.dt.bfloat16
ACT = mybir.ActivationFunctionType
ALU = mybir.AluOpType

P = 128
DEPTH = 2
S = 256
TILES = S // P
D = 1024
DC = D // P
CHUNK = 64
GH, GDK, GDV, GR = 4, 128, 256, 16
GATE_TAU = 16.0
SGW, SGG = 1024, 4
MH, QR, KVR, NOPE, ROPE, MV = 8, 384, 256, 128, 64, 128
QK = NOPE + ROPE
HALF = ROPE // 2
NE, NG, TOPG, TOPK, DE = 64, 8, 4, 8, 256
PLE = 256
ROUTED_SCALE = 2.5
ALPHA = (2 * DEPTH) ** 0.25
COL_GQ = 0
COL_GK = COL_GQ + GH * GDK
COL_GV = COL_GK + GH * GDK
COL_GR = COL_GV + GH * GDV
COL_GF = COL_GR + GH * GDV
COL_SG = COL_GF + GR
COL_MQ = COL_SG + 2 * SGW
COL_MKV = COL_MQ + QR
COL_GATE = COL_MKV + KVR + ROPE
SLOTS = 6
SLOT = 4096
BANKS = 8
SLOTS_E = 64
OVER, SPARE = 256 // SLOTS_E - 1, 256 * 8 // SLOTS_E
LN_EPS, RMS_EPS = 1e-5, 1e-6
PARAMS = 12
LOW_FILL = -3.0e38
TAKEN = 3.0e38

JOBS = (
    [("hT", t, f) for t in range(2) for f in range(2)] + [("gfr",)]
    + [("q", i) for i in range(2)] + [("k", i) for i in range(2)] + [("fg", i) for i in range(2)]
    + [("v", j, t) for j in range(2) for t in range(2)] + [("gr", j, t) for j in range(2) for t in range(2)]
    + [("ke", t) for t in range(2)] + [("sgwT",)]
    + [x for h in range(GH + 1) for x in
       ([("att", h), ("ds", h, 0), ("ds", h, 1)] if h < GH else []) + ([("o", h - 1)] if h else [])]
    + [("sg", z, t) for z in range(4) for t in range(2)]
    + [("mq", t) for t in range(2)] + [("mkv", t) for t in range(2)]
    + [("oaT", t, f) for t in range(2) for f in range(2)]
    + [x for j in range(2) for t in range(2) for x in (("gate", 0, j, t), ("proj", 0, j, t))]
    + [("qnT", t) for t in range(2)] + [("ckT", t) for t in range(2)] + [("krT",)]
    + [("sv", t, i) for t in range(2) for i in range(2)]
    + [("obT", t, f) for t in range(2) for f in range(2)]
    + [x for j in range(2) for t in range(2) for x in (("gate", 1, j, t), ("proj", 1, j, t))]
    + [("qn", i) for i in range(4)] + [("qr", t) for t in range(2)]
    + [("kn", i) for i in range(4)] + [("vm", t, j) for t in range(2) for j in range(2)]
    + [("qrT", t) for t in range(2)]
    + [x for h in range(MH + 2) for x in
       ([("s", h)] if h < MH else []) + ([("pT", h - 1)] if 1 <= h <= MH else []) + ([("oc", h - 2)] if h >= 2 else [])]
    + [x for j in range(2) for t in range(2) for x in (("gate", 2, j, t), ("proj", 2, j, t))]
    + [("mT", t, f) for t in range(2) for f in range(2)]
    + [("wo", j, t) for j in range(2) for t in range(2)]
    + [("hT2", t, f) for t in range(2) for f in range(2)]
    + [("rt", t) for t in range(2)] + [("ppT",)]
    + [x for j in range(2) for x in [y for t in range(2) for y in (("pli", j, t), ("plg", j, t))]
       + ([("rank", 0), ("rank", 1)] if j == 0 else [])]
    + [("shgu", 0), ("shgu", 1), ("shT",)]
)
BANK, NTH, TOTAL = {}, {}, [0] * BANKS
for n_, key_ in enumerate(JOBS):
    BANK[key_] = n_ % BANKS
    TOTAL[n_ % BANKS] += 1
    NTH[key_] = TOTAL[n_ % BANKS]
PAIRS = NE // 2
STEP = {"gate_up0": (4, 3, -2), "gate_up1": (4, 3, -1), "down0": (4, 3, 0),
        "gather0": (5, 3, -3), "gather1": (5, 3, -1), "down1": (5, 3, 1),
        "hidden0": (6, 2, -1), "hidden1": (6, 2, 0),
        "rows0": (7, 3, -2), "rows1": (7, 3, -1), "places": (7, 3, 0)}
EXPERT_BASE = {b: TOTAL[b] for b in range(4, 8)}
for b_, jobs_, _ in {x[:2] + (0,) for x in STEP.values()}:
    TOTAL[b_] += jobs_ * PAIRS
for t_ in range(2):
    for j_ in range(2):
        b_ = 2 * t_ + j_
        TOTAL[b_] += 1
        BANK["y", t_, j_], NTH["y", t_, j_] = b_, TOTAL[b_]

LOADS = [
    ("gf", ("gfr",)), ("gq", ("q", 1)), ("gk", ("k", 1)), ("gv0", ("v", 0, 1)), ("gv1", ("v", 1, 1)),
    ("gr0", ("gr", 0, 1)), ("gr1", ("gr", 1, 1)), ("sg0", ("sg", 0, 1)), ("sg1", ("sg", 1, 1)),
    ("sg2", ("sg", 2, 1)), ("sg3", ("sg", 3, 1)), ("mq", ("mq", 1)), ("mkv", ("mkv", 1)),
]
for n_ in range(3):
    if n_ == 2:
        LOADS += [("uq0", ("qr", 1)), ("uq1", ("qr", 1)), ("uq2", ("qr", 1)), ("ukv", ("vm", 1, 1))]
    for j_ in range(2):
        LOADS += [(f"g{n_}{j_}", ("gate", n_, j_, 1)), (f"b{n_}{j_}", ("proj", n_, j_, 1))]
LOADS += [("wo0", ("wo", 0, 1)), ("wo1", ("wo", 1, 1)), ("shgu", ("shgu", 1)), ("rt", "shared_down"),
          ("pli", ("pli", 1, 1)), ("plg0", ("plg", 0, 1)), ("plg1", ("plg", 1, 1))]
LOADS = [x for x in LOADS if x[0] != "gf"]
LOADS = [("gf", ("gfr",))] + LOADS
assert len(LOADS) == 36, len(LOADS)
assert len(LOADS) % SLOTS == 0
POS = {name: n for n, (name, _) in enumerate(LOADS)}
DMAS = {"shgu": 2, "rt": 2}
LANDED, SLOT_DMAS = {}, [0] * SLOTS
for n_, (name_, _) in enumerate(LOADS):
    SLOT_DMAS[n_ % SLOTS] += DMAS.get(name_, 1)
    LANDED[name_] = SLOT_DMAS[n_ % SLOTS]
TRUNK_DMAS = list(SLOT_DMAS)
ROUNDS = NE // 4
EXPERT_DMAS = [2, 2, 1, 2, 2, 1]
SLOT_DMAS = [a + ROUNDS * b for a, b in zip(TRUNK_DMAS, EXPERT_DMAS)]


def build_trunk(nc, w, cos_tab, sin_tab, out):
    with ExitStack() as ctx:
        sb = lambda name, shape, dt=F32: ctx.enter_context(nc.sbuf_tensor(name, shape, dt))
        sem = lambda name: ctx.enter_context(nc.semaphore(name))

        ring = sb("ring", [P, SLOTS, SLOT])
        h = sb("h", [P, TILES, D])
        hT = sb("hT", [P, DC, S])
        bT = sb("bT", [P, DC, S])
        mixed = sb("mixed", [P, TILES, D])
        arena = sb("arena", [P, 11520])
        ident = sb("ident", [P, P])
        gla_mask = sb("gla_mask", [P, TILES, P], I32)
        restart = sb("restart", [P, S])
        cos_t = sb("cos_t", [P, TILES, HALF])
        sin_t = sb("sin_t", [P, TILES, HALF])
        ln_g = sb("ln_g", [P, D])
        ln_b = sb("ln_b", [P, D])
        sgn_g = sb("sgn_g", [P, SGW])
        sgn_b = sb("sgn_b", [P, SGW])
        sgw = sb("sgw", [P, SGG, P])
        sgwT = sb("sgwT", [P, SGG, P])
        sgb = sb("sgb", [P, SGG])
        gsig = sb("gsig", [P, 2, 512])
        junk = gsig
        gfrT = sb("gfrT", [GR, S])
        fgw = sb("fgw", [GR, GH * GDK])
        fgb = sb("fgb", [P, GH])
        glag = sb("glag", [P, DC])
        qng = sb("qng", [P, QR // P])
        kvng = sb("kvng", [P, KVR // P])
        rbias = sb("rbias", [P, NE])
        ssq = sb("ssq", [P, 16])
        rstd = sb("rstd", [P, 16])
        neg_half = sb("neg_half", [P, 8])
        stats = sb("stats", [P, TILES, 2, 6])
        mv = sb("mv", [P, TILES, 2])
        decay = sb("decay", [P, GH, S // CHUNK])
        earlier = sb("earlier", [P, NG, NG])
        sm_top = sb("sm_top", [P, 2, 2])
        sm_max = sb("sm_max", [P, 2, 2])
        sm_sum = sb("sm_sum", [P, 2, 2])
        sm_inv = sb("sm_inv", [P, 2, 2])

        def carve(start, *shape):
            size = 1
            for x in shape:
                size *= x
            view = arena[:, start:start + size]
            if len(shape) == 2:
                view = view.rearrange("p (a b) -> p a b", a=shape[0])
            if len(shape) == 3:
                view = view.rearrange("p (a b c) -> p a b c", a=shape[0], b=shape[1])
            return view

        qd, ki, b_cum, tmp_e, keT = (carve(i * 1024, GH, S) for i in range(5))
        ke = carve(5 * 1024, TILES, GH * GDK)
        gv = carve(6144, TILES, GH * GDV)
        gr = carve(8192, TILES, GH * GDV)
        att = carve(10240, 2, TILES * P)
        state = carve(10752, 3, GDV)
        u = carve(0, TILES, SGW)
        vv = carve(2048, TILES, SGW)
        mq = carve(4096, TILES, QR)
        mkv = carve(4864, TILES, KVR + ROPE)
        qnT = carve(5504, QR // P, S)
        ckT = carve(6272, KVR // P, S)
        rtmp = carve(6784, 4, MH * HALF)
        krot = carve(7808, TILES, P)
        qnope = carve(8192, MH, S)
        qrT = carve(10240, 4, S)
        krT = carve(11264, S)
        knope = carve(0, MH, S)
        vm = carve(2048, TILES, MH * MV)
        prob = carve(6784, 2, 384)
        pT = carve(5120, 2, 384)
        qrot = carve(4096, 2, 512)
        regions = [(slice(CHUNK * i, CHUNK * i + CHUNK), P * t, P * t + CHUNK * (i + 1)) for t in range(2) for i in range(2)]
        pleT = carve(0, PLE // P, S)
        hb = carve(0, P)
        hbT = carve(256, 2, 2, SLOTS_E)
        ptok = carve(512, TILES, PLE)
        sgate = carve(1024, TILES, DE)
        sh_hb = carve(1536, TILES * DE)
        sh_hbT = carve(2560, 2, S)
        ybuf = carve(1024, 2, 512)
        score = carve(3072, TILES, NE)
        biased = carve(3200, TILES, NE)
        wts = carve(3328, TILES, NE)
        grp8 = carve(3456, NG, 8)
        gsum = carve(3520, NG)
        cmp = carve(3584, NG, NG)
        cmp2 = carve(3648, NG, NG)
        top8 = carve(3712, 8)
        rep = carve(3776, NE)
        wsum = carve(3840, 2)
        gkeep = carve(3856, NG)
        sel = carve(3904, TILES, NE)
        pos = sb("pos", [P, TILES, NE])
        iota = sb("iota", [P, 2 * SLOTS_E])
        before = sb("before", [P, P])
        ones = sb("ones", [P, P])
        spare_code = sb("spare_code", [P, OVER, NE])
        spare_key = carve(7168, OVER * NE)
        spare_top = sb("spare_top", [P, SPARE])
        spare_unit = sb("spare_unit", [P, SPARE], I32)
        spare_expert = sb("spare_expert", [P, SPARE], I32)
        spare_rank = sb("spare_rank", [P, SPARE])
        spare_pos = sb("spare_pos", [P, TILES])
        spare_sum = sb("spare_sum", [P, 1])
        spare_count = sb("spare_count", [P, 1], I32)
        parts = arena[:, 4096:7168].bitcast(BF16).rearrange("p (s t a i c) -> p s t a i c", s=3, t=2, a=2, i=4)
        rest = carve(7168, TILES, D)
        xg = carve(9216, 512)
        xgT = carve(9728, 4, 2 * SLOTS_E)
        placesT = carve(10240, S)
        places_w = carve(10496, TILES, 2 * SLOTS_E)
        places = arena[:, 11264:11392].bitcast(BF16).rearrange("p (b t s) -> p b t s", b=2, t=2)
        sgate_e = carve(11392, P)

        psum = ctx.enter_context(nc.psum_tensor("psum", [P, BANKS, 512], F32))

        bank_filled = [sem(f"bank_filled{b}") for b in range(BANKS)]
        bank_drained = [sem(f"bank_drained{b}") for b in range(BANKS)]
        slot_loaded = [sem(f"slot_loaded{s}") for s in range(SLOTS)]
        names = dict(params_loaded=16 * PARAMS, ln2_loaded=32, p_loaded=16, h_ready=1, ln1_done=1, var_ready=3,
                     rstd_ready=3, ms_ready=GH + 2, rms_ready=GH + 2, sgw_masked=1, abs_ready=1, log_ready=1,
                     cum_ready=2, exp_ready=3, ke_ready=1, vln_ready=1, krot_ready=1, qrot_ready=2,
                     max_ready=MH, exp_p=MH, prob_ready=MH, silu_ready=NE, shared_silu=2, shared_down_done=1,
                     split_ready=1, places_ready=3 * PAIRS, score_taken=1, spare_ready=1)
        sems = {k: sem(k) for k in names}
        spare_loaded, spare_used, pe_to_dve, pe_to_act, act_to_pe, act_to_dve, dve_to_pe = (
            sem(f"spare_{k}") for k in ("loaded", "used", "pe_to_dve", "pe_to_act", "act_to_pe", "act_to_dve",
                                        "dve_to_pe"))
        dve_step = sem("dve_step")
        settled = {k: sem(f"settled_{k}") for k in ("SP", "Pool", "DVE", "PE", "Activation")}
        setup_done, x_loaded, tables_loaded, var_in_ready, rstd_in_ready, dve_chain, act_chain, pool_chain, out_stored = (
            sem(k) for k in ("setup_done", "x_loaded", "tables_loaded", "var_in_ready", "rstd_in_ready", "dve_chain",
                             "act_chain", "pool_chain", "out_stored"))

        def settle(eng):
            eng.sem_inc(settled[eng.engine.name], 1)

        def filled(eng, l, key, more=0):
            b = BANK[key]
            eng.wait_ge(bank_filled[b], l * TOTAL[b] + (NTH[key] + more))

        def drained(eng, l, key, before=False):
            b = BANK[key]
            n = NTH[key] - before
            if n > 0:
                eng.wait_ge(bank_drained[b], l * TOTAL[b] + (n - TOTAL[b]))

        def signal(eng, l, name, n):
            eng.wait_ge(sems[name], l * names[name] + (n - names[name]))

        def loaded(eng, l, name):
            s = POS[name] % SLOTS
            eng.wait_ge(slot_loaded[s], l * (16 * SLOT_DMAS[s]) + 16 * (LANDED[name] - SLOT_DMAS[s]))

        def step_count(what, i, q):
            b, per, more = STEP[what]
            if isinstance(i, int):
                more = {("gather0", 1): -2, ("down1", PAIRS): 0}.get((what, 2 * i + q), more)
            return b, per * (PAIRS // ROUNDS), per * q + more

        def step_filled(eng, l, what, i, q):
            b, per, n = step_count(what, i, q)
            eng.wait_ge(bank_filled[b], l * TOTAL[b] + (i * per + (EXPERT_BASE[b] + n)))

        def step_drained(eng, l, what, i, q, before=False):
            b, per, n = step_count(what, i, q)
            eng.wait_ge(bank_drained[b], l * TOTAL[b] + (i * per + (EXPERT_BASE[b] + n - before - TOTAL[b])))

        def slot(name, chunks, cols):
            return ring[:, POS[name] % SLOTS, 0:chunks * cols].rearrange("p (c n) -> p c n", c=chunks)

        def bank(key):
            return psum[:, BANK[key], :]

        def layer_of(name, l):
            return w[name][bass.ds(l - 1, 1)]

        block = ctx.enter_context(nc.Block())

        @block.sync
        def _(sp):
            def cols(l, a, n):
                return layer_of("w_in", l).rearrange("o (p c) n -> p (o c) n", c=DC)[:, :, a:a + n]

            def source(name, l):
                if name == "gf":
                    return [(slot(name, DC, GR), cols(l, COL_GF, GR))]
                if name == "gq":
                    return [(slot(name, DC, 512), cols(l, COL_GQ, 512))]
                if name == "gk":
                    return [(slot(name, DC, 512), cols(l, COL_GK, 512))]
                if name[:2] in ("gv", "gr", "sg"):
                    a = {"gv": COL_GV, "gr": COL_GR, "sg": COL_SG}[name[:2]] + 512 * int(name[2])
                    return [(slot(name, DC, 512), cols(l, a, 512))]
                if name == "mq":
                    return [(slot(name, DC, QR), cols(l, COL_MQ, QR))]
                if name == "mkv":
                    return [(slot(name, DC, KVR + ROPE), cols(l, COL_MKV, KVR + ROPE))]
                if name[0] == "g":
                    a = COL_GATE + int(name[1]) * D + 512 * int(name[2])
                    return [(slot(name, DC, 512), cols(l, a, 512))]
                if name[0] == "b":
                    n, j = int(name[1]), int(name[2])
                    src = w["w_branch"][bass.ds(l - 1, 1), n].rearrange("o (c p) n -> p (o c) n", p=P)
                    return [(slot(name, DC, 512), src[:, :, 512 * j:512 * j + 512])]
                if name[:2] == "uq":
                    c = int(name[2])
                    src = layer_of("mla_w_uq", l)[:, P * c:P * c + P].rearrange("o p n -> p (o n)")
                    return [(ring[:, POS[name] % SLOTS, 0:MH * QK], src)]
                if name == "ukv":
                    return [(slot(name, 2, 2048), layer_of("mla_w_ukv", l).rearrange("o (c p) n -> p (o c) n", p=P))]
                if name[:2] == "wo":
                    j = int(name[2])
                    src = layer_of("w_out", l).rearrange("o (c p) n -> p (o c) n", p=P)
                    return [(slot(name, DC, 512), src[:, :, 512 * j:512 * j + 512])]
                if name == "shgu":
                    return [(ring[:, POS[name] % SLOTS, i * 2048:i * 2048 + 2048],
                             layer_of(k, l).rearrange("o (p c) n -> p (o c n)", c=DC))
                            for i, k in enumerate(("sh_w_gate", "sh_w_up"))]
                if name == "rt":
                    s = POS[name] % SLOTS
                    return [(ring[:, s, 0:2048], layer_of("sh_w_down", l).rearrange("o (p c) n -> p (o c n)", c=2)),
                            (ring[:, s, 2048:2560], layer_of("router_w", l).rearrange("o (p c) n -> p (o c n)", c=DC))]
                if name == "pli":
                    return [(slot(name, 2, D), layer_of("ple_w_in", l).rearrange("o (c p) n -> p (o c) n", p=P))]
                j = int(name[3])
                src = layer_of("ple_w_gate", l).rearrange("o (p c) n -> p (o c) n", c=DC)
                return [(slot(name, DC, 512), src[:, :, 512 * j:512 * j + 512])]

            def expert_loads(l, i, wait):
                for s in range(SLOTS):
                    wait(s)
                    settle(sp)
                    if s % 3 < 2:
                        e = 4 * i + (2 * (s // 3) + s % 3)
                        for k, name in enumerate(("exp_w_gate", "exp_w_up")):
                            src = w[name][bass.ds(l - 1, 1), bass.ds(e, 1)].rearrange("o e (p c) n -> p (o e c n)", c=DC)
                            sp.dma_start(ring[:, s, 2048 * k:2048 * k + 2048], src).then_inc(slot_loaded[s], 16)
                    else:
                        e = 4 * i + 2 * (s // 3)
                        src = w["exp_w_down"][bass.ds(l - 1, 1), bass.ds(e, 2)].rearrange("o e (c p) n -> p (o e c) n", c=2)
                        sp.dma_start(ring[:, s, :].rearrange("p (e n) -> p e n", e=4), src).then_inc(slot_loaded[s], 16)

            def expert_slot_free(l, i, s):
                step_filled(sp, l, ("gate_up0", "gate_up1", "down1")[s % 3], i, s // 3 + 1)

            with sp.Fori(1, DEPTH + 1) as l:
                for n, (name, _) in enumerate(LOADS):
                    if n < SLOTS:
                        expert_slot_free(l - 1, ROUNDS - 1, n)
                    else:
                        filled(sp, l, LOADS[n - SLOTS][1])
                    settle(sp)
                    for dst, src in source(name, l):
                        sp.dma_start(dst, src).then_inc(slot_loaded[n % SLOTS], 16)

                def trunk_slot_free(s):
                    last = LOADS[len(LOADS) - SLOTS + s][1]
                    if last == "shared_down":
                        signal(sp, l, "shared_down_done", 1)
                    else:
                        filled(sp, l, last)

                expert_loads(l, 0, trunk_slot_free)
                with sp.Fori(1, ROUNDS) as i:
                    expert_loads(l, i, lambda s: expert_slot_free(l, i - 1, s))
                signal(sp, l, "spare_ready", 1)
                settle(sp)
                passes = sp.value_load(spare_count[0:1, 0:1], min_val=0, max_val=SPARE - 1)
                with sp.If(passes > 0):
                    for s in (0, 2):
                        expert_slot_free(l, ROUNDS - 1, s)
                        settle(sp)
                    with sp.Fori(0, passes) as n:
                        e = sp.value_load(spare_expert[0:1, bass.ds(n, 1)], min_val=0, max_val=NE - 1)
                        for k, name in enumerate(("exp_w_gate", "exp_w_up")):
                            src = w[name][bass.ds(l - 1, 1), bass.ds(e, 1)].rearrange("o e (p c) n -> p (o e c n)", c=DC)
                            sp.dma_start(ring[:, 0, 2048 * k:2048 * k + 2048], src).then_inc(spare_loaded, 16)
                        src = w["exp_w_down"][bass.ds(l - 1, 1), bass.ds(e, 1)].rearrange("o e (c p) n -> p (o e c) n", p=P)
                        sp.dma_start(ring[:, 2, 0:2048].rearrange("p (c n) -> p c n", c=2), src).then_inc(spare_loaded, 16)
                        sp.wait_ge(spare_used, n + 1)
                        settle(sp)
                    sp.sem_clear(spare_used)
            sp.wait_ge(sems["h_ready"], DEPTH + 1)
            sp.dma_start(out.rearrange("b (t p) d -> p (b t) d", p=P), h[:]).then_inc(out_stored, 16)
            sp.wait_ge(out_stored, 16)

        @block.gpsimd
        def _(pool):
            chain = [0]

            def link(ins):
                chain[0] += 1
                ins.then_inc(pool_chain, 1)
                pool.wait_ge(pool_chain, chain[0])

            pool.dma_start(h[:], w["x"].rearrange("b (t p) d -> p (b t) d", p=P)).then_inc(x_loaded, 16)
            pool.dma_start(ln_g[:], w["ln_in_g"].partition_broadcast(P)).then_inc(x_loaded, 16)
            pool.dma_start(ln_b[:], w["ln_in_b"].partition_broadcast(P)).then_inc(x_loaded, 16)
            pool.dma_start(cos_t[:], cos_tab.rearrange("(t p) i -> p t i", p=P)).then_inc(tables_loaded, 16)
            pool.dma_start(sin_t[:], sin_tab.rearrange("(t p) i -> p t i", p=P)).then_inc(tables_loaded, 16)
            link(pool.memset(neg_half[:], -0.5))
            link(pool.memset(ident[:], 0.0))
            link(pool.affine_select(out=ident[:], in_=ident[:], compare_op=ALU.not_equal, fill=1.0, base=0,
                                    pattern=[[-1, P]], channel_multiplier=1))
            link(pool.memset(gla_mask[:], 1))
            link(pool.affine_select(out=gla_mask[:], in_=gla_mask[:], compare_op=ALU.is_ge, fill=0.0, base=0,
                                    pattern=[[0, TILES], [1, P]], channel_multiplier=-1))
            right = gla_mask[:, :, CHUNK:P]
            link(pool.affine_select(out=right, in_=right, compare_op=ALU.is_ge, fill=0.0, base=-CHUNK,
                                    pattern=[[0, TILES], [0, P - CHUNK]], channel_multiplier=1))
            link(pool.memset(restart[:], 1.0))
            link(pool.memset(restart[:, 0:S:CHUNK], 0.0))
            link(pool.memset(earlier[:], 1.0))
            link(pool.affine_select(out=earlier[:], in_=earlier[:], compare_op=ALU.is_gt, fill=0.0, base=0,
                                    pattern=[[1, NG], [-1, NG]], channel_multiplier=0))
            link(pool.memset(ones[:], 1.0))
            link(pool.affine_select(out=before[:], in_=ones[:], compare_op=ALU.is_gt, fill=0.0, base=0,
                                    pattern=[[1, P]], channel_multiplier=-1))
            link(pool.iota(spare_code[:], pattern=[[-NE, OVER], [-1, NE]], base=256, channel_multiplier=0,
                           allow_small_or_imprecise_dtypes=True))
            pool.iota(iota[:], pattern=[[0, 2], [1, SLOTS_E]], base=0, channel_multiplier=0,
                      allow_small_or_imprecise_dtypes=True).then_inc(setup_done, 1)

            def rsqrt(x):
                return pool.tensor_tensor(x, x, neg_half[:, 0:2], ALU.pow)

            pool.wait_ge(var_in_ready, 1)
            rsqrt(rstd[:, 0:2]).then_inc(rstd_in_ready, 1)

            with pool.Fori(1, DEPTH + 1) as l:
                signal(pool, l, "h_ready", 1)
                settle(pool)

                def small(dst, src):
                    pool.dma_start(dst, src).then_inc(sems["params_loaded"], 16)

                row = lambda name: layer_of(name, l).partition_broadcast(P).rearrange("p o n -> p (o n)")
                with nc.allow_non_contiguous_dma(reason="per-channel vectors onto partitions"):
                    small(fgw[:], layer_of("gla_fg_w", l).rearrange("o r n -> r (o n)"))
                    small(fgb[:], layer_of("gla_fg_b", l).rearrange("o (c p) -> p (o c)", p=P))
                    small(glag[:], layer_of("gla_norm_g", l).rearrange("o (c p) -> p (o c)", p=P))
                    small(qng[:], layer_of("mla_qn_g", l).rearrange("o (c p) -> p (o c)", p=P))
                    small(kvng[:], layer_of("mla_kvn_g", l).rearrange("o (c p) -> p (o c)", p=P))
                    small(sgb[:], layer_of("sg_b", l).rearrange("o g t -> t (o g)"))
                small(sgw[:], layer_of("sg_w", l).rearrange("o g t s -> t (o g) s"))
                small(sgn_g[:], row("sg_norm_g"))
                small(sgn_b[:], row("sg_norm_b"))
                small(ln_g[:], row("ln1_g"))
                small(ln_b[:], row("ln1_b"))
                small(rbias[:], row("router_b"))
                pool.wait_ge(sems["params_loaded"], l * (16 * PARAMS))
                settle(pool)
                pool.affine_select(out=sgw[:], in_=sgw[:], compare_op=ALU.is_ge, fill=0.0, base=0,
                                   pattern=[[0, SGG], [-1, P]], channel_multiplier=1).then_inc(sems["sgw_masked"], 1)
                for i in range(GH):
                    signal(pool, l, "ms_ready", i + 1)
                    rsqrt(rstd[:, 2 * i:2 * i + 2]).then_inc(sems["rms_ready"], 1)
                for i in range(2):
                    signal(pool, l, "ms_ready", GH + i + 1)
                    rsqrt(rstd[:, 8 + 2 * i:10 + 2 * i]).then_inc(sems["rms_ready"], 1)
                signal(pool, l, "var_ready", 1)
                rsqrt(rstd[:, 12:14]).then_inc(sems["rstd_ready"], 1)
                signal(pool, l, "var_ready", 2)
                rsqrt(rstd[:, 12:14]).then_inc(sems["rstd_ready"], 1)
                signal(pool, l, "ln1_done", 1)
                settle(pool)
                pool.dma_start(ptok, w["p"][bass.ds(l - 1, 1)].rearrange("l b (t p) d -> p (l b t) d", p=P)
                               ).then_inc(sems["p_loaded"], 16)
                pool.dma_start(ln_g[:], row("ln2_g")).then_inc(sems["ln2_loaded"], 16)
                pool.dma_start(ln_b[:], row("ln2_b")).then_inc(sems["ln2_loaded"], 16)
                signal(pool, l, "var_ready", 3)
                rsqrt(rstd[:, 12:14]).then_inc(sems["rstd_ready"], 1)

        @block.tensor
        def _(pe):
            for b in range(BANKS):
                pe.sem_inc(bank_filled[b], TOTAL[b])
            pe.wait_ge(setup_done, 1)

            def rows(t):
                return slice(t * P, t * P + P)

            with pe.Fori(1, DEPTH + 1) as l:

                def transposes(key, tiles):
                    drained(pe, l, key, before=True)
                    for i, x in enumerate(tiles):
                        last = pe.transpose(bank(key)[:, i * P:i * P + P], x, ident[:])
                    last.then_inc(bank_filled[BANK[key]], 1)

                def by_token(key, name, t, left, cols, chunks=DC, at=None):
                    drained(pe, l, key, before=True)
                    src = slot(name, chunks, cols) if at is None else at
                    for c in range(chunks):
                        last = pe.matmul(bank(key)[:, 0:cols], left[:, c, rows(t)], src[:, c, :],
                                         start=c == 0, stop=c == chunks - 1)
                    last.then_inc(bank_filled[BANK[key]], 1)

                def by_channel(key, stationary, right, m=P):
                    drained(pe, l, key, before=True)
                    for i, blocks in enumerate(stationary):
                        for c, x in enumerate(blocks):
                            last = pe.matmul(bank(key)[0:m, i * S:i * S + S], x, right[:, c, :],
                                             start=c == 0, stop=c == len(blocks) - 1)
                    last.then_inc(bank_filled[BANK[key]], 1)

                signal(pe, l, "h_ready", 1)
                for t in range(2):
                    for f in range(2):
                        transposes(("hT", t, f), [h[:, t, 4 * f + i:D:DC] for i in range(4)])
                for t in range(2):
                    for f in range(2):
                        drained(pe, l, ("hT", t, f))
                loaded(pe, l, "gf")
                by_channel(("gfr",), [[slot("gf", DC, GR)[:, c, :] for c in range(DC)]], hT, m=GR)
                for kind, name in (("q", "gq"), ("k", "gk")):
                    loaded(pe, l, name)
                    for i in range(2):
                        by_channel((kind, i), [[slot(name, DC, 512)[:, c, (2 * i + n) * P:(2 * i + n + 1) * P]
                                                for c in range(DC)] for n in range(2)], hT)
                pe.wait_ge(sems["params_loaded"], l * (16 * PARAMS))
                drained(pe, l, ("gfr",))
                for i in range(2):
                    drained(pe, l, ("fg", i), before=True)
                    for n in range(2):
                        last = pe.matmul(bank(("fg", i))[:, n * S:n * S + S], fgw[:, (2 * i + n) * P:(2 * i + n + 1) * P],
                                         gfrT[:], start=True, stop=True)
                    last.then_inc(bank_filled[BANK["fg", i]], 1)
                for kind, name in (("v", "gv"), ("gr", "gr")):
                    for j in range(2):
                        loaded(pe, l, f"{name}{j}")
                        for t in range(2):
                            by_token((kind, j, t), f"{name}{j}", t, hT, 512)
                signal(pe, l, "ke_ready", 1)
                for t in range(2):
                    transposes(("ke", t), [keT[:, n, rows(t)] for n in range(GH)])
                signal(pe, l, "sgw_masked", 1)
                transposes(("sgwT",), [sgw[:, g, :] for g in range(SGG)])
                for j in range(2):
                    for t in range(2):
                        drained(pe, l, ("v", j, t))
                for t in range(2):
                    drained(pe, l, ("ke", t))
                for n in range(GH + 1):
                    if n < GH:
                        key = ("att", n)
                        drained(pe, l, key, before=True)
                        for t in range(2):
                            last = pe.matmul(bank(key)[:, rows(t)], ki[:, n, rows(t)], qd[:, n, rows(t)],
                                             start=True, stop=True)
                        last.then_inc(bank_filled[BANK[key]], 1)
                        for c in (0, 2, 1):
                            key = ("ds", n, c % 2)
                            if c < 2:
                                drained(pe, l, key, before=True)
                            part = slice(CHUNK * (c % 2), CHUNK * (c % 2) + CHUNK)
                            last = pe.matmul(bank(key)[:, GDV * (c // 2):GDV * (c // 2) + GDV],
                                             ke[part, c // 2, n * P:n * P + P], gv[part, c // 2, n * GDV:(n + 1) * GDV],
                                             start=True, stop=True)
                            if c:
                                last.then_inc(bank_filled[BANK[key]], 1)
                    if n:
                        key, m = ("o", n - 1), n - 1
                        drained(pe, l, key, before=True)
                        drained(pe, l, ("att", m))
                        drained(pe, l, ("ds", m, 0))
                        for c in range(S // CHUNK):
                            t, queries = c // 2, slice(CHUNK * c, CHUNK * c + CHUNK)
                            o = bank(key)[CHUNK * (c % 2):CHUNK * (c % 2) + CHUNK, t * GDV:(t + 1) * GDV]
                            last = pe.matmul(o, att[:, m % 2, queries], gv[:, t, m * GDV:(m + 1) * GDV],
                                             start=True, stop=c == 0)
                            if c:
                                last = pe.matmul(o, qd[:, m, queries], state[:, c - 1, :], start=False, stop=True)
                        last.then_inc(bank_filled[BANK[key]], 1)
                for z in range(4):
                    loaded(pe, l, f"sg{z}")
                    for t in range(2):
                        by_token(("sg", z, t), f"sg{z}", t, hT, 512)
                for kind, n in (("mq", QR), ("mkv", KVR + ROPE)):
                    loaded(pe, l, kind)
                    for t in range(2):
                        by_token((kind, t), kind, t, hT, n)

                def branch(n):
                    for j in range(2):
                        loaded(pe, l, f"g{n}{j}")
                        loaded(pe, l, f"b{n}{j}")
                        for t in range(2):
                            by_token(("gate", n, j, t), f"g{n}{j}", t, hT, 512)
                            by_token(("proj", n, j, t), f"b{n}{j}", t, bT, 512)

                drained(pe, l, ("o", GH - 1))
                for t in range(2):
                    for f in range(2):
                        transposes(("oaT", t, f), [gr[:, t, (4 * f + i) * P:(4 * f + i + 1) * P] for i in range(4)])
                for t in range(2):
                    for f in range(2):
                        drained(pe, l, ("oaT", t, f))
                branch(0)
                for t in range(2):
                    drained(pe, l, ("mq", t))
                    transposes(("qnT", t), [mq[:, t, c * P:c * P + P] for c in range(QR // P)])
                for t in range(2):
                    drained(pe, l, ("mkv", t))
                    transposes(("ckT", t), [mkv[:, t, c * P:c * P + P] for c in range(KVR // P)])
                signal(pe, l, "krot_ready", 1)
                transposes(("krT",), [krot[:, t, :] for t in range(2)])
                drained(pe, l, ("sgwT",))
                signal(pe, l, "vln_ready", 1)
                for t in range(2):
                    for i in range(2):
                        key = ("sv", t, i)
                        drained(pe, l, key, before=True)
                        for n in range(2):
                            g = 2 * i + n
                            last = pe.matmul(bank(key)[:, n * 256:n * 256 + 256], sgwT[:, g, :],
                                             vv[:, t, g * 256:g * 256 + 256], start=True, stop=True)
                        last.then_inc(bank_filled[BANK[key]], 1)
                for t in range(2):
                    for i in range(2):
                        drained(pe, l, ("sv", t, i))
                    for f in range(2):
                        transposes(("obT", t, f), [u[:, t, (4 * f + i) * P:(4 * f + i + 1) * P] for i in range(4)])
                for t in range(2):
                    for f in range(2):
                        drained(pe, l, ("obT", t, f))
                branch(1)
                for c in range(3):
                    loaded(pe, l, f"uq{c}")
                uq = [ring[:, POS[f"uq{c}"] % SLOTS, 0:MH * QK].rearrange("p (h n) -> p h n", h=MH) for c in range(3)]
                for t in range(2):
                    drained(pe, l, ("qnT", t))
                    drained(pe, l, ("ckT", t))
                drained(pe, l, ("krT",))
                for i in range(4):
                    by_channel(("qn", i), [[uq[c][:, 2 * i + n, 0:NOPE] for c in range(3)] for n in range(2)], qnT)
                for t in range(2):
                    key = ("qr", t)
                    drained(pe, l, key, before=True)
                    for c in range(3):
                        last = pe.matmul(bank(key), qnT[:, c, rows(t)], uq[c][:, :, NOPE:QK], start=c == 0, stop=c == 2)
                    last.then_inc(bank_filled[BANK[key]], 1)
                loaded(pe, l, "ukv")
                ukv = slot("ukv", 2, 2048).rearrange("p c (h n) -> p c h n", h=MH)
                for i in range(4):
                    by_channel(("kn", i), [[ukv[:, c, 2 * i + n, 0:NOPE] for c in range(2)] for n in range(2)], ckT)
                for t in range(2):
                    for j in range(2):
                        key = ("vm", t, j)
                        drained(pe, l, key, before=True)
                        for c in range(2):
                            last = pe.matmul(bank(key), ckT[:, c, rows(t)], ukv[:, c, 4 * j:4 * j + 4, NOPE:NOPE + MV],
                                             start=c == 0, stop=c == 1)
                        last.then_inc(bank_filled[BANK[key]], 1)
                for t in range(2):
                    signal(pe, l, "qrot_ready", t + 1)
                    transposes(("qrT", t), [qrot[:, t, i * P:i * P + P] for i in range(4)])
                for i in range(4):
                    drained(pe, l, ("qn", i))
                    drained(pe, l, ("kn", i))
                for t in range(2):
                    drained(pe, l, ("qrT", t))
                    for j in range(2):
                        drained(pe, l, ("vm", t, j))
                for n in range(MH + 2):
                    if n < MH:
                        key = ("s", n)
                        drained(pe, l, key, before=True)
                        part = slice(ROPE * (n % 2), ROPE * (n % 2) + ROPE)
                        for t in range(2):
                            o, keys = bank(key)[:, P * t:P * t + P * (t + 1)], P * (t + 1)
                            pe.matmul(o, qnope[:, n, rows(t)], knope[:, n, 0:keys], start=True, stop=False)
                            last = pe.matmul(o, qrT[part, n // 2, rows(t)], krT[part, 0:keys], start=False, stop=True)
                        last.then_inc(bank_filled[BANK[key]], 1)
                    if 1 <= n <= MH:
                        signal(pe, l, "prob_ready", n)
                        m = (n - 1) % 2
                        transposes(("pT", n - 1), [prob[:, m, 0:128], prob[:, m, 128:256], prob[:, m, 256:384]])
                    if n >= 2:
                        key, m = ("oc", n - 2), n - 2
                        drained(pe, l, key, before=True)
                        drained(pe, l, ("pT", m))
                        pe.matmul(bank(key)[:, 0:S], vm[:, 0, m * MV:(m + 1) * MV], pT[:, m % 2, 0:S], start=True, stop=False)
                        pe.matmul(bank(key)[:, P:S], vm[:, 1, m * MV:(m + 1) * MV], pT[:, m % 2, S:S + P],
                                  start=False, stop=True).then_inc(bank_filled[BANK[key]], 1)
                for n in range(MH):
                    drained(pe, l, ("oc", n))
                branch(2)
                for j in range(2):
                    for t in range(2):
                        drained(pe, l, ("proj", 2, j, t))
                for t in range(2):
                    for f in range(2):
                        transposes(("mT", t, f), [mixed[:, t, (4 * f + i) * P:(4 * f + i + 1) * P] for i in range(4)])
                for t in range(2):
                    for f in range(2):
                        drained(pe, l, ("mT", t, f))
                for j in range(2):
                    loaded(pe, l, f"wo{j}")
                    for t in range(2):
                        by_token(("wo", j, t), f"wo{j}", t, bT, 512)
                signal(pe, l, "ln1_done", 1)
                for t in range(2):
                    for f in range(2):
                        transposes(("hT2", t, f), [h[:, t, 4 * f + i:D:DC] for i in range(4)])
                for t in range(2):
                    for f in range(2):
                        drained(pe, l, ("hT2", t, f))
                loaded(pe, l, "rt")
                router = ring[:, POS["rt"] % SLOTS, 2048:2560].rearrange("p (c n) -> p c n", c=DC)
                for t in range(2):
                    by_token(("rt", t), "rt", t, hT, NE, at=router)
                signal(pe, l, "p_loaded", 16)
                transposes(("ppT",), [ptok[:, t, c * P:c * P + P] for c in range(2) for t in range(2)])
                drained(pe, l, ("ppT",))
                loaded(pe, l, "pli")
                for j in range(2):
                    loaded(pe, l, f"plg{j}")
                    for t in range(2):
                        by_token(("pli", j, t), "pli", t, pleT, 512, chunks=2,
                                 at=slot("pli", 2, D)[:, :, 512 * j:512 * j + 512])
                        by_token(("plg", j, t), f"plg{j}", t, hT, 512)
                    if j == 0:
                        for t in range(2):
                            key = ("rank", t)
                            signal(pe, l, "score_taken", 1)
                            drained(pe, l, key, before=True)
                            if t:
                                pe.matmul(bank(key)[:, 0:NE], ones[:], sel[:, 0, :], start=True, stop=False)
                            last = pe.matmul(bank(key)[:, 0:NE], before[:], sel[:, t, :], start=t == 0, stop=True)
                            if t:
                                for n in range(2):
                                    last = pe.matmul(bank(key)[:, NE:2 * NE], ones[:], sel[:, n, :], start=n == 0, stop=n == 1)
                            last.then_inc(bank_filled[BANK[key]], 1)

                loaded(pe, l, "shgu")
                src = ring[:, POS["shgu"] % SLOTS, :].rearrange("p (g c n) -> p g c n", g=2, c=DC)
                for t in range(2):
                    key = ("shgu", t)
                    drained(pe, l, key, before=True)
                    for c in range(DC):
                        last = pe.matmul(bank(key), hT[:, c, rows(t)], src[:, :, c, :], start=c == 0, stop=c == DC - 1)
                    last.then_inc(bank_filled[BANK[key]], 1)

                halves = [slice(SLOTS_E * a, SLOTS_E * (a + 1)) for a in range(2)]

                def mm_gather(x):
                    for t in range(2):
                        for part in range(3):
                            for a in range(2):
                                last = pe.matmul(psum[halves[a], 5, :], x[:, t, :], parts[:, part, t, a],
                                                 start=(t, part) == (0, 0), stop=(t, part) == (1, 2))
                    return last

                def mm_rows():
                    for n in range(4):
                        last = pe.transpose(psum[:, 7, n * P:n * P + P], xg[:, n * P:n * P + P], ident[:])
                    return last

                def mm_gate_up(s):
                    src = ring[:, s, :].rearrange("p (g c n) -> p g c n", g=2, c=DC)
                    for c in range(DC):
                        for a in range(2):
                            last = pe.matmul(psum[halves[a], 4, 0:2 * P], xgT[:, c % 4, halves[c // 4]],
                                             src[:, :, c, a * P:(a + 1) * P], start=c == 0, stop=c == DC - 1)
                    return last

                def mm_down(b, j, s):
                    weights = ring[:, s, :].rearrange("p (e c n) -> p e c n", e=2, c=2)
                    for c in range(2):
                        for e in range(2):
                            last = pe.matmul(psum[halves[e], b, :], hbT[:, e, c, :],
                                             weights[:, e, c, 512 * j:512 * j + 512], start=c == 0, stop=c == 1)
                    return last

                def gather(e, i, q):
                    pe.wait_ge(sems["places_ready"], l * (3 * PAIRS) + (i * 6 + (3 * q - 2 + e - 3 * PAIRS)))
                    step_drained(pe, l, f"gather{e}", i, q, before=True)
                    mm_gather(places[:, e]).then_inc(bank_filled[5], 1)

                def rows_turned(e, i, q):
                    step_drained(pe, l, f"gather{e}", i, q)
                    step_drained(pe, l, f"rows{e}", i, q, before=True)
                    mm_rows().then_inc(bank_filled[7], 1)

                def gate_up(e, i, q, s):
                    step_drained(pe, l, f"rows{e}", i, q)
                    step_drained(pe, l, f"gate_up{e}", i, q, before=True)
                    mm_gate_up(s).then_inc(bank_filled[4], 1)

                def hidden_turned(e, i, q):
                    step_drained(pe, l, f"gate_up{e}", i, q)
                    step_drained(pe, l, f"hidden{e}", i, q, before=True)
                    pe.transpose(psum[:, 6, 0:P], hb, ident[:]).then_inc(bank_filled[6], 1)

                def places_turned(i, q):
                    pe.wait_ge(sems["places_ready"], l * (3 * PAIRS) + (i * 6 + (3 * q - 3 * PAIRS)))
                    step_drained(pe, l, "places", i, q, before=True)
                    for t in range(2):
                        last = pe.transpose(psum[:, 7, rows(t)], places_w[:, t, :], ident[:])
                    last.then_inc(bank_filled[7], 1)

                def down(j, i, q, s):
                    if j == 0:
                        step_drained(pe, l, "hidden0", i, q)
                        step_drained(pe, l, "hidden1", i, q)
                    step_drained(pe, l, f"down{j}", i, q, before=True)
                    mm_down(4 + j, j, s).then_inc(bank_filled[4 + j], 1)

                def scatter(t, i, q):
                    if t == 0:
                        step_drained(pe, l, "places", i, q)
                        step_drained(pe, l, "down0", i, q)
                        step_drained(pe, l, "down1", i, q)
                    for j in range(2):
                        pe.matmul(psum[:, 2 * t + j, :], placesT[:, rows(t)], ybuf[:, j, :],
                                  start=False, stop=False, skip_group_check=True)

                gather(0, 0, 1)
                for t in range(2):
                    drained(pe, l, ("shgu", t))
                transposes(("shT",), [sh_hb[:, t * DE + c:(t + 1) * DE:2] for c in range(2) for t in range(2)])
                rows_turned(0, 0, 1)
                drained(pe, l, ("shT",))
                weights = ring[:, POS["rt"] % SLOTS, 0:2048].rearrange("p (c n) -> p c n", c=2)
                for t in range(2):
                    for j in range(2):
                        drained(pe, l, ("y", t, j), before=True)
                        for c in range(2):
                            last = pe.matmul(psum[:, 2 * t + j, :], sh_hbT[:, c, rows(t)],
                                             weights[:, c, 512 * j:512 * j + 512], start=c == 0, stop=False,
                                             skip_group_check=True)
                last.then_inc(sems["shared_down_done"], 1)

                def landed(s, i):
                    a, b = TRUNK_DMAS[s], EXPERT_DMAS[s]
                    pe.wait_ge(slot_loaded[s], l * (16 * SLOT_DMAS[s]) + (i * (16 * b) + 16 * (a + b - SLOT_DMAS[s])))

                def two_pairs(i, first=False, final=False):
                    for q in (1, 2):
                        s = 3 * (q - 1)
                        at_last = final and q == 2
                        landed(s, i)
                        gate_up(0, i, q, s)
                        gather(1, i, q)
                        hidden_turned(0, i, q)
                        if not (first and q == 1):
                            scatter(0, i, q - 1)
                        rows_turned(1, i, q)
                        if not (first and q == 1):
                            scatter(1, i, q - 1)
                        landed(s + 1, i)
                        gate_up(1, i, q, s + 1)
                        if not at_last:
                            gather(0, i, q + 1)
                        hidden_turned(1, i, q)
                        places_turned(i, q)
                        landed(s + 2, i)
                        down(0, i, q, s + 2)
                        if not at_last:
                            rows_turned(0, i, q + 1)
                        down(1, i, q, s + 2)

                two_pairs(0, first=True)
                with pe.Fori(1, ROUNDS - 1) as i:
                    two_pairs(i)
                two_pairs(ROUNDS - 1, final=True)
                for t in range(2):
                    scatter(t, ROUNDS - 1, 2)
                signal(pe, l, "spare_ready", 1)
                settle(pe)
                passes = pe.value_load(spare_count[0:1, 0:1], min_val=0, max_val=SPARE - 1)
                with pe.If(passes > 0):
                    with pe.Fori(0, passes) as n:
                        pe.drain().then_inc(pe_to_dve, 1)
                        pe.wait_ge(dve_to_pe, n * 4 + 1)
                        mm_gather(places[:, 0]).then_inc(pe_to_act, 1)
                        for t in range(2):
                            last = pe.transpose(psum[:, 6, rows(t)], places_w[:, t, :], ident[:])
                        last.then_inc(pe_to_dve, 1)
                        pe.wait_ge(act_to_pe, n * 3 + 1)
                        mm_rows().then_inc(pe_to_act, 1)
                        pe.wait_ge(spare_loaded, n * 48 + 48)
                        pe.wait_ge(act_to_pe, n * 3 + 2)
                        mm_gate_up(0).then_inc(pe_to_act, 1)
                        pe.wait_ge(dve_to_pe, n * 4 + 3)
                        pe.transpose(psum[:, 6, 0:P], hb, ident[:]).then_inc(pe_to_act, 1)
                        pe.wait_ge(act_to_pe, n * 3 + 3)
                        weights = ring[:, 2, 0:2048].rearrange("p (c n) -> p c n", c=2)
                        for c in range(2):
                            for j in range(2):
                                last = pe.matmul(psum[halves[j], 5, :], hbT[:, 0, c, :],
                                                 weights[:, c, 512 * j:512 * j + 512], start=c == 0, stop=c == 1)
                        last.then_inc(pe_to_dve, 1)
                        pe.drain().then_inc(spare_used, 1)
                        pe.wait_ge(dve_to_pe, n * 4 + 4)
                        for t in range(2):
                            for j in range(2):
                                pe.matmul(psum[:, 2 * t + j, :], placesT[halves[j], rows(t)], ybuf[halves[j], 0, :],
                                          start=False, stop=False, skip_group_check=True)
                    pe.sem_clear(dve_to_pe)
                    pe.sem_clear(act_to_pe)
                    pe.sem_clear(spare_loaded)
                for b in range(4):
                    pe.drain().then_inc(bank_filled[b], 1)

        @block.scalar
        def _(act):
            chain = [0]

            def link(ins):
                chain[0] += 1
                ins.then_inc(act_chain, 1)
                act.wait_ge(act_chain, chain[0])

            with act.Fori(1, DEPTH + 1) as l:
                chain[0] = 0

                def move(key, dst, src, func=ACT.Copy, scale=1.0):
                    filled(act, l, key)
                    act.activation(dst, src, func, scale=scale).then_inc(bank_drained[BANK[key]], 1)

                def four_blocks(key):
                    return bank(key).rearrange("p (c n) -> p c n", c=4)

                for t in range(2):
                    move(("hT", t, 0), hT[:, 0:4, t * P:t * P + P], four_blocks(("hT", t, 0)))
                move(("gfr",), gfrT[:], psum[0:GR, BANK["gfr",], 0:S])
                signal(act, l, "abs_ready", 1)
                link(act.activation(tmp_e, tmp_e, ACT.Exp, scale=-1.0))
                act.activation(tmp_e, tmp_e, ACT.Ln, bias=1.0).then_inc(sems["log_ready"], 1)
                signal(act, l, "cum_ready", 1)
                act.activation(qd, b_cum, ACT.Exp, scale=1.0 / GATE_TAU).then_inc(sems["exp_ready"], 1)
                act.activation(ki, b_cum, ACT.Exp, scale=-1.0 / GATE_TAU).then_inc(sems["exp_ready"], 1)
                signal(act, l, "cum_ready", 2)
                act.activation(keT, tmp_e, ACT.Exp, scale=1.0 / GATE_TAU).then_inc(sems["exp_ready"], 1)
                for j in range(2):
                    for t in range(2):
                        move(("v", j, t), gv[:, t, 512 * j:512 * j + 512], bank(("v", j, t)))
                for j in range(2):
                    for t in range(2):
                        move(("gr", j, t), gr[:, t, 512 * j:512 * j + 512], bank(("gr", j, t)), ACT.Silu)
                for t in range(2):
                    move(("ke", t), ke[:, t, :], bank(("ke", t)))
                move(("sgwT",), sgwT[:], four_blocks(("sgwT",)))
                for n in range(GH):
                    key = ("o", n)
                    filled(act, l, key)
                    for t in range(2):
                        ins = act.activation(junk[:, t, 0:GDV], bank(key)[:, t * GDV:(t + 1) * GDV], ACT.Square,
                                             accum_out=ssq[:, 2 * n + t:2 * n + t + 1])
                        if t == 0:
                            link(ins)
                    link(ins)
                    act.activation(rstd[:, 2 * n:2 * n + 2], ssq[:, 2 * n:2 * n + 2], ACT.Copy, scale=1.0 / GDV,
                                   bias=RMS_EPS).then_inc(sems["ms_ready"], 1)
                for z in range(4):
                    for t in range(2):
                        half = u if z < 2 else vv
                        move(("sg", z, t), half[:, t, 512 * (z % 2):512 * (z % 2) + 512], bank(("sg", z, t)), ACT.Gelu)
                for t in range(2):
                    filled(act, l, ("mq", t))
                    filled(act, l, ("mkv", t))
                    link(act.activation(junk[:, t, 0:QR], bank(("mq", t))[:, 0:QR], ACT.Square,
                                        accum_out=ssq[:, 8 + 2 * t:9 + 2 * t]))
                    link(act.activation(junk[:, t, 0:KVR], bank(("mkv", t))[:, 0:KVR], ACT.Square,
                                        accum_out=ssq[:, 9 + 2 * t:10 + 2 * t]))
                    link(act.activation(rstd[:, 8 + 2 * t:9 + 2 * t], ssq[:, 8 + 2 * t:9 + 2 * t], ACT.Copy,
                                        scale=1.0 / QR, bias=RMS_EPS))
                    act.activation(rstd[:, 9 + 2 * t:10 + 2 * t], ssq[:, 9 + 2 * t:10 + 2 * t], ACT.Copy,
                                   scale=1.0 / KVR, bias=RMS_EPS).then_inc(sems["ms_ready"], 1)

                def gates(kind, pair):
                    for j in range(2):
                        for t in range(2):
                            key = kind(j, t)
                            filled(act, l, key)
                            if (j, t) != (0, 0):
                                before = pair(*[(0, 0), (0, 1), (1, 0)][2 * j + t - 1])
                                drained(act, l, before)
                            act.activation(gsig[:, t, :], bank(key), ACT.Sigmoid).then_inc(bank_drained[BANK[key]], 1)

                gates(lambda j, t: ("gate", 0, j, t), lambda j, t: ("proj", 0, j, t))
                for t in range(2):
                    for f in range(2):
                        move(("obT", t, f), bT[:, 4 * f:4 * f + 4, t * P:t * P + P], four_blocks(("obT", t, f)))
                gates(lambda j, t: ("gate", 1, j, t), lambda j, t: ("proj", 1, j, t))
                for kind, dst in (("qn", qnope), ("kn", knope)):
                    for i in range(4):
                        move((kind, i), dst[:, 2 * i:2 * i + 2, :], bank((kind, i)).rearrange("p (c n) -> p c n", c=2))
                for t in range(2):
                    for j in range(2):
                        move(("vm", t, j), vm[:, t, 512 * j:512 * j + 512], bank(("vm", t, j)))
                for t in range(2):
                    move(("qrT", t), qrT[:, :, t * P:t * P + P], four_blocks(("qrT", t)))
                for n in range(MH + 1):
                    if n < MH:
                        signal(act, l, "max_ready", n + 1)
                        if n >= 2:
                            filled(act, l, ("pT", n - 2))
                        for r, (part, a, k) in enumerate(regions):
                            ins = act.activation(prob[part, n % 2, a:a + k], bank(("s", n))[part, a:a + k], ACT.Exp,
                                                 bias=sm_max[part, n % 2, a // P:a // P + 1], scale=QK ** -0.5,
                                                 accum_out=sm_sum[part, n % 2, a // P:a // P + 1])
                            if r < 3:
                                link(ins)
                        ins.then_inc(sems["exp_p"], 1)
                    if n:
                        move(("pT", n - 1), pT[:, (n - 1) % 2, :], bank(("pT", n - 1))[:, 0:384])
                gates(lambda j, t: ("gate", 2, j, t), lambda j, t: ("proj", 2, j, t))
                for t in range(2):
                    move(("mT", t, 0), bT[:, 0:4, t * P:t * P + P], four_blocks(("mT", t, 0)))
                for t in range(2):
                    move(("hT2", t, 0), hT[:, 0:4, t * P:t * P + P], four_blocks(("hT2", t, 0)))
                for t in range(2):
                    move(("rt", t), score[:, t, :], bank(("rt", t))[:, 0:NE], ACT.Sigmoid)
                move(("ppT",), pleT, bank(("ppT",)).rearrange("p (c n) -> p c n", c=2))
                gates(lambda j, t: ("plg", j, t), lambda j, t: ("pli", j, t))

                for t in range(2):
                    filled(act, l, ("shgu", t))
                    act.activation(sgate[:, t, :], bank(("shgu", t))[:, 0:DE], ACT.Silu).then_inc(sems["shared_silu"], 1)

                def take(what, dst, src, b, i, q):
                    step_filled(act, l, what, i, q)
                    act.activation(dst, src, ACT.Copy).then_inc(bank_drained[b], 1)

                def take_gathered(e, i, q):
                    take(f"gather{e}", xg, psum[:, 5, :], 5, i, q)

                def take_rows(e, i, q):
                    take(f"rows{e}", xgT.rearrange("p a b -> p (a b)"), psum[:, 7, :], 7, i, q)

                def take_hidden(e, i, q):
                    take(f"hidden{e}", hbT[:, e].rearrange("p a b -> p (a b)"), psum[:, 6, 0:P], 6, i, q)

                def silu(e, i, q):
                    step_filled(act, l, f"gate_up{e}", i, q)
                    act.activation(sgate_e, psum[:, 4, 0:P], ACT.Silu).then_inc(sems["silu_ready"], 1)

                def act_pairs(i, final=False):
                    for q in (1, 2):
                        silu(0, i, q)
                        take_gathered(1, i, q)
                        take_hidden(0, i, q)
                        take_rows(1, i, q)
                        silu(1, i, q)
                        if not (final and q == 2):
                            take_gathered(0, i, q + 1)
                        take_hidden(1, i, q)
                        if not (final and q == 2):
                            take_rows(0, i, q + 1)

                take_gathered(0, 0, 1)
                take_rows(0, 0, 1)
                act_pairs(0)
                with act.Fori(1, ROUNDS - 1) as i:
                    act_pairs(i)
                act_pairs(ROUNDS - 1, final=True)
                signal(act, l, "spare_ready", 1)
                settle(act)
                passes = act.value_load(spare_count[0:1, 0:1], min_val=0, max_val=SPARE - 1)
                with act.If(passes > 0):
                    with act.Fori(0, passes) as n:
                        act.wait_ge(pe_to_act, n * 4 + 1)
                        act.activation(xg, psum[:, 5, :], ACT.Copy).then_inc(act_to_pe, 1)
                        act.wait_ge(pe_to_act, n * 4 + 2)
                        act.activation(xgT.rearrange("p a b -> p (a b)"), psum[:, 7, :], ACT.Copy).then_inc(act_to_pe, 1)
                        act.wait_ge(pe_to_act, n * 4 + 3)
                        act.activation(sgate_e, psum[:, 4, 0:P], ACT.Silu).then_inc(act_to_dve, 1)
                        act.wait_ge(pe_to_act, n * 4 + 4)
                        act.activation(hbT[:, 0].rearrange("p a b -> p (a b)"), psum[:, 6, 0:P], ACT.Copy).then_inc(act_to_pe, 1)
                    act.sem_clear(pe_to_act)
                act.wait_ge(act_chain, chain[0])
                act.sem_clear(act_chain)

        @block.vector
        def _(dve):
            chain = [0]

            def link(ins):
                chain[0] += 1
                ins.then_inc(dve_chain, 1)
                dve.wait_ge(dve_chain, chain[0])

            def end_chain():
                dve.sem_clear(dve_chain)
                chain[0] = 0

            def link_clear(ins):
                ins.then_inc(dve_step, 1)
                dve.wait_ge(dve_step, 1)
                dve.sem_clear(dve_step)

            def normalise(x, g, b, announce_var, wait_rstd, column, announce):
                for t in range(2):
                    for i in range(2):
                        link(dve.bn_stats(stats[:, t, i, :], x[:, t, 512 * i:512 * i + 512]))
                    link(dve.bn_aggr(mv[:, t, :], stats[:, t, :, :].rearrange("p a b -> p (a b)")))
                announce_var(dve.tensor_scalar(rstd[:, column:column + 2], mv[:, :, 1], LN_EPS, None, ALU.add))
                wait_rstd()
                for t in range(2):
                    link(dve.tensor_scalar(x[:, t, :], x[:, t, :], mv[:, t, 0:1], rstd[:, column + t:column + t + 1],
                                           ALU.subtract, ALU.mult))
                link(dve.tensor_tensor(x, x, g[:].unsqueeze(1).to_broadcast([P, 2, D]), ALU.mult))
                announce(dve.tensor_tensor(x, x, b[:].unsqueeze(1).to_broadcast([P, 2, D]), ALU.add))

            dve.wait_ge(x_loaded, 48)
            normalise(h[:], ln_g, ln_b, lambda ins: ins.then_inc(var_in_ready, 1),
                      lambda: dve.wait_ge(rstd_in_ready, 1), 0, lambda ins: ins.then_inc(sems["h_ready"], 1))
            dve.wait_ge(setup_done, 1)
            dve.wait_ge(tables_loaded, 32)
            end_chain()

            with dve.Fori(1, DEPTH + 1) as l:

                def done(ins, key):
                    ins.then_inc(bank_drained[BANK[key]], 1)

                def four_blocks(key):
                    return bank(key).rearrange("p (c n) -> p c n", c=4)

                for t in range(2):
                    filled(dve, l, ("hT", t, 1))
                    done(dve.tensor_copy(hT[:, 4:8, t * P:t * P + P], four_blocks(("hT", t, 1))), ("hT", t, 1))
                link(dve.memset(att, 0.0))
                dve.wait_ge(sems["params_loaded"], l * (16 * PARAMS))
                for i in range(2):
                    filled(dve, l, ("fg", i))
                    for n in range(2):
                        ins = dve.tensor_scalar(b_cum[:, 2 * i + n, :], bank(("fg", i))[:, n * S:n * S + S],
                                                fgb[:, 2 * i + n:2 * i + n + 1], None, ALU.add)
                        if n == 0:
                            link(ins)
                    done(ins, ("fg", i))
                    drained(dve, l, ("fg", i))
                dve.scalar_tensor_tensor(tmp_e, b_cum, -1.0, b_cum, ALU.mult, ALU.max).then_inc(sems["abs_ready"], 1)
                signal(dve, l, "log_ready", 1)
                link(dve.scalar_tensor_tensor(keT, b_cum, 0.0, tmp_e, ALU.min, ALU.subtract))
                for n in range(GH):
                    ins = dve.tensor_tensor_scan(b_cum[:, n, :], restart[:], keT[:, n, :], 0.0, ALU.mult, ALU.add)
                    if n < GH - 1:
                        link(ins)
                ins.then_inc(sems["cum_ready"], 1)
                signal(dve, l, "cum_ready", 1)
                chunks = lambda x: x.rearrange("p h (c t) -> p (h c) t", t=CHUNK)
                ends = chunks(b_cum)[:, :, CHUNK - 1:CHUNK].to_broadcast([P, GH * S // CHUNK, CHUNK])
                dve.tensor_tensor(chunks(tmp_e), ends, chunks(b_cum), ALU.subtract).then_inc(sems["cum_ready"], 1)
                signal(dve, l, "exp_ready", 1)
                link(dve.tensor_copy(decay[:].rearrange("p h c -> p (h c)"), chunks(qd)[:, :, CHUNK - 1]))
                two = lambda key: bank(key).rearrange("p (c n) -> p c n", c=2)
                for i in range(2):
                    filled(dve, l, ("q", i))
                    done(dve.scalar_tensor_tensor(qd[:, 2 * i:2 * i + 2, :], two(("q", i)), GDK ** -0.5,
                                                  qd[:, 2 * i:2 * i + 2, :], ALU.mult, ALU.mult), ("q", i))
                signal(dve, l, "exp_ready", 3)
                for i in range(2):
                    filled(dve, l, ("k", i))
                    link(dve.tensor_tensor(ki[:, 2 * i:2 * i + 2, :], two(("k", i)), ki[:, 2 * i:2 * i + 2, :], ALU.mult))
                    done(dve.tensor_tensor(keT[:, 2 * i:2 * i + 2, :], two(("k", i)), keT[:, 2 * i:2 * i + 2, :],
                                           ALU.mult), ("k", i))
                    drained(dve, l, ("k", i))
                dve.nop().then_inc(sems["ke_ready"], 1)
                for n in range(GH + 1):
                    if n < GH:
                        filled(dve, l, ("att", n))
                        settle(dve)
                        done(dve.copy_predicated(att[:, n % 2, :], gla_mask[:].rearrange("p t s -> p (t s)"),
                                                 bank(("att", n))[:, 0:S]), ("att", n))
                        filled(dve, l, ("ds", n, 1))
                        if n:
                            filled(dve, l, ("o", n - 1))
                        ds = bank(("ds", n, 0))
                        link(dve.tensor_copy(state[:, 0, :], ds[:, 0:GDV]))
                        done(dve.scalar_tensor_tensor(state[:, 1, :], state[:, 0, :], decay[:, n, 1:2],
                                                      bank(("ds", n, 1))[:, 0:GDV], ALU.mult, ALU.add), ("ds", n, 1))
                        drained(dve, l, ("ds", n, 1))
                        done(dve.scalar_tensor_tensor(state[:, 2, :], state[:, 1, :], decay[:, n, 2:3],
                                                      ds[:, GDV:2 * GDV], ALU.mult, ALU.add), ("ds", n, 0))
                    if n:
                        m = n - 1
                        if n == 1:
                            for j in range(2):
                                for t in range(2):
                                    drained(dve, l, ("gr", j, t))
                        signal(dve, l, "rms_ready", m + 1)
                        for t in range(2):
                            g = gr[:, t, m * GDV:(m + 1) * GDV]
                            ins = dve.scalar_tensor_tensor(g, bank(("o", m))[:, t * GDV:(t + 1) * GDV],
                                                           rstd[:, 2 * m + t:2 * m + t + 1], g, ALU.mult, ALU.mult)
                        done(ins, ("o", m))
                for t in range(2):
                    signal(dve, l, "rms_ready", GH + t + 1)
                    done(dve.tensor_scalar(mq[:, t, :], bank(("mq", t))[:, 0:QR], rstd[:, 8 + 2 * t:9 + 2 * t], None,
                                           ALU.mult), ("mq", t))
                    link(dve.tensor_scalar(mkv[:, t, 0:KVR], bank(("mkv", t))[:, 0:KVR], rstd[:, 9 + 2 * t:10 + 2 * t],
                                           None, ALU.mult))
                    done(dve.tensor_copy(mkv[:, t, KVR:KVR + ROPE], bank(("mkv", t))[:, KVR:KVR + ROPE]), ("mkv", t))
                    drained(dve, l, ("mkv", t))
                for z in (2, 3):
                    for t in range(2):
                        drained(dve, l, ("sg", z, t))
                normalise(vv, sgn_g, sgn_b, lambda ins: ins.then_inc(sems["var_ready"], 1),
                          lambda: signal(dve, l, "rstd_ready", 1), 12, lambda ins: ins.then_inc(sems["vln_ready"], 1))
                k1, k2 = mkv[:, :, KVR:KVR + HALF], mkv[:, :, KVR + HALF:KVR + ROPE]
                kt = [rtmp[:, i, 0:2 * HALF].rearrange("p (t n) -> p t n", t=2) for i in range(4)]
                for i, (a, b) in enumerate(((k1, cos_t), (k2, sin_t), (k1, sin_t), (k2, cos_t))):
                    link(dve.tensor_tensor(kt[i], a, b[:], ALU.mult))
                for n in range(2):
                    link(dve.tensor_tensor(krot[:, :, ROPE * n:ROPE * n + HALF], kt[0], kt[1], ALU.subtract))
                    ins = dve.tensor_tensor(krot[:, :, ROPE * n + HALF:ROPE * n + ROPE], kt[2], kt[3], ALU.add)
                    if n == 0:
                        link(ins)
                ins.then_inc(sems["krot_ready"], 1)
                for t in range(2):
                    for f in range(2):
                        key = ("oaT", t, f)
                        filled(dve, l, key)
                        gain = glag[:, 4 * f:4 * f + 4].unsqueeze(2).to_broadcast([P, 4, P])
                        done(dve.tensor_tensor(bT[:, 4 * f:4 * f + 4, t * P:t * P + P], four_blocks(key), gain,
                                               ALU.mult), key)

                def merge(n):
                    for j in range(2):
                        for t in range(2):
                            filled(dve, l, ("proj", n, j, t))
                            drained(dve, l, ("gate", n, j, t))
                            m = mixed[:, t, 512 * j:512 * j + 512]
                            if n == 0:
                                done(dve.tensor_tensor(m, bank(("proj", n, j, t)), gsig[:, t, :], ALU.mult),
                                     ("proj", n, j, t))
                            else:
                                if (j, t) == (0, 0):
                                    drained(dve, l, ("proj", n - 1, 1, 1))
                                link(dve.tensor_tensor(gsig[:, t, :], bank(("proj", n, j, t)), gsig[:, t, :], ALU.mult))
                                done(dve.tensor_tensor(m, m, gsig[:, t, :], ALU.add), ("proj", n, j, t))

                merge(0)
                for t in range(2):
                    key = ("qnT", t)
                    filled(dve, l, key)
                    done(dve.tensor_tensor(qnT[:, :, t * P:t * P + P],
                                           bank(key)[:, 0:QR].rearrange("p (c n) -> p c n", c=3),
                                           qng[:].unsqueeze(2).to_broadcast([P, 3, P]), ALU.mult), key)
                for t in range(2):
                    key = ("ckT", t)
                    filled(dve, l, key)
                    done(dve.tensor_tensor(ckT[:, :, t * P:t * P + P],
                                           bank(key)[:, 0:KVR].rearrange("p (c n) -> p c n", c=2),
                                           kvng[:].unsqueeze(2).to_broadcast([P, 2, P]), ALU.mult), key)
                filled(dve, l, ("krT",))
                done(dve.tensor_copy(krT, bank(("krT",))[:, 0:S]), ("krT",))
                for z in (0, 1):
                    for t in range(2):
                        drained(dve, l, ("sg", z, t))
                for t in range(2):
                    for i in range(2):
                        filled(dve, l, ("sv", t, i))
                        for n in range(2):
                            g = 2 * i + n
                            part = u[:, t, g * 256:g * 256 + 256]
                            ins = dve.scalar_tensor_tensor(part, bank(("sv", t, i))[:, n * 256:n * 256 + 256],
                                                           sgb[:, g:g + 1], part, ALU.add, ALU.mult)
                        done(ins, ("sv", t, i))
                merge(1)
                pair = lambda x: x.rearrange("p (h n) -> p h n", h=MH)
                for t in range(2):
                    key = ("qr", t)
                    filled(dve, l, key)
                    q1, q2 = pair(bank(key))[:, :, 0:HALF], pair(bank(key))[:, :, HALF:ROPE]
                    cs, sn = (x[:, t, :].unsqueeze(1).to_broadcast([P, MH, HALF]) for x in (cos_t, sin_t))
                    qt = [rtmp[:, i, :].rearrange("p (h n) -> p h n", h=MH) for i in range(4)]
                    for i, (a, b) in enumerate(((q1, cs), (q2, sn), (q1, sn), (q2, cs))):
                        link(dve.tensor_tensor(qt[i], a, b, ALU.mult))
                    dve.nop().then_inc(bank_drained[BANK[key]], 1)
                    link(dve.tensor_tensor(pair(qrot[:, t, :])[:, :, 0:HALF], qt[0], qt[1], ALU.subtract))
                    link(dve.tensor_tensor(pair(qrot[:, t, :])[:, :, HALF:ROPE], qt[2], qt[3], ALU.add))
                    dve.nop().then_inc(sems["qrot_ready"], 1)
                for n in range(2):
                    link(dve.memset(prob[0:CHUNK, n, P - CHUNK:P], 0.0))
                    link(dve.memset(prob[0:CHUNK, n, 3 * P - CHUNK:3 * P], 0.0))
                for n in range(MH + 2):
                    if n < MH:
                        filled(dve, l, ("s", n))
                        if n >= 2:
                            signal(dve, l, "exp_p", n - 1)
                        for part, a, k in regions:
                            link(dve.reduce_max(sm_top[part, n % 2, a // P:a // P + 1], bank(("s", n))[part, a:a + k],
                                                axis=mybir.AxisListType.X))
                        dve.tensor_scalar(sm_max[:, n % 2, :], sm_top[:, n % 2, :], -(QK ** -0.5), None,
                                          ALU.mult).then_inc(sems["max_ready"], 1)
                        signal(dve, l, "exp_p", n + 1)
                        link(dve.reciprocal(sm_inv[:, n % 2, :], sm_sum[:, n % 2, :]))
                        dve.nop().then_inc(bank_drained[BANK["s", n]], 1)
                        link(dve.tensor_scalar(prob[:, n % 2, 0:P], prob[:, n % 2, 0:P], sm_inv[:, n % 2, 0:1], None,
                                               ALU.mult))
                        dve.tensor_scalar(prob[:, n % 2, P:3 * P], prob[:, n % 2, P:3 * P], sm_inv[:, n % 2, 1:2], None,
                                          ALU.mult).then_inc(sems["prob_ready"], 1)
                    if n >= 2:
                        filled(dve, l, ("oc", n - 2))
                        done(dve.tensor_copy(bT[:, n - 2, :], bank(("oc", n - 2))[:, 0:S]), ("oc", n - 2))
                merge(2)
                for t in range(2):
                    key = ("mT", t, 1)
                    filled(dve, l, key)
                    done(dve.tensor_copy(bT[:, 4:8, t * P:t * P + P], four_blocks(key)), key)
                for j in range(2):
                    for t in range(2):
                        key, part = ("wo", j, t), h[:, t, 512 * j:512 * j + 512]
                        filled(dve, l, key)
                        done(dve.scalar_tensor_tensor(part, part, ALPHA, bank(key), ALU.mult, ALU.add), key)
                for j in range(2):
                    for t in range(2):
                        drained(dve, l, ("wo", j, t))
                normalise(h[:], ln_g, ln_b, lambda ins: ins.then_inc(sems["var_ready"], 1),
                          lambda: signal(dve, l, "rstd_ready", 2), 12, lambda ins: ins.then_inc(sems["ln1_done"], 1))
                for t in range(2):
                    key = ("hT2", t, 1)
                    filled(dve, l, key)
                    done(dve.tensor_copy(hT[:, 4:8, t * P:t * P + P], four_blocks(key)), key)
                end_chain()
                signal(dve, l, "ln1_done", 1)
                for t in range(2):
                    drained(dve, l, ("rt", t))
                    link(dve.tensor_tensor(biased[:, t, :], score[:, t, :], rbias[:], ALU.add))
                    for g in range(NG):
                        ins = dve.max(grp8[:, g, :], biased[:, t, 8 * g:8 * g + 8])
                    link(ins)
                    link(dve.tensor_tensor(gsum, grp8[:, :, 0], grp8[:, :, 1], ALU.add))
                    mine = gsum.unsqueeze(2).to_broadcast([P, NG, NG])
                    other = gsum.unsqueeze(1).to_broadcast([P, NG, NG])
                    link(dve.tensor_tensor(cmp, other, mine, ALU.is_equal))
                    link(dve.tensor_tensor(cmp2, cmp, earlier[:], ALU.mult))
                    link(dve.tensor_tensor(cmp, other, mine, ALU.is_gt))
                    link(dve.tensor_tensor(cmp, cmp, cmp2, ALU.add))
                    link(dve.reduce_sum(gkeep, cmp, axis=mybir.AxisListType.X))
                    link(dve.tensor_scalar(gkeep, gkeep, TOPG - 0.5, None, ALU.is_lt))
                    keep8 = gkeep.unsqueeze(2).to_broadcast([P, NG, 8])
                    by_group = lambda x: x.rearrange("p (g n) -> p g n", g=NG)
                    link(dve.tensor_tensor(by_group(biased[:, t, :]), by_group(biased[:, t, :]), keep8, ALU.mult))
                    link(dve.tensor_scalar(gkeep, gkeep, 1.0, -LOW_FILL, ALU.subtract, ALU.mult))
                    link(dve.tensor_tensor(by_group(biased[:, t, :]), by_group(biased[:, t, :]), keep8, ALU.add))
                    link(dve.max(top8, biased[:, t, :]))
                    link(dve.match_replace(rep, top8, biased[:, t, :], TAKEN))
                    link(dve.tensor_tensor(rep, rep, biased[:, t, :], ALU.not_equal))
                    link(dve.tensor_copy(sel[:, t, :], rep))
                    link(dve.tensor_tensor(wts[:, t, :], rep, score[:, t, :], ALU.mult))
                    link(dve.reduce_sum(wsum[:, 0:1], wts[:, t, :], axis=mybir.AxisListType.X))
                    link(dve.reciprocal(wsum[:, 1:2], wsum[:, 0:1]))
                    link(dve.tensor_scalar(wts[:, t, :], wts[:, t, :], wsum[:, 1:2], ROUTED_SCALE, ALU.mult, ALU.mult))
                dve.nop().then_inc(sems["score_taken"], 1)
                permuted = lambda x: x.rearrange("p t (c a i) -> p t a i c", a=2, i=4)
                for t in range(2):
                    for a in range(2):
                        whole, left = permuted(h[:])[:, t, a], permuted(rest)[:, t, a]
                        link(dve.tensor_copy(parts[:, 0, t, a], whole))
                        link(dve.tensor_tensor(left, whole, parts[:, 0, t, a], ALU.subtract))
                        link(dve.tensor_copy(parts[:, 1, t, a], left))
                        link(dve.tensor_tensor(parts[:, 2, t, a], left, parts[:, 1, t, a], ALU.subtract))
                for j in range(2):
                    if j:
                        for t in range(2):
                            filled(dve, l, ("rank", t))
                            link(dve.scalar_tensor_tensor(pos[:, t, :], bank(("rank", t))[:, 0:NE], 1.0, sel[:, t, :],
                                                          ALU.add, ALU.mult))
                            link(dve.tensor_scalar(pos[:, t, :], pos[:, t, :], 1.0, None, ALU.subtract))
                            if t == 0:
                                done(dve.nop(), ("rank", 0))
                                continue
                            chosen = bank(("rank", t))[:, NE:2 * NE]
                        for b in range(OVER):
                            link(dve.scalar_tensor_tensor(spare_key[:, b * NE:(b + 1) * NE], chosen, (b + 1) * SLOTS_E + 0.5,
                                                          spare_code[:, b, :], ALU.is_gt, ALU.mult))
                        done(dve.nop(), ("rank", 1))
                        for n in range(SPARE // 8):
                            best = spare_top[:, 8 * n:8 * n + 8]
                            link(dve.max(best, spare_key))
                            link(dve.match_replace(spare_key, best, spare_key, 0.0))
                        link(dve.tensor_scalar(spare_unit[:], spare_top[:], -1.0, 256.0, ALU.mult, ALU.add))
                        link(dve.tensor_single_scalar(spare_expert[:], spare_unit[:], NE - 1, ALU.bitwise_and))
                        link(dve.tensor_tensor(spare_rank[:], spare_unit[:], spare_expert[:], ALU.subtract))
                        link(dve.tensor_scalar(spare_rank[:], spare_rank[:], SLOTS_E / NE, float(SLOTS_E), ALU.mult, ALU.add))
                        link(dve.tensor_scalar(spare_top[:], spare_top[:], 0.5, None, ALU.is_gt))
                        link(dve.reduce_sum(spare_sum[:], spare_top[:], axis=mybir.AxisListType.X))
                        dve.tensor_copy(spare_count[:], spare_sum[:]).then_inc(sems["spare_ready"], 1)
                    for t in range(2):
                        filled(dve, l, ("pli", j, t))
                        drained(dve, l, ("plg", j, t))
                        link(dve.tensor_tensor(mixed[:, t, 512 * j:512 * j + 512], bank(("pli", j, t)), gsig[:, t, :],
                                               ALU.mult))
                        dve.nop().then_inc(bank_drained[BANK["pli", j, t]], 1)
                for t in range(2):
                    link(dve.scalar_tensor_tensor(mixed[:, t, :], h[:, t, :], ALPHA, mixed[:, t, :], ALU.mult, ALU.add))

                def column(x, t, e, i, q):
                    return x[:, t, bass.ds(4 * i + (2 * q - 2 + e), 1)]

                def place(e, i, q):
                    for t in range(2):
                        last = dve.tensor_scalar(places[:, e, t, :], iota[:, 0:SLOTS_E], column(pos, t, e, i, q), None,
                                                 ALU.is_equal)
                    last.then_inc(sems["places_ready"], 1)

                def place_weights(i, q):
                    for e in range(2):
                        for t in range(2):
                            last = dve.tensor_scalar(places_w[:, t, SLOTS_E * e:SLOTS_E * (e + 1)], iota[:, 0:SLOTS_E],
                                                     column(pos, t, e, i, q), column(wts, t, e, i, q), ALU.is_equal,
                                                     ALU.mult)
                    last.then_inc(sems["places_ready"], 1)

                def gated(e, i, q):
                    dve.wait_ge(sems["silu_ready"], l * NE + (4 * i + (2 * q - 1 + e - NE)))
                    dve.tensor_tensor(hb, psum[:, 4, P:2 * P], sgate_e, ALU.mult).then_inc(bank_drained[4], 1)

                place(0, 0, 1)
                for t in range(2):
                    filled(dve, l, ("shgu", t))
                    signal(dve, l, "shared_silu", t + 1)
                    done(dve.tensor_tensor(sh_hb[:, t * DE:(t + 1) * DE], bank(("shgu", t))[:, DE:2 * DE], sgate[:, t, :],
                                           ALU.mult), ("shgu", t))
                filled(dve, l, ("shT",))
                done(dve.tensor_copy(sh_hbT, bank(("shT",)).rearrange("p (c n) -> p c n", c=2)), ("shT",))
                place(1, 0, 1)
                place_weights(0, 1)

                def dve_pairs(i, final=False):
                    for q in (1, 2):
                        more = not (final and q == 2)
                        gated(0, i, q)
                        if more:
                            place(0, i, q + 1)
                        gated(1, i, q)
                        if more:
                            place(1, i, q + 1)
                        step_filled(dve, l, "places", i, q)
                        dve.tensor_copy(placesT, psum[:, 7, 0:S]).then_inc(bank_drained[7], 1)
                        for j in range(2):
                            step_filled(dve, l, f"down{j}", i, q)
                            dve.tensor_copy(ybuf[:, j, :], psum[:, 4 + j, :]).then_inc(bank_drained[4 + j], 1)
                        if more:
                            place_weights(i, q + 1)

                dve_pairs(0)
                with dve.Fori(1, ROUNDS - 1) as i:
                    dve_pairs(i)
                dve_pairs(ROUNDS - 1, final=True)
                signal(dve, l, "spare_ready", 1)
                settle(dve)
                passes = dve.value_load(spare_count[0:1, 0:1], min_val=0, max_val=SPARE - 1)
                with dve.If(passes > 0):
                    with dve.Fori(0, passes) as n:
                        e = dve.value_load(spare_expert[0:1, bass.ds(n, 1)], min_val=0, max_val=NE - 1)
                        dve.wait_ge(pe_to_dve, n * 3 + 1)
                        for t in range(2):
                            link_clear(dve.tensor_scalar(spare_pos[:, t:t + 1], pos[:, t, bass.ds(e, 1)],
                                                         spare_rank[:, bass.ds(n, 1)], None, ALU.subtract))
                            dve.tensor_scalar(places[:, 0, t, :], iota[:, 0:SLOTS_E], spare_pos[:, t:t + 1], None, ALU.is_equal)
                            last = dve.tensor_scalar(places_w[:, t, :], iota[:], spare_pos[:, t:t + 1],
                                                     wts[:, t, bass.ds(e, 1)], ALU.is_equal, ALU.mult)
                        last.then_inc(dve_to_pe, 1)
                        dve.wait_ge(pe_to_dve, n * 3 + 2)
                        dve.tensor_copy(placesT, psum[:, 6, 0:S]).then_inc(dve_to_pe, 1)
                        dve.wait_ge(act_to_dve, n + 1)
                        dve.tensor_tensor(hb, psum[:, 4, P:2 * P], sgate_e, ALU.mult).then_inc(dve_to_pe, 1)
                        dve.wait_ge(pe_to_dve, n * 3 + 3)
                        dve.tensor_copy(ybuf[:, 0, :], psum[:, 5, :]).then_inc(dve_to_pe, 1)
                    dve.sem_clear(pe_to_dve)
                    dve.sem_clear(act_to_dve)
                for t in range(2):
                    for j in range(2):
                        key, part = ("y", t, j), slice(512 * j, 512 * j + 512)
                        filled(dve, l, key)
                        done(dve.tensor_tensor(h[:, t, part], bank(key), mixed[:, t, part], ALU.add), key)
                for t in range(2):
                    for j in range(2):
                        drained(dve, l, ("y", t, j))
                signal(dve, l, "ln2_loaded", 32)
                normalise(h[:], ln_g, ln_b, lambda ins: ins.then_inc(sems["var_ready"], 1),
                          lambda: signal(dve, l, "rstd_ready", 3), 12, lambda ins: ins.then_inc(sems["h_ready"], 1))
                end_chain()


NAMES = ["x", "p", "ln_in_g", "ln_in_b", "w_in", "gla_fg_w", "gla_fg_b", "gla_norm_g", "sg_norm_g", "sg_norm_b", "sg_w",
         "sg_b", "mla_qn_g", "mla_w_uq", "mla_kvn_g", "mla_w_ukv", "w_branch", "w_out", "ln1_g", "ln1_b", "router_w",
         "router_b", "exp_w_gate", "exp_w_up", "exp_w_down", "sh_w_gate", "sh_w_up", "sh_w_down", "ple_w_in",
         "ple_w_gate", "ln2_g", "ln2_b"]


def kernel(**inputs):
    import numpy as np
    import concourse.bacc as bacc
    from concourse.bass_utils import run_bass_kernel_spmd

    nc = bacc.Bacc("TRN2", target_bir_lowering=False, num_devices=1)
    arrays, weights = {}, {}

    def given(name, a):
        arrays[f"in_{name}"] = a
        return nc.dram_tensor(f"in_{name}", a.shape, mybir.dt.from_np(a.dtype), kind="ExternalInput").ap()

    for name in NAMES:
        weights[name] = given(name, np.ascontiguousarray(inputs[name]))
    inv = np.float32(10000.0) ** (-np.arange(HALF, dtype=np.float32) / np.float32(HALF))
    angle = np.arange(S, dtype=np.float32)[:, None] * inv
    cos_tab, sin_tab = given("cos", np.cos(angle).astype(np.float32)), given("sin", np.sin(angle).astype(np.float32))
    out = nc.dram_tensor("out_0", (1, S, D), F32, kind="ExternalOutput").ap()
    build_trunk(nc, weights, cos_tab, sin_tab, out)
    r = run_bass_kernel_spmd(nc, [arrays], core_ids=[0])
    return r.results[0]["out_0"]
```

```python
from contextlib import ExitStack

import concourse.bass as bass
from concourse import mybir

F32 = mybir.dt.float32
F32R = mybir.dt.float32r
I32 = mybir.dt.int32
BF16 = mybir.dt.bfloat16
ACT = mybir.ActivationFunctionType
ALU = mybir.AluOpType

P = 128
DEPTH = 2
S = 256
TILES = S // P
D = 1024
DC = D // P
CHUNK = 64
GH, GDK, GDV, GR = 4, 128, 256, 16
GATE_TAU = 16.0
SGW, SGG = 1024, 4
MH, QR, KVR, NOPE, ROPE, MV = 8, 384, 256, 128, 64, 128
QK = NOPE + ROPE
HALF = ROPE // 2
NE, NG, TOPG, TOPK, DE = 64, 8, 4, 8, 256
PLE = 256
ROUTED_SCALE = 2.5
ALPHA = (2 * DEPTH) ** 0.25
COL_GQ = 0
COL_GK = COL_GQ + GH * GDK
COL_GV = COL_GK + GH * GDK
COL_GR = COL_GV + GH * GDV
COL_GF = COL_GR + GH * GDV
COL_SG = COL_GF + GR
COL_MQ = COL_SG + 2 * SGW
COL_MKV = COL_MQ + QR
COL_GATE = COL_MKV + KVR + ROPE
SLOTS = 6
SLOT = 4096
BANKS = 8
SLOTS_E = 64
OVER, SPARE = S // SLOTS_E - 1, S * TOPK // SLOTS_E
LN_EPS, RMS_EPS = 1e-5, 1e-6
PARAMS = 8
LOW_FILL = -3.0e38
TAKEN = 3.0e38

JOBS = (
    [("hT", t, f) for t in range(2) for f in range(2)] + [("gfr",)]
    + [("fg", i) for i in range(2)] + [("q", i) for i in range(2)] + [("k", i) for i in range(2)]
    + [("v", j, t) for j in range(2) for t in range(2)] + [("gr", j, t) for j in range(2) for t in range(2)]
    + [("ke", t) for t in range(2)] + [("sgwT",)]
    + [x for h in range(GH + 1) for x in
       ([("att", h), ("ds", h, 0), ("ds", h, 1)] if h < GH else []) + ([("o", h - 1)] if h else [])]
    + [("sg", z, t) for z in range(2) for t in range(2)]
    + [("oaT", t, f) for t in range(2) for f in range(2)]
    + [("sg", z, t) for z in range(2, 4) for t in range(2)]
    + [("mq", t) for t in range(2)] + [("mkv", t) for t in range(2)]
    + [(kind, 0, 0, t) for kind in ("gate", "proj") for t in range(2)] + [("gate", 0, 1, t) for t in range(2)]
    + [("sv", t, i) for t in range(2) for i in range(2)] + [("proj", 0, 1, t) for t in range(2)]
    + [("obT", t, f) for t in range(2) for f in range(2)]
    + [("qnT", t) for t in range(2)] + [("ckT", t) for t in range(2)] + [("krT",)]
    + [(kind, 1, j, t) for j in range(2) for kind in ("gate", "proj") for t in range(2)]
    + [("qn", i) for i in range(4)] + [("qr", t) for t in range(2)]
    + [("kn", i) for i in range(4)] + [("vm", t, j) for t in range(2) for j in range(2)]
    + [("qrT", t) for t in range(2)]
    + [("s", 0)] + [x for h in range(MH + 2) for x in
       ([("s", h + 1)] if h < MH - 1 else []) + ([("pT", h - 1)] if 1 <= h <= MH else [])
       + ([("oc", h - 2)] if h >= 2 else [])]
    + [(kind, 2, 0, t) for kind in ("gate", "proj") for t in range(2)]
    + [("gate", 2, 1, t) for t in range(2)] + [("mT", 0, t) for t in range(2)] + [("proj", 2, 1, t) for t in range(2)]
    + [("ppT",)] + [("mT", 1, t) for t in range(2)]
    + [("wo", j, t) for j in range(2) for t in range(2)]
    + [("pli", j, t) for j in range(2) for t in range(2)]
    + [("hT2", t, f) for t in range(2) for f in range(2)]
    + [("rt", t) for t in range(2)]
    + [x for j in range(2) for x in [("plg", j, t) for t in range(2)] + ([("rank", 0), ("rank", 1)] if j == 0 else [])]
)
BANK, NTH, TOTAL = {}, {}, [0] * BANKS
for n_, key_ in enumerate(JOBS):
    BANK[key_] = n_ % BANKS
    TOTAL[n_ % BANKS] += 1
    NTH[key_] = TOTAL[n_ % BANKS]
PAIRS = NE // 2
STEP = {"gate_up0": (4, 3, -2), "gate_up1": (4, 3, -1), "down0": (4, 3, 0),
        "gather0": (5, 2, -2), "down1": (5, 2, 1), "gather1": (7, 1, 0),
        "hidden0": (6, 3, -2), "hidden1": (6, 3, -1), "places": (6, 3, 0)}
ROUNDS = NE // 4
GATHER_BANKS = [STEP[f"gather{a}"][0] for a in range(2)]
TURN_BANK = STEP["places"][0]
EXPERT_BASE = {b: TOTAL[b] for b in range(4, 8)}
for b_, jobs_ in {x[:2] for x in STEP.values()}:
    TOTAL[b_] += jobs_ * PAIRS
SHARED_AT = (5, 8, 11, 14)
SHARED_BANK = STEP["gather1"][0]
TOTAL[SHARED_BANK] += 3
for t_ in range(2):
    for j_ in range(2):
        b_ = 2 * t_ + j_
        TOTAL[b_] += 1
        BANK["y", t_, j_], NTH["y", t_, j_] = b_, TOTAL[b_]

USES = [("gf", ("gfr",)), ("gq", ("q", 1)), ("gk", ("k", 1)), ("gv0", ("v", 0, 1)), ("gv1", ("v", 1, 1)),
        ("gr0", ("gr", 0, 1)), ("gr1", ("gr", 1, 1)), ("sg0", ("sg", 0, 1)), ("sg1", ("sg", 1, 1)),
        ("sg2", ("sg", 2, 1)), ("sg3", ("sg", 3, 1)), ("mq", ("mq", 1)), ("mkv", ("mkv", 1))]
for n_ in range(3):
    if n_ == 2:
        USES += [("uq0", ("qr", 1)), ("uq1", ("qr", 1)), ("ukv", ("vm", 1, 1))]
    for j_ in range(2):
        USES += [(f"g{n_}{j_}", ("gate", n_, j_, 1)), (f"b{n_}{j_}", ("proj", n_, j_, 1))]
USES += [("wo0", ("wo", 0, 1)), ("wo1", ("wo", 1, 1))]
RAW = ("uq0", "uq1", "ukv")
SPLIT = [name for name, _ in USES if name not in RAW]
RING = 3
LOADS = [(name, n % RING, USES[n - RING][1] if n >= RING else None) for n, (name, _) in enumerate(USES)]
n_ = len(LOADS)
assert n_ % RING == 0 and SPLIT.index("wo0") % 2 == 1
LOADS += [("pli", 0, USES[-3][1]), ("plg0", 1, ("wo", 0, 1)), ("plg1", 2, ("wo", 1, 1))]
LAST_USE = [("pli", 1, 1), ("plg", 0, 1), ("plg", 1, 1), ("wo", 1, 1), ("wo", 0, 1), ("proj", 2, 1, 1)]
EXPERT_SLOTS = (5, 4, 3, 0, 1, 2)
SPARE_SLOTS = (5, 4)
POS = {name: slot for name, slot, _ in LOADS}
LANDED, SLOT_DMAS = {}, [0] * SLOTS
for name_, slot_, _ in LOADS:
    SLOT_DMAS[slot_] += 1
    LANDED[name_] = SLOT_DMAS[slot_]
TRUNK_DMAS = list(SLOT_DMAS)
EXPERT_DMAS = [2 if EXPERT_SLOTS.index(s) % 3 < 2 else 1 for s in range(SLOTS)]
SLOT_DMAS = [a + ROUNDS * b for a, b in zip(TRUNK_DMAS, EXPERT_DMAS)]


def build_trunk(nc, w, cos_tab, sin_tab, out):
    with ExitStack() as ctx:
        sb = lambda name, shape, dt=F32: ctx.enter_context(nc.sbuf_tensor(name, shape, dt))
        sem = lambda name: ctx.enter_context(nc.semaphore(name))

        def aligned():
            return -(-nc.sbuf_base // 32) * 32

        base = aligned()
        ring = sb("ring", [P, SLOTS, SLOT])
        slot_at = lambda n: base + 4 * SLOT * n
        at = lambda name, shape, dt, offset: nc.alloc_sbuf_tensor_at(name, shape, dt, offset=offset)
        weight_low = at("weight_low", [P, RING, SLOT], F32R, slot_at(0))
        weight_high = at("weight_high", [P, 2, SLOT], F32R, slot_at(RING))
        hT_low = at("hT_low", [P, DC, S], F32R, slot_at(5))
        bT_low = at("bT_low", [P, DC, S], F32R, slot_at(5) + 4 * DC * S)
        bT_whole = at("bT_whole", [P, DC, S], F32, slot_at(5) + 4 * DC * S)
        h = sb("h", [P, TILES, D])
        base_hT = aligned()
        hT = sb("hT", [P, DC, S])
        hT_high = at("hT_high", [P, DC, S], F32R, base_hT)
        base_bT = aligned()
        bT_high = sb("bT_high", [P, DC, S], F32R)
        shared_gate_weights = at("shared_gate_weights", [P, DC, DE], F32, base_bT)
        mixed = sb("mixed", [P, TILES, D])
        base_arena = aligned()
        arena = sb("arena", [P, 11520])
        mT_high = at("mT_high", [P, DC, S], F32R, base_arena + 4 * 8192)
        mT_low = at("mT_low", [P, DC, S], F32R, base_arena + 4 * 1024)
        ident = sb("ident", [P, P])
        gla_mask = sb("gla_mask", [P, TILES, P], I32)
        restart = sb("restart", [P, S])
        cos_t = sb("cos_t", [P, TILES, HALF])
        sin_t = sb("sin_t", [P, TILES, HALF])
        ln_g = sb("ln_g", [P, D])
        ln_b = sb("ln_b", [P, D])
        sgn = sb("sgn", [P, 2, SGW])
        sgn_g, sgn_b = sgn[:, 0, :], sgn[:, 1, :]
        shared_down_weights = sgn
        sgw = sb("sgw", [P, SGG, P])
        sgwT = sb("sgwT", [P, SGG, P])
        sgb = sb("sgb", [P, SGG])
        gsig = sb("gsig", [P, 2, 512])
        squares = gsig
        gfrT = sb("gfrT", [GR, S])
        fgw = sb("fgw", [GR, GH * GDK])
        fgb = sb("fgb", [P, GH])
        glag = sb("glag", [P, DC])
        qng = sb("qng", [P, QR // P])
        kvng = sb("kvng", [P, KVR // P])
        rbias = sb("rbias", [P, NE])
        ssq = sb("ssq", [P, 16])
        rstd = sb("rstd", [P, 16])
        neg_half = sb("neg_half", [P, 8])
        stats = sb("stats", [P, TILES, 2, 6])
        mv = sb("mv", [P, TILES, 2])
        decay = sb("decay", [P, GH, S // CHUNK])
        earlier = sb("earlier", [P, NG, NG])
        sm_top = sb("sm_top", [P, 2, 2])
        sm_max = sb("sm_max", [P, 2, 2])
        sm_sum = sb("sm_sum", [P, 2, 2])
        sm_inv = sb("sm_inv", [P, 2, 2])

        def carve(start, *shape):
            size = 1
            for x in shape:
                size *= x
            view = arena[:, start:start + size]
            if len(shape) == 2:
                view = view.rearrange("p (a b) -> p a b", a=shape[0])
            if len(shape) == 3:
                view = view.rearrange("p (a b c) -> p a b c", a=shape[0], b=shape[1])
            return view

        qd, ki, b_cum, tmp_e, keT = (carve(i * 1024, GH, S) for i in range(5))
        ke = carve(5 * 1024, TILES, GH * GDK)
        gv = carve(6144, TILES, GH * GDV)
        gr = carve(8192, TILES, GH * GDV)
        att = carve(10240, 2, TILES * P)
        state = carve(10752, 3, GDV)
        u = carve(0, TILES, SGW)
        vv = carve(2048, TILES, SGW)
        mq = carve(4096, TILES, QR)
        mkv = carve(4864, TILES, KVR + ROPE)
        qnT = carve(5504, QR // P, S)
        ckT = carve(6272, KVR // P, S)
        rtmp = carve(6784, 4, MH * HALF)
        krot = carve(7808, TILES, P)
        qnope = carve(8192, MH, S)
        qrT = carve(10240, 4, S)
        krT = carve(11264, S)
        knope = carve(0, MH, S)
        vm = carve(2048, TILES, MH * MV)
        prob = carve(6784, 2, 384)
        pT = carve(5120, 2, 384)
        qrot = carve(4096, 2, 512)
        regions = [(slice(CHUNK * i, CHUNK * i + CHUNK), P * t, P * t + CHUNK * (i + 1)) for t in range(2) for i in range(2)]
        pleT = carve(0, PLE // P, S)
        hb = carve(0, P)
        hbT = carve(256, 2, 2, SLOTS_E)
        ptok = carve(512, TILES, PLE)
        shared_gate = carve(512, TILES, DE)
        shared_hidden = carve(10752, TILES * DE)
        shared_hiddenT = gsig[:, 0, :].rearrange("p (c n) -> p c n", c=2)
        shared_up_weights = carve(7168, DC, DE)
        y_high = at("y_high", [P, 2, 512], F32R, base_arena + 4 * 1024)
        y_low = at("y_low", [P, 2, 512], F32R, base_arena + 4 * 2048)
        placesT = at("placesT", [P, S], F32R, base_arena + 4 * 10240)
        slot_weight = sb("slot_weight", [P, 1])
        score = carve(3072, TILES, NE)
        biased = carve(3200, TILES, NE)
        wts = carve(3328, TILES, NE)
        grp8 = carve(3456, NG, 8)
        gsum = carve(3520, NG)
        cmp = carve(3584, NG, NG)
        cmp2 = carve(3648, NG, NG)
        top8 = carve(3712, 8)
        rep = carve(3776, NE)
        wsum = carve(3840, 2)
        gkeep = carve(3856, NG)
        sel = carve(3904, TILES, NE)
        pos = sb("pos", [P, TILES, NE])
        iota = sb("iota", [P, 2 * SLOTS_E])
        before = sb("before", [P, P])
        ones = sb("ones", [P, P])
        spare_code = sb("spare_code", [P, OVER, NE])
        spare_key = carve(7168, OVER * NE)
        spare_top = sb("spare_top", [P, SPARE])
        spare_unit = sb("spare_unit", [P, SPARE], I32)
        spare_expert = sb("spare_expert", [P, SPARE], I32)
        spare_rank = sb("spare_rank", [P, SPARE])
        spare_pos = sb("spare_pos", [P, TILES])
        spare_sum = sb("spare_sum", [P, 1])
        spare_count = sb("spare_count", [P, 1], I32)
        parts = arena[:, 4096:7168].bitcast(BF16).rearrange("p (s t a i c) -> p s t a i c", s=3, t=2, a=2, i=4)
        rest = carve(7168, TILES, D)
        xgT = carve(9216, DC, 2 * SLOTS_E)
        places_w = carve(10496, TILES, 2 * SLOTS_E)
        places = arena[:, 11264:11392].bitcast(BF16).rearrange("p (t s) -> p t s", t=2)
        sgate_e = carve(11392, P)

        psum = ctx.enter_context(nc.psum_tensor("psum", [P, BANKS, 512], F32))

        bank_filled = [sem(f"bank_filled{b}") for b in range(BANKS)]
        bank_drained = [sem(f"bank_drained{b}") for b in range(BANKS)]
        x_loaded = [sem(f"x_loaded{t}") for t in range(TILES)]
        slot_loaded = [sem(f"slot_loaded{s}") for s in range(SLOTS)]
        names = dict(fg_loaded=32, params_loaded=16 * PARAMS, ln1_loaded=32, ln2_loaded=32, p_loaded=16,
                     router_loaded=16, h_ready=TILES, ln1_done=TILES, var_ready=3,
                     rstd_ready=3, ms_ready=GH + 2, rms_ready=GH + 2, sgw_masked=1, abs_ready=1, log_ready=1,
                     cum_ready=2, exp_ready=3, ke_ready=1, vln_ready=TILES, krot_ready=1, qrot_ready=2,
                     max_ready=MH, exp_p=MH, prob_ready=MH, silu_ready=NE, shared_silu=2, shared_loaded=48,
                     act_high=16, whole_ready=4, embedded=4, weight_rounded=len(SPLIT), weight_split=len(SPLIT),
                     places_ready=3 * PAIRS, score_taken=1, spare_ready=1)
        sems = {k: sem(k) for k in names}
        spare_loaded, spare_used, pe_to_dve, pe_to_act, act_to_pe, act_to_dve, dve_to_pe = (
            sem(f"spare_{k}") for k in ("loaded", "used", "pe_to_dve", "pe_to_act", "act_to_pe", "act_to_dve",
                                        "dve_to_pe"))
        dve_step = sem("dve_step")
        settled = {k: sem(f"settled_{k}") for k in ("SP", "Pool", "DVE", "PE", "Activation")}
        setup_done, ln_in_loaded, tables_loaded, dve_chain, act_chain, pool_chain, out_stored = (
            sem(k) for k in ("setup_done", "ln_in_loaded", "tables_loaded", "dve_chain",
                             "act_chain", "pool_chain", "out_stored"))

        def settle(eng):
            eng.sem_inc(settled[eng.engine.name], 1)

        def filled(eng, l, key, more=0):
            b = BANK[key]
            eng.wait_ge(bank_filled[b], l * TOTAL[b] + (NTH[key] + more))

        def drained(eng, l, key, before=False):
            b = BANK[key]
            n = NTH[key] - before
            if n > 0:
                eng.wait_ge(bank_drained[b], l * TOTAL[b] + (n - TOTAL[b]))

        def signal(eng, l, name, n):
            eng.wait_ge(sems[name], l * names[name] + (n - names[name]))

        def loaded(eng, l, name):
            s = POS[name]
            eng.wait_ge(slot_loaded[s], l * (16 * SLOT_DMAS[s]) + 16 * (LANDED[name] - SLOT_DMAS[s]))

        def high_slot(name, chunks, cols):
            return weight_high[:, SPLIT.index(name) % 2, 0:chunks * cols].rearrange("p (c n) -> p c n", c=chunks)

        def low_slot(name, chunks, cols):
            return weight_low[:, POS[name], 0:chunks * cols].rearrange("p (c n) -> p c n", c=chunks)

        def used_columns(name):
            return DC * {"gf": P, "mq": QR, "mkv": KVR + ROPE}.get(name, 512)

        def step_count(what, i, q):
            b, per, more = STEP[what]
            if isinstance(i, int):
                more = {("gather0", 1): -1, ("down1", PAIRS): 0}.get((what, 2 * i + q), more)
            return b, per * (PAIRS // ROUNDS), per * q + more

        passed = {}

        def segments(eng, rounds, shared_job):
            passed[eng] = 0
            rounds(0, first=True)
            start = 1
            for n, stop in enumerate(SHARED_AT + (ROUNDS - 1,)):
                with eng.Fori(start, stop) as i:
                    rounds(i)
                start = stop
                if n < len(SHARED_AT):
                    shared_job(n)
                    passed[eng] = min(n + 1, 3)
            rounds(ROUNDS - 1, final=True)

        def shared_number(l, n, semaphore_lag):
            return l * TOTAL[SHARED_BANK] + (EXPERT_BASE[SHARED_BANK] + 2 * SHARED_AT[n] + n + 2 - semaphore_lag)

        def shared_filled(eng, l, n):
            eng.wait_ge(bank_filled[SHARED_BANK], shared_number(l, n, 0))

        def shared_drained(eng, l, n, before=False):
            eng.wait_ge(bank_drained[SHARED_BANK], shared_number(l, n, TOTAL[SHARED_BANK] + before))

        def step_filled(eng, l, what, i, q):
            b, per, n = step_count(what, i, q)
            n += passed.get(eng, 0) * (b == SHARED_BANK)
            eng.wait_ge(bank_filled[b], l * TOTAL[b] + (i * per + (EXPERT_BASE[b] + n)))

        def step_drained(eng, l, what, i, q, before=False):
            b, per, n = step_count(what, i, q)
            n += passed.get(eng, 0) * (b == SHARED_BANK)
            eng.wait_ge(bank_drained[b], l * TOTAL[b] + (i * per + (EXPERT_BASE[b] + n - before - TOTAL[b])))

        def expert_slot_free(eng, l, i, s):
            n = EXPERT_SLOTS.index(s)
            step_filled(eng, l, ("gate_up0", "gate_up1", "down1")[n % 3], i, n // 3 + 1)

        router = carve(10752, DC, NE)

        def slot(name, chunks, cols):
            return ring[:, POS[name], 0:chunks * cols].rearrange("p (c n) -> p c n", c=chunks)

        def bank(key):
            return psum[:, BANK[key], :]

        def layer_of(name, l):
            return w[name][bass.ds(l - 1, 1)]

        block = ctx.enter_context(nc.Block())

        @block.sync
        def _(sp):
            def cols(l, a, n):
                return layer_of("w_in", l).rearrange("o (p c) n -> p (o c) n", c=DC)[:, :, a:a + n]

            def source(name, l):
                if name == "gf":
                    return [(slot(name, DC, P), cols(l, COL_GF, P))]
                if name == "gq":
                    return [(slot(name, DC, 512), cols(l, COL_GQ, 512))]
                if name == "gk":
                    return [(slot(name, DC, 512), cols(l, COL_GK, 512))]
                if name[:2] in ("gv", "gr", "sg"):
                    a = {"gv": COL_GV, "gr": COL_GR, "sg": COL_SG}[name[:2]] + 512 * int(name[2])
                    return [(slot(name, DC, 512), cols(l, a, 512))]
                if name == "mq":
                    return [(slot(name, DC, QR), cols(l, COL_MQ, QR))]
                if name == "mkv":
                    return [(slot(name, DC, KVR + ROPE), cols(l, COL_MKV, KVR + ROPE))]
                if name[0] == "g":
                    a = COL_GATE + int(name[1]) * D + 512 * int(name[2])
                    return [(slot(name, DC, 512), cols(l, a, 512))]
                if name[0] == "b":
                    n, j = int(name[1]), int(name[2])
                    src = w["w_branch"][bass.ds(l - 1, 1), n].rearrange("o (c p) n -> p (o c) n", p=P)
                    return [(slot(name, DC, 512), src[:, :, 512 * j:512 * j + 512])]
                if name[:2] == "uq":
                    j, n = int(name[2]), MH * QK // 2
                    src = layer_of("mla_w_uq", l).rearrange("o (c p) n -> p (o c) n", p=P)
                    return [(slot(name, QR // P, n), src[:, :, n * j:n * (j + 1)])]
                if name == "ukv":
                    return [(slot(name, 2, 2048), layer_of("mla_w_ukv", l).rearrange("o (c p) n -> p (o c) n", p=P))]
                if name[:2] == "wo":
                    j = int(name[2])
                    src = layer_of("w_out", l).rearrange("o (c p) n -> p (o c) n", p=P)
                    return [(slot(name, DC, 512), src[:, :, 512 * j:512 * j + 512])]
                if name == "pli":
                    return [(slot(name, 2, D), layer_of("ple_w_in", l).rearrange("o (c p) n -> p (o c) n", p=P))]
                j = int(name[3])
                src = layer_of("ple_w_gate", l).rearrange("o (p c) n -> p (o c) n", c=DC)
                return [(slot(name, DC, 512), src[:, :, 512 * j:512 * j + 512])]

            def expert_load(l, i, n):
                s, e = EXPERT_SLOTS[n], 4 * i + 2 * (n // 3)
                if n % 3 < 2:
                    for k, name in enumerate(("exp_w_gate", "exp_w_up")):
                        src = w[name][bass.ds(l - 1, 1), bass.ds(e + n % 3, 1)].rearrange("o e (p c) n -> p (o e c n)", c=DC)
                        sp.dma_start(ring[:, s, 2048 * k:2048 * k + 2048], src).then_inc(slot_loaded[s], 16)
                else:
                    src = w["exp_w_down"][bass.ds(l - 1, 1), bass.ds(e, 2)].rearrange("o e (c p) n -> p (o e c) n", c=2)
                    sp.dma_start(ring[:, s, :].rearrange("p (e n) -> p e n", e=4), src).then_inc(slot_loaded[s], 16)

            for t in range(TILES):
                sp.dma_start(h[:, t, :], w["x"][:, t * P:t * P + P, :].rearrange("b p d -> p (b d)")
                             ).then_inc(x_loaded[t], 16)
            sp.dma_start(ln_g[:], w["ln_in_g"].partition_broadcast(P)).then_inc(ln_in_loaded, 16)
            sp.dma_start(ln_b[:], w["ln_in_b"].partition_broadcast(P)).then_inc(ln_in_loaded, 16)
            with sp.Fori(1, DEPTH + 1) as l:

                def shared_load(dst, name, c):
                    sp.dma_start(dst, layer_of(name, l).rearrange("o (p c) n -> p (o c) n", c=c)
                                 ).then_inc(sems["shared_loaded"], 16)

                def first_expert_load(n):
                    filled(sp, l, LAST_USE[EXPERT_SLOTS[n]])
                    settle(sp)
                    expert_load(l, 0, n)

                for name, s, free_after in LOADS:
                    if free_after is None:
                        expert_slot_free(sp, l - 1, ROUNDS - 1, s)
                    else:
                        filled(sp, l, free_after)
                    settle(sp)
                    for dst, src in source(name, l):
                        sp.dma_start(dst, src).then_inc(slot_loaded[s], 16)
                    if name == "pli":
                        sp.dma_start(router, layer_of("router_w", l).rearrange("o (p c) n -> p (o c) n", c=DC)
                                     ).then_inc(sems["router_loaded"], 16)
                        first_expert_load(0)
                        shared_load(shared_gate_weights[:], "sh_w_gate", DC)
                        shared_load(shared_down_weights[:], "sh_w_down", 2)
                for n in range(1, SLOTS):
                    first_expert_load(n)
                signal(sp, l, "spare_ready", 1)
                settle(sp)
                shared_load(shared_up_weights, "sh_w_up", DC)
                with sp.Fori(1, ROUNDS) as i:
                    for n, s in enumerate(EXPERT_SLOTS):
                        expert_slot_free(sp, l, i - 1, s)
                        settle(sp)
                        expert_load(l, i, n)
                passes = sp.value_load(spare_count[0:1, 0:1], min_val=0, max_val=SPARE - 1)
                with sp.If(passes > 0):
                    for s in SPARE_SLOTS:
                        expert_slot_free(sp, l, ROUNDS - 1, s)
                        settle(sp)
                    with sp.Fori(0, passes) as n:
                        e = sp.value_load(spare_expert[0:1, bass.ds(n, 1)], min_val=0, max_val=NE - 1)
                        for k, name in enumerate(("exp_w_gate", "exp_w_up")):
                            src = w[name][bass.ds(l - 1, 1), bass.ds(e, 1)].rearrange("o e (p c) n -> p (o e c n)", c=DC)
                            sp.dma_start(ring[:, SPARE_SLOTS[0], 2048 * k:2048 * k + 2048], src).then_inc(spare_loaded, 16)
                        src = w["exp_w_down"][bass.ds(l - 1, 1), bass.ds(e, 1)].rearrange("o e (c p) n -> p (o e c) n", p=P)
                        sp.dma_start(ring[:, SPARE_SLOTS[1], 0:2048].rearrange("p (c n) -> p c n", c=2),
                                     src).then_inc(spare_loaded, 16)
                        sp.wait_ge(spare_used, n + 1)
                        settle(sp)
                    sp.sem_clear(spare_used)
            for t in range(TILES):
                sp.wait_ge(sems["h_ready"], TILES * DEPTH + t + 1)
                sp.dma_start(out[:, t * P:t * P + P, :].rearrange("b p d -> p (b d)"), h[:, t, :]).then_inc(out_stored, 16)
            sp.wait_ge(out_stored, 16 * TILES)

        @block.gpsimd
        def _(pool):
            chain = [0]

            def link(ins):
                chain[0] += 1
                ins.then_inc(pool_chain, 1)
                pool.wait_ge(pool_chain, chain[0])

            pool.dma_start(cos_t[:], cos_tab.rearrange("(t p) i -> p t i", p=P)).then_inc(tables_loaded, 16)
            pool.dma_start(sin_t[:], sin_tab.rearrange("(t p) i -> p t i", p=P)).then_inc(tables_loaded, 16)
            link(pool.memset(neg_half[:], -0.5))
            link(pool.memset(ident[:], 0.0))
            link(pool.affine_select(out=ident[:], in_=ident[:], compare_op=ALU.not_equal, fill=1.0, base=0,
                                    pattern=[[-1, P]], channel_multiplier=1))
            link(pool.memset(gla_mask[:], 1))
            link(pool.affine_select(out=gla_mask[:], in_=gla_mask[:], compare_op=ALU.is_ge, fill=0.0, base=0,
                                    pattern=[[0, TILES], [1, P]], channel_multiplier=-1))
            right = gla_mask[:, :, CHUNK:P]
            link(pool.affine_select(out=right, in_=right, compare_op=ALU.is_ge, fill=0.0, base=-CHUNK,
                                    pattern=[[0, TILES], [0, P - CHUNK]], channel_multiplier=1))
            link(pool.memset(restart[:], 1.0))
            link(pool.memset(restart[:, 0:S:CHUNK], 0.0))
            link(pool.memset(earlier[:], 1.0))
            link(pool.affine_select(out=earlier[:], in_=earlier[:], compare_op=ALU.is_gt, fill=0.0, base=0,
                                    pattern=[[1, NG], [-1, NG]], channel_multiplier=0))
            link(pool.memset(ones[:], 1.0))
            link(pool.affine_select(out=before[:], in_=ones[:], compare_op=ALU.is_gt, fill=0.0, base=0,
                                    pattern=[[1, P]], channel_multiplier=-1))
            link(pool.iota(spare_code[:], pattern=[[-NE, OVER], [-1, NE]], base=256, channel_multiplier=0,
                           allow_small_or_imprecise_dtypes=True))
            pool.iota(iota[:], pattern=[[0, 2], [1, SLOTS_E]], base=0, channel_multiplier=0,
                      allow_small_or_imprecise_dtypes=True).then_inc(setup_done, 1)

            def rsqrt(x):
                return pool.tensor_tensor(x, x, neg_half[:, 0:2], ALU.pow)

            with pool.Fori(1, DEPTH + 1) as l:
                signal(pool, l, "var_ready", 1)
                rsqrt(rstd[:, 12:14]).then_inc(sems["rstd_ready"], 1)

                def small(dst, src):
                    pool.dma_start(dst, src).then_inc(sems["params_loaded"], 16)

                row = lambda name: layer_of(name, l).partition_broadcast(P).rearrange("p o n -> p (o n)")
                with nc.allow_non_contiguous_dma(reason="per-channel vectors onto partitions"):
                    pool.dma_start(fgw[:], layer_of("gla_fg_w", l).rearrange("o r n -> r (o n)")
                                   ).then_inc(sems["fg_loaded"], 16)
                    pool.dma_start(fgb[:], layer_of("gla_fg_b", l).rearrange("o (c p) -> p (o c)", p=P)
                                   ).then_inc(sems["fg_loaded"], 16)
                    small(glag[:], layer_of("gla_norm_g", l).rearrange("o (c p) -> p (o c)", p=P))
                    small(qng[:], layer_of("mla_qn_g", l).rearrange("o (c p) -> p (o c)", p=P))
                    small(kvng[:], layer_of("mla_kvn_g", l).rearrange("o (c p) -> p (o c)", p=P))
                    small(sgb[:], layer_of("sg_b", l).rearrange("o g t -> t (o g)"))
                small(sgw[:], layer_of("sg_w", l).rearrange("o g t s -> t (o g) s"))
                small(sgn_g, row("sg_norm_g"))
                small(sgn_b, row("sg_norm_b"))
                small(rbias[:], row("router_b"))
                signal(pool, l, "h_ready", TILES)
                settle(pool)
                pool.dma_start(ln_g[:], row("ln1_g")).then_inc(sems["ln1_loaded"], 16)
                pool.dma_start(ln_b[:], row("ln1_b")).then_inc(sems["ln1_loaded"], 16)
                pool.wait_ge(sems["params_loaded"], l * (16 * PARAMS))
                settle(pool)
                pool.affine_select(out=sgw[:], in_=sgw[:], compare_op=ALU.is_ge, fill=0.0, base=0,
                                   pattern=[[0, SGG], [-1, P]], channel_multiplier=1).then_inc(sems["sgw_masked"], 1)
                for i in range(GH):
                    signal(pool, l, "ms_ready", i + 1)
                    rsqrt(rstd[:, 2 * i:2 * i + 2]).then_inc(sems["rms_ready"], 1)
                for i in range(2):
                    signal(pool, l, "ms_ready", GH + i + 1)
                    rsqrt(rstd[:, 8 + 2 * i:10 + 2 * i]).then_inc(sems["rms_ready"], 1)
                signal(pool, l, "var_ready", 2)
                rsqrt(rstd[:, 12:14]).then_inc(sems["rstd_ready"], 1)
                filled(pool, l, ("s", MH - 1))
                settle(pool)
                pool.dma_start(ptok, w["p"][bass.ds(l - 1, 1)].rearrange("l b (t p) d -> p (l b t) d", p=P)
                               ).then_inc(sems["p_loaded"], 16)
                signal(pool, l, "var_ready", 3)
                rsqrt(rstd[:, 12:14]).then_inc(sems["rstd_ready"], 1)
                signal(pool, l, "ln1_done", TILES)
                settle(pool)
                pool.dma_start(ln_g[:], row("ln2_g")).then_inc(sems["ln2_loaded"], 16)
                pool.dma_start(ln_b[:], row("ln2_b")).then_inc(sems["ln2_loaded"], 16)
            pool.wait_ge(sems["var_ready"], 3 * DEPTH + 1)
            rsqrt(rstd[:, 12:14]).then_inc(sems["rstd_ready"], 1)

        @block.tensor
        def _(pe):
            for b in range(BANKS):
                pe.sem_inc(bank_filled[b], TOTAL[b])
            pe.wait_ge(setup_done, 1)

            def rows(t):
                return slice(t * P, t * P + P)

            with pe.Fori(1, DEPTH + 1) as l:

                def transposes(key, tiles):
                    drained(pe, l, key, before=True)
                    for i, x in enumerate(tiles):
                        last = pe.transpose(bank(key)[:, i * P:i * P + P], x, ident[:])
                    last.then_inc(bank_filled[BANK[key]], 1)

                def by_token(key, src, t, left, cols, chunks=DC):
                    drained(pe, l, key, before=True)
                    for c in range(chunks):
                        last = pe.matmul(bank(key)[:, 0:cols], left[:, c, rows(t)], src[:, c, :],
                                         start=c == 0, stop=c == chunks - 1)
                    last.then_inc(bank_filled[BANK[key]], 1)

                def by_token_split(key, name, t, left, cols, middle=lambda: None):
                    drained(pe, l, key, before=True)
                    high, low = high_slot(name, DC, cols), low_slot(name, DC, cols)
                    for c in range(DC):
                        if c == DC // 2:
                            middle()
                        for n, (x, y) in enumerate(((left[0], high), (left[0], low), (left[1], high))):
                            last = pe.matmul(bank(key)[:, 0:cols], x[:, c, rows(t)], y[:, c, :],
                                             start=c + n == 0, stop=(c, n) == (DC - 1, 2))
                    last.then_inc(bank_filled[BANK[key]], 1)

                def by_channel_split(key, name, blocks, right):
                    drained(pe, l, key, before=True)
                    cols = used_columns(name) // DC
                    high, low = high_slot(name, DC, cols), low_slot(name, DC, cols)
                    for i, b in enumerate(blocks):
                        part = slice(b * P, (b + 1) * P)
                        for c in range(DC):
                            for n, (x, y) in enumerate(((high, right[0]), (high, right[1]), (low, right[0]))):
                                last = pe.matmul(bank(key)[:, i * S:i * S + S], x[:, c, part], y[:, c, :],
                                                 start=c + n == 0, stop=(c, n) == (DC - 1, 2))
                    last.then_inc(bank_filled[BANK[key]], 1)

                def weights_split(name):
                    signal(pe, l, "weight_split", SPLIT.index(name) + 1)

                hT_parts, bT_parts, mT_parts = (hT_high, hT_low), (bT_high, bT_low), (mT_high, mT_low)

                def by_channel(key, stationary, right, m=P):
                    drained(pe, l, key, before=True)
                    for i, blocks in enumerate(stationary):
                        for c, x in enumerate(blocks):
                            last = pe.matmul(bank(key)[0:m, i * S:i * S + S], x, right[:, c, :],
                                             start=c == 0, stop=c == len(blocks) - 1)
                    last.then_inc(bank_filled[BANK[key]], 1)

                for t in range(2):
                    signal(pe, l, "h_ready", t + 1)
                    for f in range(2):
                        transposes(("hT", t, f), [h[:, t, 4 * f + i:D:DC] for i in range(4)])
                for t in range(2):
                    for f in range(2):
                        drained(pe, l, ("hT", t, f))
                weights_split("gf")
                by_channel_split(("gfr",), "gf", [0], hT_parts)
                signal(pe, l, "fg_loaded", 32)
                drained(pe, l, ("gfr",))
                for i in range(2):
                    drained(pe, l, ("fg", i), before=True)
                    for n in range(2):
                        last = pe.matmul(bank(("fg", i))[:, n * S:n * S + S], fgw[:, (2 * i + n) * P:(2 * i + n + 1) * P],
                                         gfrT[:], start=True, stop=True)
                    last.then_inc(bank_filled[BANK["fg", i]], 1)
                for kind, name in (("q", "gq"), ("k", "gk")):
                    weights_split(name)
                    for i in range(2):
                        by_channel_split((kind, i), name, [2 * i, 2 * i + 1], hT_parts)
                for kind, name in (("v", "gv"), ("gr", "gr")):
                    for j in range(2):
                        weights_split(f"{name}{j}")
                        for t in range(2):
                            by_token_split((kind, j, t), f"{name}{j}", t, hT_parts, 512)
                signal(pe, l, "ke_ready", 1)
                for t in range(2):
                    transposes(("ke", t), [keT[:, n, rows(t)] for n in range(GH)])
                signal(pe, l, "sgw_masked", 1)
                transposes(("sgwT",), [sgw[:, g, :] for g in range(SGG)])
                for j in range(2):
                    for t in range(2):
                        drained(pe, l, ("v", j, t))
                for t in range(2):
                    drained(pe, l, ("ke", t))
                for n in range(GH + 1):
                    if n < GH:
                        key = ("att", n)
                        drained(pe, l, key, before=True)
                        for t in range(2):
                            last = pe.matmul(bank(key)[:, rows(t)], ki[:, n, rows(t)], qd[:, n, rows(t)],
                                             start=True, stop=True)
                        last.then_inc(bank_filled[BANK[key]], 1)
                        for c in (0, 2, 1):
                            key = ("ds", n, c % 2)
                            if c < 2:
                                drained(pe, l, key, before=True)
                            part = slice(CHUNK * (c % 2), CHUNK * (c % 2) + CHUNK)
                            last = pe.matmul(bank(key)[:, GDV * (c // 2):GDV * (c // 2) + GDV],
                                             ke[part, c // 2, n * P:n * P + P], gv[part, c // 2, n * GDV:(n + 1) * GDV],
                                             start=True, stop=True)
                            if c:
                                last.then_inc(bank_filled[BANK[key]], 1)
                    if n:
                        key, m = ("o", n - 1), n - 1
                        drained(pe, l, key, before=True)
                        drained(pe, l, ("att", m))
                        drained(pe, l, ("ds", m, 0))
                        for c in range(S // CHUNK):
                            t, queries = c // 2, slice(CHUNK * c, CHUNK * c + CHUNK)
                            o = bank(key)[CHUNK * (c % 2):CHUNK * (c % 2) + CHUNK, t * GDV:(t + 1) * GDV]
                            last = pe.matmul(o, att[:, m % 2, queries], gv[:, t, m * GDV:(m + 1) * GDV],
                                             start=True, stop=c == 0)
                            if c:
                                last = pe.matmul(o, qd[:, m, queries], state[:, c - 1, :], start=False, stop=True)
                        last.then_inc(bank_filled[BANK[key]], 1)
                for z in range(4):
                    if z == 2:
                        drained(pe, l, ("o", GH - 1))
                        for t in range(2):
                            for f in range(2):
                                transposes(("oaT", t, f), [gr[:, t, (4 * f + i) * P:(4 * f + i + 1) * P] for i in range(4)])
                    weights_split(f"sg{z}")
                    for t in range(2):
                        by_token_split(("sg", z, t), f"sg{z}", t, hT_parts, 512)
                for kind, n in (("mq", QR), ("mkv", KVR + ROPE)):
                    weights_split(kind)
                    for t in range(2):
                        by_token_split((kind, t), kind, t, hT_parts, n)

                def branch(kind, n, j):
                    name = f"{'g' if kind == 'gate' else 'b'}{n}{j}"
                    weights_split(name)
                    for t in range(2):
                        by_token_split((kind, n, j, t), name, t, hT_parts if kind == "gate" else bT_parts, 512)

                branch("gate", 0, 0)
                for t in range(2):
                    for f in range(2):
                        drained(pe, l, ("oaT", t, f))
                branch("proj", 0, 0)
                branch("gate", 0, 1)
                drained(pe, l, ("sgwT",))
                signal(pe, l, "vln_ready", TILES)
                for t in range(2):
                    for i in range(2):
                        key = ("sv", t, i)
                        drained(pe, l, key, before=True)
                        for n in range(2):
                            g = 2 * i + n
                            last = pe.matmul(bank(key)[:, n * 256:n * 256 + 256], sgwT[:, g, :],
                                             vv[:, t, g * 256:g * 256 + 256], start=True, stop=True)
                        last.then_inc(bank_filled[BANK[key]], 1)
                branch("proj", 0, 1)
                for t in range(2):
                    for i in range(2):
                        drained(pe, l, ("sv", t, i))
                    for f in range(2):
                        transposes(("obT", t, f), [u[:, t, (4 * f + i) * P:(4 * f + i + 1) * P] for i in range(4)])
                for t in range(2):
                    drained(pe, l, ("mq", t))
                    transposes(("qnT", t), [mq[:, t, c * P:c * P + P] for c in range(QR // P)])
                for t in range(2):
                    drained(pe, l, ("mkv", t))
                    transposes(("ckT", t), [mkv[:, t, c * P:c * P + P] for c in range(KVR // P)])
                signal(pe, l, "krot_ready", 1)
                transposes(("krT",), [krot[:, t, :] for t in range(2)])
                branch("gate", 1, 0)
                for t in range(2):
                    for f in range(2):
                        drained(pe, l, ("obT", t, f))
                branch("proj", 1, 0)
                branch("gate", 1, 1)
                branch("proj", 1, 1)
                loaded(pe, l, "uq0")
                uq = [slot(f"uq{j}", QR // P, MH * QK // 2).rearrange("p c (h n) -> p c h n", h=MH // 2) for j in range(2)]
                for t in range(2):
                    drained(pe, l, ("qnT", t))
                    drained(pe, l, ("ckT", t))
                drained(pe, l, ("krT",))
                for i in range(4):
                    if i == 2:
                        loaded(pe, l, "uq1")
                    by_channel(("qn", i), [[uq[i // 2][:, c, 2 * (i % 2) + n, 0:NOPE] for c in range(3)]
                                           for n in range(2)], qnT)
                for t in range(2):
                    key = ("qr", t)
                    drained(pe, l, key, before=True)
                    for j in range(2):
                        for c in range(3):
                            last = pe.matmul(bank(key)[:, 256 * j:256 * j + 256], qnT[:, c, rows(t)],
                                             uq[j][:, c, :, NOPE:QK], start=c == 0, stop=c == 2)
                    last.then_inc(bank_filled[BANK[key]], 1)
                loaded(pe, l, "ukv")
                ukv = slot("ukv", 2, 2048).rearrange("p c (h n) -> p c h n", h=MH)
                for i in range(4):
                    by_channel(("kn", i), [[ukv[:, c, 2 * i + n, 0:NOPE] for c in range(2)] for n in range(2)], ckT)
                for t in range(2):
                    for j in range(2):
                        key = ("vm", t, j)
                        drained(pe, l, key, before=True)
                        for c in range(2):
                            last = pe.matmul(bank(key), ckT[:, c, rows(t)], ukv[:, c, 4 * j:4 * j + 4, NOPE:NOPE + MV],
                                             start=c == 0, stop=c == 1)
                        last.then_inc(bank_filled[BANK[key]], 1)
                for t in range(2):
                    signal(pe, l, "qrot_ready", t + 1)
                    transposes(("qrT", t), [qrot[:, t, i * P:i * P + P] for i in range(4)])
                for i in range(4):
                    drained(pe, l, ("qn", i))
                    drained(pe, l, ("kn", i))
                for t in range(2):
                    drained(pe, l, ("qrT", t))
                    for j in range(2):
                        drained(pe, l, ("vm", t, j))
                def scores(n):
                    key = ("s", n)
                    drained(pe, l, key, before=True)
                    part = slice(ROPE * (n % 2), ROPE * (n % 2) + ROPE)
                    for t in range(2):
                        o, keys = bank(key)[:, P * t:P * t + P * (t + 1)], P * (t + 1)
                        pe.matmul(o, qnope[:, n, rows(t)], knope[:, n, 0:keys], start=True, stop=False)
                        last = pe.matmul(o, qrT[part, n // 2, rows(t)], krT[part, 0:keys], start=False, stop=True)
                    last.then_inc(bank_filled[BANK[key]], 1)

                scores(0)
                for n in range(MH + 2):
                    if n < MH - 1:
                        scores(n + 1)
                    if 1 <= n <= MH:
                        signal(pe, l, "prob_ready", n)
                        m = (n - 1) % 2
                        transposes(("pT", n - 1), [prob[:, m, 0:128], prob[:, m, 128:256], prob[:, m, 256:384]])
                    if n >= 2:
                        key, m = ("oc", n - 2), n - 2
                        drained(pe, l, key, before=True)
                        drained(pe, l, ("pT", m))
                        pe.matmul(bank(key)[:, 0:S], vm[:, 0, m * MV:(m + 1) * MV], pT[:, m % 2, 0:S], start=True, stop=False)
                        pe.matmul(bank(key)[:, P:S], vm[:, 1, m * MV:(m + 1) * MV], pT[:, m % 2, S:S + P],
                                  start=False, stop=True).then_inc(bank_filled[BANK[key]], 1)
                branch("gate", 2, 0)
                for n in range(MH):
                    drained(pe, l, ("oc", n))
                branch("proj", 2, 0)
                branch("gate", 2, 1)

                def merged_turned(j):
                    for t in range(2):
                        drained(pe, l, ("proj", 2, j, t))
                        transposes(("mT", j, t), [mixed[:, t, (4 * j + i) * P:(4 * j + i + 1) * P] for i in range(4)])

                merged_turned(0)
                branch("proj", 2, 1)
                signal(pe, l, "p_loaded", 16)
                transposes(("ppT",), [ptok[:, t, c * P:c * P + P] for c in range(2) for t in range(2)])
                merged_turned(1)
                for j in range(2):
                    weights_split(f"wo{j}")
                    for t in range(2):
                        if j == 0:
                            drained(pe, l, ("mT", 0, t))
                        by_token_split(("wo", j, t), f"wo{j}", t, mT_parts, 512,
                                       middle=lambda: drained(pe, l, ("mT", 1, t)) if j == 0 else None)
                drained(pe, l, ("ppT",))
                loaded(pe, l, "pli")
                for j in range(2):
                    for t in range(2):
                        by_token(("pli", j, t), slot("pli", 2, D)[:, :, 512 * j:512 * j + 512], t, pleT, 512, chunks=2)
                for t in range(2):
                    signal(pe, l, "ln1_done", t + 1)
                    for f in range(2):
                        transposes(("hT2", t, f), [h[:, t, 4 * f + i:D:DC] for i in range(4)])
                for t in range(2):
                    for f in range(2):
                        drained(pe, l, ("hT2", t, f))
                signal(pe, l, "router_loaded", 16)
                for t in range(2):
                    by_token(("rt", t), router, t, hT, NE)
                for j in range(2):
                    loaded(pe, l, f"plg{j}")
                    for t in range(2):
                        by_token(("plg", j, t), slot(f"plg{j}", DC, 512), t, hT, 512)
                    if j == 0:
                        for t in range(2):
                            key = ("rank", t)
                            signal(pe, l, "score_taken", 1)
                            drained(pe, l, key, before=True)
                            if t:
                                pe.matmul(bank(key)[:, 0:NE], ones[:], sel[:, 0, :], start=True, stop=False)
                            last = pe.matmul(bank(key)[:, 0:NE], before[:], sel[:, t, :], start=t == 0, stop=True)
                            if t:
                                for n in range(2):
                                    last = pe.matmul(bank(key)[:, NE:2 * NE], ones[:], sel[:, n, :], start=n == 0, stop=n == 1)
                            last.then_inc(bank_filled[BANK[key]], 1)

                halves = [slice(SLOTS_E * a, SLOTS_E * (a + 1)) for a in range(2)]

                def mm_gather(b, a, n):
                    for i in range(4):
                        for t in range(2):
                            for part in range(3):
                                last = pe.matmul(psum[:, b, i * P:i * P + n], parts[:, part, t, a, i, :],
                                                 places[:, t, 0:n], start=(t, part) == (0, 0), stop=(t, part) == (1, 2))
                    return last

                def mm_gate_up(s, e):
                    src = ring[:, s, :].rearrange("p (g c n) -> p g c n", g=2, c=DC)
                    for c in range(DC):
                        for a in range(2):
                            last = pe.matmul(psum[halves[a], 4, 0:2 * P], xgT[:, c, halves[e]],
                                             src[:, :, c, a * P:(a + 1) * P], start=c == 0, stop=c == DC - 1)
                    return last

                def mm_down(b, j, s):
                    weights = ring[:, s, :].rearrange("p (e c n) -> p e c n", e=2, c=2)
                    for c in range(2):
                        for e in range(2):
                            last = pe.matmul(psum[halves[e], b, :], hbT[:, e, c, :],
                                             weights[:, e, c, 512 * j:512 * j + 512], start=c == 0, stop=c == 1)
                    return last

                def gather(i, q):
                    pe.wait_ge(sems["places_ready"], l * (3 * PAIRS) + (i * 6 + (3 * q - 1 - 3 * PAIRS)))
                    for a in range(2):
                        step_drained(pe, l, f"gather{a}", i, q, before=True)
                        mm_gather(GATHER_BANKS[a], a, 2 * SLOTS_E).then_inc(bank_filled[GATHER_BANKS[a]], 1)

                def gate_up(e, i, q, s):
                    if e == 0:
                        step_drained(pe, l, "gather0", i, q)
                        step_drained(pe, l, "gather1", i, q)
                    step_drained(pe, l, f"gate_up{e}", i, q, before=True)
                    mm_gate_up(s, e).then_inc(bank_filled[4], 1)

                def hidden_turned(e, i, q):
                    step_drained(pe, l, f"gate_up{e}", i, q)
                    step_drained(pe, l, f"hidden{e}", i, q, before=True)
                    pe.transpose(psum[:, TURN_BANK, 0:P], hb, ident[:]).then_inc(bank_filled[TURN_BANK], 1)

                def places_turned(i, q):
                    pe.wait_ge(sems["places_ready"], l * (3 * PAIRS) + (i * 6 + (3 * q - 3 * PAIRS)))
                    step_drained(pe, l, "places", i, q, before=True)
                    for t in range(2):
                        last = pe.transpose(psum[:, TURN_BANK, rows(t)], places_w[:, t, :], ident[:])
                    last.then_inc(bank_filled[TURN_BANK], 1)

                def down(j, i, q, s):
                    if j == 0:
                        step_drained(pe, l, "hidden0", i, q)
                        step_drained(pe, l, "hidden1", i, q)
                    step_drained(pe, l, f"down{j}", i, q, before=True)
                    mm_down(4 + j, j, s).then_inc(bank_filled[4 + j], 1)

                def scatter(t, i, q, opens=False):
                    if t == 0:
                        step_drained(pe, l, "places", i, q)
                        step_drained(pe, l, "down0", i, q)
                        step_drained(pe, l, "down1", i, q)
                    for j in range(2):
                        if opens:
                            drained(pe, l, ("y", t, j), before=True)
                        for y in (y_high, y_low):
                            pe.matmul(psum[:, 2 * t + j, :], placesT[:, rows(t)], y[:, j, :],
                                      start=opens and y is y_high, stop=False, skip_group_check=True)

                gather(0, 1)
                def landed(s, i):
                    a, b = TRUNK_DMAS[s], EXPERT_DMAS[s]
                    pe.wait_ge(slot_loaded[s], l * (16 * SLOT_DMAS[s]) + (i * (16 * b) + 16 * (a + b - SLOT_DMAS[s])))

                def two_pairs(i, first=False, final=False):
                    for q in (1, 2):
                        first_slot, second_slot, down_slot = EXPERT_SLOTS[3 * (q - 1):3 * q]
                        at_last = final and q == 2
                        landed(first_slot, i)
                        gate_up(0, i, q, first_slot)
                        if not (first and q == 1):
                            scatter(0, i, q - 1, opens=first)
                        hidden_turned(0, i, q)
                        landed(second_slot, i)
                        gate_up(1, i, q, second_slot)
                        if not (first and q == 1):
                            scatter(1, i, q - 1, opens=first)
                        hidden_turned(1, i, q)
                        if not at_last:
                            gather(i, q + 1)
                        places_turned(i, q)
                        landed(down_slot, i)
                        down(0, i, q, down_slot)
                        down(1, i, q, down_slot)

                def shared_job(n):
                    if n < 2:
                        signal(pe, l, "shared_loaded", 48)
                        shared_drained(pe, l, n, before=True)
                        for k, weights in enumerate((shared_gate_weights, shared_up_weights)):
                            for c in range(DC):
                                last = pe.matmul(psum[:, SHARED_BANK, k * DE:(k + 1) * DE], hT[:, c, rows(n)],
                                                 weights[:, c, :], start=c == 0, stop=c == DC - 1)
                        last.then_inc(bank_filled[SHARED_BANK], 1)
                    elif n == 2:
                        shared_drained(pe, l, 0)
                        shared_drained(pe, l, n, before=True)
                        for i in range(4):
                            t, c = i % 2, i // 2
                            last = pe.transpose(psum[:, SHARED_BANK, i * P:(i + 1) * P],
                                                shared_hidden[:, t * DE + c:(t + 1) * DE:2], ident[:])
                        last.then_inc(bank_filled[SHARED_BANK], 1)
                    else:
                        shared_drained(pe, l, 2)
                        for t in range(2):
                            for j in range(2):
                                for c in range(2):
                                    pe.matmul(psum[:, 2 * t + j, :], shared_hiddenT[:, c, rows(t)],
                                              shared_down_weights[:, c, 512 * j:512 * j + 512], start=False, stop=False,
                                              skip_group_check=True)

                segments(pe, two_pairs, shared_job)
                for t in range(2):
                    scatter(t, ROUNDS - 1, 2)
                signal(pe, l, "spare_ready", 1)
                settle(pe)
                passes = pe.value_load(spare_count[0:1, 0:1], min_val=0, max_val=SPARE - 1)
                with pe.If(passes > 0):
                    with pe.Fori(0, passes) as n:
                        pe.drain().then_inc(pe_to_dve, 1)
                        pe.wait_ge(dve_to_pe, n * 4 + 1)
                        for a in range(2):
                            mm_gather(GATHER_BANKS[a], a, SLOTS_E).then_inc(pe_to_act, 1)
                        for t in range(2):
                            last = pe.transpose(psum[:, TURN_BANK, rows(t)], places_w[:, t, :], ident[:])
                        last.then_inc(pe_to_dve, 1)
                        pe.wait_ge(spare_loaded, n * 48 + 48)
                        pe.wait_ge(act_to_pe, n * 3 + 2)
                        mm_gate_up(SPARE_SLOTS[0], 0).then_inc(pe_to_act, 1)
                        pe.wait_ge(dve_to_pe, n * 4 + 3)
                        pe.transpose(psum[:, TURN_BANK, 0:P], hb, ident[:]).then_inc(pe_to_act, 1)
                        pe.wait_ge(act_to_pe, n * 3 + 3)
                        weights = ring[:, SPARE_SLOTS[1], 0:2048].rearrange("p (c n) -> p c n", c=2)
                        for c in range(2):
                            for j in range(2):
                                last = pe.matmul(psum[halves[j], 5, :], hbT[:, 0, c, :],
                                                 weights[:, c, 512 * j:512 * j + 512], start=c == 0, stop=c == 1)
                        last.then_inc(pe_to_dve, 1)
                        pe.drain().then_inc(spare_used, 1)
                        pe.wait_ge(dve_to_pe, n * 4 + 4)
                        for t in range(2):
                            for j in range(2):
                                for y in (y_high, y_low):
                                    pe.matmul(psum[:, 2 * t + j, :], placesT[halves[j], rows(t)], y[halves[j], 0, :],
                                              start=False, stop=False, skip_group_check=True)
                    pe.sem_clear(dve_to_pe)
                    pe.sem_clear(act_to_pe)
                    pe.sem_clear(spare_loaded)
                for b in range(4):
                    pe.drain().then_inc(bank_filled[b], 1)

        @block.scalar
        def _(act):
            chain = [0]

            def link(ins):
                chain[0] += 1
                ins.then_inc(act_chain, 1)
                act.wait_ge(act_chain, chain[0])

            with act.Fori(1, DEPTH + 1) as l:
                chain[0] = 0

                def move(key, dst, src, func=ACT.Copy, scale=1.0):
                    filled(act, l, key)
                    act.activation(dst, src, func, scale=scale).then_inc(bank_drained[BANK[key]], 1)

                def four_blocks(key):
                    return bank(key).rearrange("p (c n) -> p c n", c=4)

                split = [0]

                def round_weights(names):
                    for name in names.split():
                        n = split[0]
                        assert SPLIT[n] == name
                        split[0] += 1
                        if n >= 2:
                            filled(act, l, dict(USES)[SPLIT[n - 2]])
                        else:
                            expert_slot_free(act, l - 1, ROUNDS - 1, RING + n)
                        loaded(act, l, name)
                        size = used_columns(name)
                        act.activation(weight_high[:, n % 2, 0:size], ring[:, POS[name], 0:size],
                                       ACT.Copy).then_inc(sems["weight_rounded"], 1)

                def round_turned(what, dst):
                    for t in range(2):
                        for f in range(2):
                            filled(act, l, (what, t, f))
                            act.activation(dst[:, 4 * f:4 * f + 4, t * P:t * P + P], four_blocks((what, t, f)),
                                           ACT.Copy).then_inc(sems["act_high"], 1)

                round_weights("gf")
                round_turned("hT", hT_high)
                round_weights("gq")
                move(("gfr",), gfrT[:], psum[0:GR, BANK["gfr",], 0:S])
                round_weights("gk")
                signal(act, l, "abs_ready", 1)
                link(act.activation(tmp_e, tmp_e, ACT.Exp, scale=-1.0))
                act.activation(tmp_e, tmp_e, ACT.Ln, bias=1.0).then_inc(sems["log_ready"], 1)
                signal(act, l, "cum_ready", 1)
                act.activation(qd, b_cum, ACT.Exp, scale=1.0 / GATE_TAU).then_inc(sems["exp_ready"], 1)
                act.activation(ki, b_cum, ACT.Exp, scale=-1.0 / GATE_TAU).then_inc(sems["exp_ready"], 1)
                signal(act, l, "cum_ready", 2)
                act.activation(keT, tmp_e, ACT.Exp, scale=1.0 / GATE_TAU).then_inc(sems["exp_ready"], 1)
                round_weights("gv0 gv1")
                for j in range(2):
                    for t in range(2):
                        move(("v", j, t), gv[:, t, 512 * j:512 * j + 512], bank(("v", j, t)))
                    round_weights(f"gr{j}")
                for j in range(2):
                    for t in range(2):
                        move(("gr", j, t), gr[:, t, 512 * j:512 * j + 512], bank(("gr", j, t)), ACT.Silu)
                    if j == 0:
                        round_weights("sg0")
                for t in range(2):
                    move(("ke", t), ke[:, t, :], bank(("ke", t)))
                move(("sgwT",), sgwT[:], four_blocks(("sgwT",)))
                round_weights("sg1")
                for n in range(GH):
                    key = ("o", n)
                    filled(act, l, key)
                    for t in range(2):
                        ins = act.activation(squares[:, t, 0:GDV], bank(key)[:, t * GDV:(t + 1) * GDV], ACT.Square,
                                             accum_out=ssq[:, 2 * n + t:2 * n + t + 1])
                        if t == 0:
                            link(ins)
                    link(ins)
                    act.activation(rstd[:, 2 * n:2 * n + 2], ssq[:, 2 * n:2 * n + 2], ACT.Copy, scale=1.0 / GDV,
                                   bias=RMS_EPS).then_inc(sems["ms_ready"], 1)
                for z in range(4):
                    for t in range(2):
                        half = u if z < 2 else vv
                        move(("sg", z, t), half[:, t, 512 * (z % 2):512 * (z % 2) + 512], bank(("sg", z, t)), ACT.Gelu)
                    round_weights(("sg2", "sg3", "mq", "mkv")[z])
                    if z == 1:
                        for t in range(2):
                            for f in range(2):
                                signal(act, l, "whole_ready", 2 * t + f + 1)
                                part = (slice(None), slice(4 * f, 4 * f + 4), slice(t * P, t * P + P))
                                act.activation(bT_high[part], bT_whole[part], ACT.Copy).then_inc(sems["act_high"], 1)
                round_weights("g00 b00")
                for t in range(2):
                    filled(act, l, ("mq", t))
                    filled(act, l, ("mkv", t))
                    link(act.activation(squares[:, t, 0:QR], bank(("mq", t))[:, 0:QR], ACT.Square,
                                        accum_out=ssq[:, 8 + 2 * t:9 + 2 * t]))
                    link(act.activation(squares[:, t, 0:KVR], bank(("mkv", t))[:, 0:KVR], ACT.Square,
                                        accum_out=ssq[:, 9 + 2 * t:10 + 2 * t]))
                    link(act.activation(rstd[:, 8 + 2 * t:9 + 2 * t], ssq[:, 8 + 2 * t:9 + 2 * t], ACT.Copy,
                                        scale=1.0 / QR, bias=RMS_EPS))
                    act.activation(rstd[:, 9 + 2 * t:10 + 2 * t], ssq[:, 9 + 2 * t:10 + 2 * t], ACT.Copy,
                                   scale=1.0 / KVR, bias=RMS_EPS).then_inc(sems["ms_ready"], 1)


                def gates(kind, pair, previous=None, rounded=("", "", "", ""), between=lambda j: None):
                    for j in range(2):
                        for t in range(2):
                            key, before = kind(j, t), pair(0, t) if j else previous
                            filled(act, l, key)
                            if before is not None:
                                drained(act, l, before)
                            act.activation(gsig[:, t, :], bank(key), ACT.Sigmoid).then_inc(bank_drained[BANK[key]], 1)
                        round_weights(rounded[2 * j])
                        between(j)
                        round_weights(rounded[2 * j + 1])

                branch = lambda n: (lambda j, t: ("gate", n, j, t), lambda j, t: ("proj", n, j, t))
                gates(*branch(0), rounded=("g01", "b01", "g10", ""))
                round_turned("obT", bT_high)
                round_weights("b10")
                gates(*branch(1), previous=("proj", 0, 1, 1), rounded=("g11", "b11", "", ""))
                for kind, dst in (("qn", qnope), ("kn", knope)):
                    for i in range(4):
                        move((kind, i), dst[:, 2 * i:2 * i + 2, :], bank((kind, i)).rearrange("p (c n) -> p c n", c=2))
                round_weights("g20")
                for t in range(2):
                    for j in range(2):
                        move(("vm", t, j), vm[:, t, 512 * j:512 * j + 512], bank(("vm", t, j)))
                for t in range(2):
                    move(("qrT", t), qrT[:, :, t * P:t * P + P], four_blocks(("qrT", t)))
                for n in range(MH + 1):
                    if n < MH:
                        signal(act, l, "max_ready", n + 1)
                        if n >= 2:
                            filled(act, l, ("pT", n - 2))
                        for r, (part, a, k) in enumerate(regions):
                            ins = act.activation(prob[part, n % 2, a:a + k], bank(("s", n))[part, a:a + k], ACT.Exp,
                                                 bias=sm_max[part, n % 2, a // P:a // P + 1], scale=QK ** -0.5,
                                                 accum_out=sm_sum[part, n % 2, a // P:a // P + 1])
                            if r < 3:
                                link(ins)
                        ins.then_inc(sems["exp_p"], 1)
                    if n:
                        move(("pT", n - 1), pT[:, (n - 1) % 2, :], bank(("pT", n - 1))[:, 0:384])
                round_weights("b20")

                def round_merged(j):
                    if j == 1:
                        move(("ppT",), pleT, bank(("ppT",)).rearrange("p (c n) -> p c n", c=2))
                    for t in range(2):
                        filled(act, l, ("mT", j, t))
                        act.activation(mT_high[:, 4 * j:4 * j + 4, t * P:t * P + P], four_blocks(("mT", j, t)),
                                       ACT.Copy).then_inc(sems["act_high"], 1)

                gates(*branch(2), previous=("proj", 1, 1, 1), rounded=("g21", "b21", "wo0", ""),
                      between=lambda j: round_merged(0) if j else None)
                round_merged(1)
                round_weights("wo1")
                for j in range(2):
                    for t in range(2):
                        move(("pli", j, t), mixed[:, t, 512 * j:512 * j + 512], bank(("pli", j, t)))
                for t in range(2):
                    move(("hT2", t, 0), hT[:, 0:4, t * P:t * P + P], four_blocks(("hT2", t, 0)))
                for t in range(2):
                    move(("rt", t), score[:, t, :], bank(("rt", t))[:, 0:NE], ACT.Sigmoid)
                for j in range(2):
                    for t in range(2):
                        filled(act, l, ("plg", j, t))
                        if j:
                            signal(act, l, "embedded", t + 1)
                        act.activation(gsig[:, t, :], bank(("plg", j, t)),
                                       ACT.Sigmoid).then_inc(bank_drained[BANK["plg", j, t]], 1)

                def take(what, dst, src, b, i, q):
                    step_filled(act, l, what, i, q)
                    act.activation(dst, src, ACT.Copy).then_inc(bank_drained[b], 1)

                def take_gathered(i, q):
                    for a in range(2):
                        take(f"gather{a}", xgT[:, 4 * a:4 * a + 4, :].rearrange("p a b -> p (a b)"), psum[:, GATHER_BANKS[a], :],
                             GATHER_BANKS[a], i, q)

                def take_hidden(e, i, q):
                    take(f"hidden{e}", hbT[:, e].rearrange("p a b -> p (a b)"), psum[:, TURN_BANK, 0:P], TURN_BANK, i, q)

                def silu(e, i, q):
                    step_filled(act, l, f"gate_up{e}", i, q)
                    act.activation(sgate_e, psum[:, 4, 0:P], ACT.Silu).then_inc(sems["silu_ready"], 1)

                def act_pairs(i, first=False, final=False):
                    for q in (1, 2):
                        silu(0, i, q)
                        take_hidden(0, i, q)
                        silu(1, i, q)
                        take_hidden(1, i, q)
                        if not (final and q == 2):
                            take_gathered(i, q + 1)

                take_gathered(0, 1)

                def silu_shared(n):
                    if n < 2:
                        shared_filled(act, l, n)
                        act.activation(shared_gate[:, n, :], psum[:, SHARED_BANK, 0:DE],
                                       ACT.Silu).then_inc(sems["shared_silu"], 1)

                segments(act, act_pairs, silu_shared)
                signal(act, l, "spare_ready", 1)
                settle(act)
                passes = act.value_load(spare_count[0:1, 0:1], min_val=0, max_val=SPARE - 1)
                with act.If(passes > 0):
                    with act.Fori(0, passes) as n:
                        for a in range(2):
                            act.wait_ge(pe_to_act, n * 4 + (a + 1))
                            act.activation(xgT[:, 4 * a:4 * a + 4, 0:SLOTS_E],
                                           psum[:, GATHER_BANKS[a], :].rearrange("p (i s) -> p i s", i=4)[:, :, 0:SLOTS_E],
                                           ACT.Copy).then_inc(act_to_pe, 1)
                        act.wait_ge(pe_to_act, n * 4 + 3)
                        act.activation(sgate_e, psum[:, 4, 0:P], ACT.Silu).then_inc(act_to_dve, 1)
                        act.wait_ge(pe_to_act, n * 4 + 4)
                        act.activation(hbT[:, 0].rearrange("p a b -> p (a b)"), psum[:, TURN_BANK, 0:P],
                                       ACT.Copy).then_inc(act_to_pe, 1)
                    act.sem_clear(pe_to_act)
                assert split[0] == len(SPLIT)
                act.wait_ge(act_chain, chain[0])
                act.sem_clear(act_chain)

        @block.vector
        def _(dve):
            chain = [0]

            def link(ins):
                chain[0] += 1
                ins.then_inc(dve_chain, 1)
                dve.wait_ge(dve_chain, chain[0])

            def end_chain():
                dve.sem_clear(dve_chain)
                chain[0] = 0

            def link_clear(ins):
                ins.then_inc(dve_step, 1)
                dve.wait_ge(dve_step, 1)
                dve.sem_clear(dve_step)

            def half_statistics(x, t, i):
                link(dve.bn_stats(stats[:, t, i, :], x[:, t, 512 * i:512 * i + 512]))

            def normalise(x, g, b, wait_rstd, ready, between=lambda: None, arrived=lambda t: None,
                          scale_arrived=lambda: None, counted=False):
                for t in range(2):
                    arrived(t)
                    if not counted:
                        for i in range(2):
                            half_statistics(x, t, i)
                    link(dve.bn_aggr(mv[:, t, :], stats[:, t, :, :].rearrange("p a b -> p (a b)")))
                dve.tensor_scalar(rstd[:, 12:14], mv[:, :, 1], LN_EPS, None, ALU.add).then_inc(sems["var_ready"], 1)

                def finish(t):
                    dve.scalar_tensor_tensor(x[:, t, :], x[:, t, :], rstd[:, 12 + t:13 + t], b,
                                             ALU.mult, ALU.add).then_inc(sems[ready], 1)

                scale_arrived()
                for t in range(2):
                    if t:
                        wait_rstd()
                        finish(0)
                        between()
                    link(dve.scalar_tensor_tensor(x[:, t, :], x[:, t, :], mv[:, t, 0:1], g, ALU.subtract, ALU.mult))
                finish(1)

            normalise(h[:], ln_g[:], ln_b[:], lambda: dve.wait_ge(sems["rstd_ready"], 1), "h_ready",
                      arrived=lambda t: dve.wait_ge(x_loaded[t], 16),
                      scale_arrived=lambda: dve.wait_ge(ln_in_loaded, 32))
            dve.wait_ge(setup_done, 1)
            dve.wait_ge(tables_loaded, 32)
            end_chain()

            with dve.Fori(1, DEPTH + 1) as l:

                def done(ins, key):
                    ins.then_inc(bank_drained[BANK[key]], 1)

                def four_blocks(key):
                    return bank(key).rearrange("p (c n) -> p c n", c=4)

                split, turned = [0], [0]

                def leave_weights(names):
                    for name in names.split():
                        n = split[0]
                        assert SPLIT[n] == name
                        split[0] += 1
                        signal(dve, l, "weight_rounded", n + 1)
                        size = used_columns(name)
                        dve.tensor_tensor(weight_low[:, POS[name], 0:size], ring[:, POS[name], 0:size],
                                          weight_high[:, n % 2, 0:size], ALU.subtract).then_inc(sems["weight_split"], 1)

                def leave_turned(what, high, low):
                    for t in range(2):
                        for f in range(2):
                            turned[0] += 1
                            signal(dve, l, "act_high", turned[0])
                            part = (slice(None), slice(4 * f, 4 * f + 4), slice(t * P, t * P + P))
                            whole = bT_whole[part] if what == "oaT" else four_blocks((what, t, f))
                            done(dve.tensor_tensor(low[part], whole, high[part], ALU.subtract), (what, t, f))

                leave_weights("gf")
                leave_turned("hT", hT_high, hT_low)
                leave_weights("gq")
                link(dve.memset(att, 0.0))
                signal(dve, l, "fg_loaded", 32)
                for i in range(2):
                    filled(dve, l, ("fg", i))
                    for n in range(2):
                        ins = dve.tensor_scalar(b_cum[:, 2 * i + n, :], bank(("fg", i))[:, n * S:n * S + S],
                                                fgb[:, 2 * i + n:2 * i + n + 1], None, ALU.add)
                        if n == 0:
                            link(ins)
                    done(ins, ("fg", i))
                    drained(dve, l, ("fg", i))
                dve.scalar_tensor_tensor(tmp_e, b_cum, -1.0, b_cum, ALU.mult, ALU.max).then_inc(sems["abs_ready"], 1)
                leave_weights("gk")
                signal(dve, l, "log_ready", 1)
                link(dve.scalar_tensor_tensor(keT, b_cum, 0.0, tmp_e, ALU.min, ALU.subtract))
                for n in range(GH):
                    ins = dve.tensor_tensor_scan(b_cum[:, n, :], restart[:], keT[:, n, :], 0.0, ALU.mult, ALU.add)
                    if n < GH - 1:
                        link(ins)
                ins.then_inc(sems["cum_ready"], 1)
                signal(dve, l, "cum_ready", 1)
                chunks = lambda x: x.rearrange("p h (c t) -> p (h c) t", t=CHUNK)
                ends = chunks(b_cum)[:, :, CHUNK - 1:CHUNK].to_broadcast([P, GH * S // CHUNK, CHUNK])
                dve.tensor_tensor(chunks(tmp_e), ends, chunks(b_cum), ALU.subtract).then_inc(sems["cum_ready"], 1)
                leave_weights("gv0")
                signal(dve, l, "exp_ready", 1)
                link(dve.tensor_copy(decay[:].rearrange("p h c -> p (h c)"), chunks(qd)[:, :, CHUNK - 1]))
                two = lambda key: bank(key).rearrange("p (c n) -> p c n", c=2)
                for i in range(2):
                    filled(dve, l, ("q", i))
                    done(dve.scalar_tensor_tensor(qd[:, 2 * i:2 * i + 2, :], two(("q", i)), GDK ** -0.5,
                                                  qd[:, 2 * i:2 * i + 2, :], ALU.mult, ALU.mult), ("q", i))
                leave_weights("gv1")
                signal(dve, l, "exp_ready", 3)
                for i in range(2):
                    filled(dve, l, ("k", i))
                    link(dve.tensor_tensor(ki[:, 2 * i:2 * i + 2, :], two(("k", i)), ki[:, 2 * i:2 * i + 2, :], ALU.mult))
                    done(dve.tensor_tensor(keT[:, 2 * i:2 * i + 2, :], two(("k", i)), keT[:, 2 * i:2 * i + 2, :],
                                           ALU.mult), ("k", i))
                    drained(dve, l, ("k", i))
                dve.nop().then_inc(sems["ke_ready"], 1)
                leave_weights("gr0 gr1 sg0")
                for n in range(GH + 1):
                    if n < GH:
                        filled(dve, l, ("att", n))
                        settle(dve)
                        done(dve.copy_predicated(att[:, n % 2, :], gla_mask[:].rearrange("p t s -> p (t s)"),
                                                 bank(("att", n))[:, 0:S]), ("att", n))
                        filled(dve, l, ("ds", n, 1))
                        if n:
                            filled(dve, l, ("o", n - 1))
                        ds = bank(("ds", n, 0))
                        link(dve.tensor_copy(state[:, 0, :], ds[:, 0:GDV]))
                        done(dve.scalar_tensor_tensor(state[:, 1, :], state[:, 0, :], decay[:, n, 1:2],
                                                      bank(("ds", n, 1))[:, 0:GDV], ALU.mult, ALU.add), ("ds", n, 1))
                        drained(dve, l, ("ds", n, 1))
                        done(dve.scalar_tensor_tensor(state[:, 2, :], state[:, 1, :], decay[:, n, 2:3],
                                                      ds[:, GDV:2 * GDV], ALU.mult, ALU.add), ("ds", n, 0))
                    if n:
                        m = n - 1
                        if n == 1:
                            for j in range(2):
                                for t in range(2):
                                    drained(dve, l, ("gr", j, t))
                        signal(dve, l, "rms_ready", m + 1)
                        for t in range(2):
                            g = gr[:, t, m * GDV:(m + 1) * GDV]
                            ins = dve.scalar_tensor_tensor(g, bank(("o", m))[:, t * GDV:(t + 1) * GDV],
                                                           rstd[:, 2 * m + t:2 * m + t + 1], g, ALU.mult, ALU.mult)
                        done(ins, ("o", m))
                leave_weights("sg1 sg2")
                signal(dve, l, "params_loaded", 16 * PARAMS)
                for t in range(2):
                    for f in range(2):
                        key = ("oaT", t, f)
                        filled(dve, l, key)
                        gain = glag[:, 4 * f:4 * f + 4].unsqueeze(2).to_broadcast([P, 4, P])
                        dve.tensor_tensor(bT_whole[:, 4 * f:4 * f + 4, t * P:t * P + P], four_blocks(key), gain,
                                          ALU.mult).then_inc(sems["whole_ready"], 1)
                leave_weights("sg3")
                leave_turned("oaT", bT_high, bT_low)
                leave_weights("mq mkv g00 b00")
                for t in range(2):
                    signal(dve, l, "rms_ready", GH + t + 1)
                    done(dve.tensor_scalar(mq[:, t, :], bank(("mq", t))[:, 0:QR], rstd[:, 8 + 2 * t:9 + 2 * t], None,
                                           ALU.mult), ("mq", t))
                    link(dve.tensor_scalar(mkv[:, t, 0:KVR], bank(("mkv", t))[:, 0:KVR], rstd[:, 9 + 2 * t:10 + 2 * t],
                                           None, ALU.mult))
                    done(dve.tensor_copy(mkv[:, t, KVR:KVR + ROPE], bank(("mkv", t))[:, KVR:KVR + ROPE]), ("mkv", t))
                    drained(dve, l, ("mkv", t))
                for z in (2, 3):
                    for t in range(2):
                        drained(dve, l, ("sg", z, t))
                normalise(vv, sgn_g, sgn_b, lambda: signal(dve, l, "rstd_ready", 2), "vln_ready",
                          between=lambda: leave_weights("g01"))
                def merge(n, rounded, between=lambda j: None):
                    for j in range(2):
                        leave_weights(rounded[2 * j])
                        between(j)
                        for t in range(2):
                            filled(dve, l, ("proj", n, j, t))
                            drained(dve, l, ("gate", n, j, t))
                            m = mixed[:, t, 512 * j:512 * j + 512]
                            if n == 0:
                                done(dve.tensor_tensor(m, bank(("proj", n, j, t)), gsig[:, t, :], ALU.mult),
                                     ("proj", n, j, t))
                            else:
                                if (j, t) == (0, 0):
                                    drained(dve, l, ("proj", n - 1, 1, 1))
                                link(dve.tensor_tensor(gsig[:, t, :], bank(("proj", n, j, t)), gsig[:, t, :], ALU.mult))
                                done(dve.tensor_tensor(m, m, gsig[:, t, :], ALU.add), ("proj", n, j, t))
                        leave_weights(rounded[2 * j + 1])

                def rotate_key():
                    k1, k2 = mkv[:, :, KVR:KVR + HALF], mkv[:, :, KVR + HALF:KVR + ROPE]
                    kt = [rtmp[:, i, 0:2 * HALF].rearrange("p (t n) -> p t n", t=2) for i in range(4)]
                    for i, (a, b) in enumerate(((k1, cos_t), (k2, sin_t), (k1, sin_t), (k2, cos_t))):
                        link(dve.tensor_tensor(kt[i], a, b[:], ALU.mult))
                    for n in range(2):
                        link(dve.tensor_tensor(krot[:, :, ROPE * n:ROPE * n + HALF], kt[0], kt[1], ALU.subtract))
                        ins = dve.tensor_tensor(krot[:, :, ROPE * n + HALF:ROPE * n + ROPE], kt[2], kt[3], ALU.add)
                        if n == 0:
                            link(ins)
                    ins.then_inc(sems["krot_ready"], 1)

                def mix_tokens(j):
                    if j == 0:
                        return rotate_key()
                    for z in (0, 1):
                        for t in range(2):
                            drained(dve, l, ("sg", z, t))
                    for t in range(2):
                        for i in range(2):
                            filled(dve, l, ("sv", t, i))
                            for n in range(2):
                                g = 2 * i + n
                                part = u[:, t, g * 256:g * 256 + 256]
                                ins = dve.scalar_tensor_tensor(part, bank(("sv", t, i))[:, n * 256:n * 256 + 256],
                                                               sgb[:, g:g + 1], part, ALU.add, ALU.mult)
                            done(ins, ("sv", t, i))

                merge(0, ("", "b01", "g10", ""), between=mix_tokens)
                leave_turned("obT", bT_high, bT_low)
                for t in range(2):
                    key = ("qnT", t)
                    filled(dve, l, key)
                    done(dve.tensor_tensor(qnT[:, :, t * P:t * P + P],
                                           bank(key)[:, 0:QR].rearrange("p (c n) -> p c n", c=3),
                                           qng[:].unsqueeze(2).to_broadcast([P, 3, P]), ALU.mult), key)
                for t in range(2):
                    key = ("ckT", t)
                    filled(dve, l, key)
                    done(dve.tensor_tensor(ckT[:, :, t * P:t * P + P],
                                           bank(key)[:, 0:KVR].rearrange("p (c n) -> p c n", c=2),
                                           kvng[:].unsqueeze(2).to_broadcast([P, 2, P]), ALU.mult), key)
                filled(dve, l, ("krT",))
                done(dve.tensor_copy(krT, bank(("krT",))[:, 0:S]), ("krT",))
                leave_weights("b10")
                merge(1, ("g11", "b11", "", ""))
                pair = lambda x: x.rearrange("p (h n) -> p h n", h=MH)
                for t in range(2):
                    key = ("qr", t)
                    filled(dve, l, key)
                    q1, q2 = pair(bank(key))[:, :, 0:HALF], pair(bank(key))[:, :, HALF:ROPE]
                    cs, sn = (x[:, t, :].unsqueeze(1).to_broadcast([P, MH, HALF]) for x in (cos_t, sin_t))
                    qt = [rtmp[:, i, :].rearrange("p (h n) -> p h n", h=MH) for i in range(4)]
                    for i, (a, b) in enumerate(((q1, cs), (q2, sn), (q1, sn), (q2, cs))):
                        link(dve.tensor_tensor(qt[i], a, b, ALU.mult))
                    dve.nop().then_inc(bank_drained[BANK[key]], 1)
                    link(dve.tensor_tensor(pair(qrot[:, t, :])[:, :, 0:HALF], qt[0], qt[1], ALU.subtract))
                    link(dve.tensor_tensor(pair(qrot[:, t, :])[:, :, HALF:ROPE], qt[2], qt[3], ALU.add))
                    dve.nop().then_inc(sems["qrot_ready"], 1)
                for n in range(2):
                    link(dve.memset(prob[0:CHUNK, n, P - CHUNK:P], 0.0))
                    link(dve.memset(prob[0:CHUNK, n, 3 * P - CHUNK:3 * P], 0.0))
                def negative_maxima(n):
                    filled(dve, l, ("s", n))
                    if n >= 2:
                        signal(dve, l, "exp_p", n - 1)
                    for part, a, k in regions:
                        link(dve.reduce_max(sm_top[part, n % 2, a // P:a // P + 1], bank(("s", n))[part, a:a + k],
                                            axis=mybir.AxisListType.X))
                    dve.tensor_scalar(sm_max[:, n % 2, :], sm_top[:, n % 2, :], -(QK ** -0.5), None,
                                      ALU.mult).then_inc(sems["max_ready"], 1)

                def divide(n):
                    signal(dve, l, "exp_p", n + 1)
                    link(dve.reciprocal(sm_inv[:, n % 2, :], sm_sum[:, n % 2, :]))
                    dve.nop().then_inc(bank_drained[BANK["s", n]], 1)
                    link(dve.tensor_scalar(prob[:, n % 2, 0:P], prob[:, n % 2, 0:P], sm_inv[:, n % 2, 0:1], None,
                                           ALU.mult))
                    dve.tensor_scalar(prob[:, n % 2, P:3 * P], prob[:, n % 2, P:3 * P], sm_inv[:, n % 2, 1:2], None,
                                      ALU.mult).then_inc(sems["prob_ready"], 1)

                def split_context(n):
                    x = bank(("oc", n))[:, 0:S]
                    filled(dve, l, ("oc", n))
                    link(dve.tensor_copy(bT_high[:, n, :], x))
                    done(dve.tensor_tensor(bT_low[:, n, :], x, bT_high[:, n, :], ALU.subtract), ("oc", n))

                for n in range(MH + 3):
                    if n < MH:
                        negative_maxima(n)
                    if 1 <= n <= MH:
                        divide(n - 1)
                    if n == MH:
                        leave_weights("g20")
                    if n >= 3:
                        split_context(n - 3)
                leave_weights("b20")

                def leave_merged(j):
                    for t in range(2):
                        turned[0] += 1
                        signal(dve, l, "act_high", turned[0])
                        part = (slice(None), slice(4 * j, 4 * j + 4), slice(t * P, t * P + P))
                        done(dve.tensor_tensor(mT_low[part], four_blocks(("mT", j, t)), mT_high[part], ALU.subtract),
                             ("mT", j, t))

                merge(2, ("g21", "b21", "wo0", ""), between=lambda j: leave_merged(0) if j else None)
                leave_merged(1)
                leave_weights("wo1")
                assert split[0] == len(SPLIT)
                for j in range(2):
                    for t in range(2):
                        key, part = ("wo", j, t), h[:, t, 512 * j:512 * j + 512]
                        filled(dve, l, key)
                        done(dve.scalar_tensor_tensor(part, part, ALPHA, bank(key), ALU.mult, ALU.add), key)
                        drained(dve, l, key)
                        half_statistics(h, t, j)
                normalise(h[:], ln_g[:], ln_b[:], lambda: signal(dve, l, "rstd_ready", 3), "ln1_done", counted=True,
                          scale_arrived=lambda: signal(dve, l, "ln1_loaded", 32))
                for t in range(2):
                    key = ("hT2", t, 1)
                    filled(dve, l, key)
                    done(dve.tensor_copy(hT[:, 4:8, t * P:t * P + P], four_blocks(key)), key)
                end_chain()
                signal(dve, l, "ln1_done", TILES)
                for t in range(2):
                    drained(dve, l, ("rt", t))
                    link(dve.tensor_tensor(biased[:, t, :], score[:, t, :], rbias[:], ALU.add))
                    for g in range(NG):
                        ins = dve.max(grp8[:, g, :], biased[:, t, 8 * g:8 * g + 8])
                    link(ins)
                    link(dve.tensor_tensor(gsum, grp8[:, :, 0], grp8[:, :, 1], ALU.add))
                    mine = gsum.unsqueeze(2).to_broadcast([P, NG, NG])
                    other = gsum.unsqueeze(1).to_broadcast([P, NG, NG])
                    link(dve.tensor_tensor(cmp, other, mine, ALU.is_equal))
                    link(dve.tensor_tensor(cmp2, cmp, earlier[:], ALU.mult))
                    link(dve.tensor_tensor(cmp, other, mine, ALU.is_gt))
                    link(dve.tensor_tensor(cmp, cmp, cmp2, ALU.add))
                    link(dve.reduce_sum(gkeep, cmp, axis=mybir.AxisListType.X))
                    link(dve.tensor_scalar(gkeep, gkeep, TOPG - 0.5, None, ALU.is_lt))
                    keep8 = gkeep.unsqueeze(2).to_broadcast([P, NG, 8])
                    by_group = lambda x: x.rearrange("p (g n) -> p g n", g=NG)
                    link(dve.tensor_tensor(by_group(biased[:, t, :]), by_group(biased[:, t, :]), keep8, ALU.mult))
                    link(dve.tensor_scalar(gkeep, gkeep, 1.0, -LOW_FILL, ALU.subtract, ALU.mult))
                    link(dve.tensor_tensor(by_group(biased[:, t, :]), by_group(biased[:, t, :]), keep8, ALU.add))
                    link(dve.max(top8, biased[:, t, :]))
                    link(dve.match_replace(rep, top8, biased[:, t, :], TAKEN))
                    link(dve.tensor_tensor(rep, rep, biased[:, t, :], ALU.not_equal))
                    link(dve.tensor_copy(sel[:, t, :], rep))
                    link(dve.tensor_tensor(wts[:, t, :], rep, score[:, t, :], ALU.mult))
                    link(dve.reduce_sum(wsum[:, 0:1], wts[:, t, :], axis=mybir.AxisListType.X))
                    link(dve.reciprocal(wsum[:, 1:2], wsum[:, 0:1]))
                    link(dve.tensor_scalar(wts[:, t, :], wts[:, t, :], wsum[:, 1:2], ROUTED_SCALE, ALU.mult, ALU.mult))
                dve.nop().then_inc(sems["score_taken"], 1)
                permuted = lambda x: x.rearrange("p t (c a i) -> p t a i c", a=2, i=4)
                for t in range(2):
                    for a in range(2):
                        whole, left = permuted(h[:])[:, t, a], permuted(rest)[:, t, a]
                        link(dve.tensor_copy(parts[:, 0, t, a], whole))
                        link(dve.tensor_tensor(left, whole, parts[:, 0, t, a], ALU.subtract))
                        link(dve.tensor_copy(parts[:, 1, t, a], left))
                        link(dve.tensor_tensor(parts[:, 2, t, a], left, parts[:, 1, t, a], ALU.subtract))
                def column(x, t, e, i, q):
                    return x[:, t, bass.ds(4 * i + (2 * q - 2 + e), 1)]

                def place(e, i, q):
                    for t in range(2):
                        last = dve.tensor_scalar(places[:, t, SLOTS_E * e:SLOTS_E * (e + 1)], iota[:, 0:SLOTS_E],
                                                 column(pos, t, e, i, q), None, ALU.is_equal)
                    last.then_inc(sems["places_ready"], 1)

                def place_weights(i, q):
                    for e in range(2):
                        for t in range(2):
                            last = dve.tensor_scalar(places_w[:, t, SLOTS_E * e:SLOTS_E * (e + 1)], iota[:, 0:SLOTS_E],
                                                     column(pos, t, e, i, q), column(wts, t, e, i, q), ALU.is_equal,
                                                     ALU.mult)
                    last.then_inc(sems["places_ready"], 1)

                for j in range(2):
                    if j:
                        for t in range(2):
                            filled(dve, l, ("rank", t))
                            link(dve.scalar_tensor_tensor(pos[:, t, :], bank(("rank", t))[:, 0:NE], 1.0, sel[:, t, :],
                                                          ALU.add, ALU.mult))
                            link(dve.tensor_scalar(pos[:, t, :], pos[:, t, :], 1.0, None, ALU.subtract))
                            if t == 0:
                                done(dve.nop(), ("rank", 0))
                                continue
                            chosen = bank(("rank", t))[:, NE:2 * NE]
                        for b in range(OVER):
                            link(dve.scalar_tensor_tensor(spare_key[:, b * NE:(b + 1) * NE], chosen, (b + 1) * SLOTS_E + 0.5,
                                                          spare_code[:, b, :], ALU.is_gt, ALU.mult))
                        done(dve.nop(), ("rank", 1))
                        place(0, 0, 1)
                        place(1, 0, 1)
                        place_weights(0, 1)
                        for n in range(SPARE // 8):
                            best = spare_top[:, 8 * n:8 * n + 8]
                            link(dve.max(best, spare_key))
                            link(dve.match_replace(spare_key, best, spare_key, 0.0))
                        link(dve.tensor_scalar(spare_unit[:], spare_top[:], -1.0, 256.0, ALU.mult, ALU.add))
                        link(dve.tensor_single_scalar(spare_expert[:], spare_unit[:], NE - 1, ALU.bitwise_and))
                        link(dve.tensor_tensor(spare_rank[:], spare_unit[:], spare_expert[:], ALU.subtract))
                        link(dve.tensor_scalar(spare_rank[:], spare_rank[:], SLOTS_E / NE, float(SLOTS_E), ALU.mult, ALU.add))
                        link(dve.tensor_scalar(spare_top[:], spare_top[:], 0.5, None, ALU.is_gt))
                        link(dve.reduce_sum(spare_sum[:], spare_top[:], axis=mybir.AxisListType.X))
                        dve.tensor_copy(spare_count[:], spare_sum[:]).then_inc(sems["spare_ready"], 1)
                    for t in range(2):
                        drained(dve, l, ("pli", j, t))
                        drained(dve, l, ("plg", j, t))
                        part = mixed[:, t, 512 * j:512 * j + 512]
                        dve.tensor_tensor(part, part, gsig[:, t, :], ALU.mult).then_inc(sems["embedded"], 1)
                signal(dve, l, "embedded", 4)
                for t in range(2):
                    link(dve.scalar_tensor_tensor(mixed[:, t, :], h[:, t, :], ALPHA, mixed[:, t, :], ALU.mult, ALU.add))

                def split_places(x):
                    link_clear(dve.reduce_sum(slot_weight[:], x, axis=mybir.AxisListType.X))
                    return dve.tensor_scalar(placesT[:], x, 0.0, None, ALU.not_equal)

                def split_output(j, x):
                    link_clear(dve.tensor_scalar(y_high[:, j, :], x, slot_weight[:, 0:1], None, ALU.mult))
                    return dve.scalar_tensor_tensor(y_low[:, j, :], x, slot_weight[:, 0:1], y_high[:, j, :],
                                                    ALU.mult, ALU.subtract)

                def gated(e, i, q):
                    dve.wait_ge(sems["silu_ready"], l * NE + (4 * i + (2 * q - 1 + e - NE)))
                    dve.tensor_tensor(hb, psum[:, 4, P:2 * P], sgate_e, ALU.mult).then_inc(bank_drained[4], 1)

                def shared_values(n):
                    if n < 2:
                        signal(dve, l, "shared_silu", n + 1)
                        dve.tensor_tensor(shared_hidden[:, n * DE:(n + 1) * DE], psum[:, SHARED_BANK, DE:2 * DE],
                                          shared_gate[:, n, :], ALU.mult).then_inc(bank_drained[SHARED_BANK], 1)
                    elif n == 2:
                        shared_filled(dve, l, n)
                        dve.tensor_copy(shared_hiddenT, psum[:, SHARED_BANK, :].rearrange("p (c n) -> p c n", c=2)
                                        ).then_inc(bank_drained[SHARED_BANK], 1)

                def dve_pairs(i, first=False, final=False):
                    for q in (1, 2):
                        more = not (final and q == 2)
                        gated(0, i, q)
                        if more:
                            place(0, i, q + 1)
                            place(1, i, q + 1)
                        gated(1, i, q)
                        step_filled(dve, l, "places", i, q)
                        split_places(psum[:, TURN_BANK, 0:S]).then_inc(bank_drained[TURN_BANK], 1)
                        for j in range(2):
                            step_filled(dve, l, f"down{j}", i, q)
                            split_output(j, psum[:, 4 + j, :]).then_inc(bank_drained[4 + j], 1)
                        if more:
                            place_weights(i, q + 1)

                segments(dve, dve_pairs, shared_values)
                signal(dve, l, "spare_ready", 1)
                settle(dve)
                passes = dve.value_load(spare_count[0:1, 0:1], min_val=0, max_val=SPARE - 1)
                with dve.If(passes > 0):
                    with dve.Fori(0, passes) as n:
                        e = dve.value_load(spare_expert[0:1, bass.ds(n, 1)], min_val=0, max_val=NE - 1)
                        dve.wait_ge(pe_to_dve, n * 3 + 1)
                        for t in range(2):
                            link_clear(dve.tensor_scalar(spare_pos[:, t:t + 1], pos[:, t, bass.ds(e, 1)],
                                                         spare_rank[:, bass.ds(n, 1)], None, ALU.subtract))
                            dve.tensor_scalar(places[:, t, 0:SLOTS_E], iota[:, 0:SLOTS_E], spare_pos[:, t:t + 1], None, ALU.is_equal)
                            last = dve.tensor_scalar(places_w[:, t, :], iota[:], spare_pos[:, t:t + 1],
                                                     wts[:, t, bass.ds(e, 1)], ALU.is_equal, ALU.mult)
                        last.then_inc(dve_to_pe, 1)
                        dve.wait_ge(pe_to_dve, n * 3 + 2)
                        split_places(psum[:, TURN_BANK, 0:S]).then_inc(dve_to_pe, 1)
                        dve.wait_ge(act_to_dve, n + 1)
                        dve.tensor_tensor(hb, psum[:, 4, P:2 * P], sgate_e, ALU.mult).then_inc(dve_to_pe, 1)
                        dve.wait_ge(pe_to_dve, n * 3 + 3)
                        split_output(0, psum[:, 5, :]).then_inc(dve_to_pe, 1)
                    dve.sem_clear(pe_to_dve)
                    dve.sem_clear(act_to_dve)
                for t in range(2):
                    for j in range(2):
                        key, part = ("y", t, j), slice(512 * j, 512 * j + 512)
                        filled(dve, l, key)
                        done(dve.tensor_tensor(h[:, t, part], bank(key), mixed[:, t, part], ALU.add), key)
                        drained(dve, l, key)
                        half_statistics(h, t, j)
                normalise(h[:], ln_g[:], ln_b[:], lambda: signal(dve, l, "rstd_ready", 4), "h_ready", counted=True,
                          scale_arrived=lambda: signal(dve, l, "ln2_loaded", 32))
                end_chain()


NAMES = ["x", "p", "ln_in_g", "ln_in_b", "w_in", "gla_fg_w", "gla_fg_b", "gla_norm_g", "sg_norm_g", "sg_norm_b", "sg_w",
         "sg_b", "mla_qn_g", "mla_w_uq", "mla_kvn_g", "mla_w_ukv", "w_branch", "w_out", "ln1_g", "ln1_b", "router_w",
         "router_b", "exp_w_gate", "exp_w_up", "exp_w_down", "sh_w_gate", "sh_w_up", "sh_w_down", "ple_w_in",
         "ple_w_gate", "ln2_g", "ln2_b"]


def kernel(**inputs):
    import numpy as np
    import concourse.bacc as bacc
    from concourse.bass_utils import run_bass_kernel_spmd

    nc = bacc.Bacc("TRN2", target_bir_lowering=False, num_devices=1)
    arrays, weights = {}, {}

    def given(name, a):
        arrays[f"in_{name}"] = a
        return nc.dram_tensor(f"in_{name}", a.shape, mybir.dt.from_np(a.dtype), kind="ExternalInput").ap()

    for name in NAMES:
        weights[name] = given(name, np.ascontiguousarray(inputs[name]))
    inv = np.float32(10000.0) ** (-np.arange(HALF, dtype=np.float32) / np.float32(HALF))
    angle = np.arange(S, dtype=np.float32)[:, None] * inv
    cos_tab, sin_tab = given("cos", np.cos(angle).astype(np.float32)), given("sin", np.sin(angle).astype(np.float32))
    out = nc.dram_tensor("out_0", (1, S, D), F32, kind="ExternalOutput").ap()
    build_trunk(nc, weights, cos_tab, sin_tab, out)
    r = run_bass_kernel_spmd(nc, [arrays], core_ids=[0])
    return r.results[0]["out_0"]
```
